# Optimizing a Trainium2 kernel written in Bass

```python
import math
import jax, jax.numpy as jnp
from jax import lax
import numpy as np
import jax
import jax.numpy as jnp

D_MODEL = 1024
BATCH = 1
SEQ = 256
DEPTH = 2

D_MIX = D_MODEL
D_CONV = D_MIX // 4
D_LRU = D_MIX // 4
D_ATTN = D_MIX // 2
CONV_KERNEL = 31
LRU_HEADS = 4
LRU_HEAD_DIM = D_LRU // LRU_HEADS
LRU_CONV = 4
LRU_C = 8.0
HEAD_DIM = 64
N_Q_HEADS = D_ATTN // HEAD_DIM
N_KV_HEADS = 2
GQA_REP = N_Q_HEADS // N_KV_HEADS
KV_DIM = N_KV_HEADS * HEAD_DIM
WINDOW = 128
BLOCK = 128
REL_BUCKETS = 32
REL_MAX_DIST = 128
D_FF = 2816
ALPHA = (2.0 * DEPTH) ** 0.25
BETA = (8.0 * DEPTH) ** -0.25
LN_EPS = 1e-5
D_IN = 2 * D_CONV + 2 * D_LRU + D_ATTN + 2 * KV_DIM


def _layernorm(x, g, b):
    xf = x.astype(jnp.float32)
    mu = jnp.mean(xf, axis=-1, keepdims=True)
    var = jnp.mean(jnp.square(xf - mu), axis=-1, keepdims=True)
    return ((xf - mu) * lax.rsqrt(var + LN_EPS)).astype(x.dtype) * g + b

def _swiglu(x, wg, wu, wd):
    return (jax.nn.silu(x @ wg) * (x @ wu)) @ wd

def _causal_dw_conv(x, w):
    k = w.shape[0]
    return lax.conv_general_dilated(
        x, w[:, None, :].astype(x.dtype), window_strides=(1,), padding=[(k - 1, 0)],
        dimension_numbers=('NWC', 'WIO', 'NWC'), feature_group_count=x.shape[-1])

def _conv_module(u, dw_w, dw_b, g, b):
    a, gate = jnp.split(u, 2, axis=-1)
    y = a * jax.nn.sigmoid(gate)
    y = _causal_dw_conv(y, dw_w) + dw_b
    y = _layernorm(y, g, b)
    return jax.nn.silu(y)

def _lin_combine(left, right):
    a1, b1 = left
    a2, b2 = right
    return a1 * a2, a2 * b1 + b2

def _recurrent(u, conv_w, conv_b, wa, ba, wx, bx, lam):
    B, S, _ = u.shape
    xb, gb = jnp.split(u, 2, axis=-1)
    xb = _causal_dw_conv(xb, conv_w) + conv_b
    xh = xb.reshape(B, S, LRU_HEADS, LRU_HEAD_DIM)
    r = jax.nn.sigmoid(jnp.einsum('bshi,hij->bshj', xh, wa).reshape(B, S, D_LRU) + ba)
    i = jax.nn.sigmoid(jnp.einsum('bshi,hij->bshj', xh, wx).reshape(B, S, D_LRU) + bx)
    log_a = LRU_C * r.astype(jnp.float32) * jax.nn.log_sigmoid(lam.astype(jnp.float32))
    a = jnp.exp(log_a)
    mult = jnp.sqrt(-jnp.expm1(2.0 * log_a))
    bterm = mult * (i * xb).astype(jnp.float32)
    _, h = lax.associative_scan(_lin_combine, (a, bterm), axis=1)
    return h.astype(u.dtype) * jax.nn.gelu(gb)

def _rel_bucket(dist):
    max_exact = REL_BUCKETS // 2
    is_small = dist < max_exact
    large = max_exact + (jnp.log(jnp.maximum(dist, 1).astype(jnp.float32) / max_exact)
                         / math.log(REL_MAX_DIST / max_exact)
                         * (REL_BUCKETS - max_exact)).astype(jnp.int32)
    large = jnp.minimum(large, REL_BUCKETS - 1)
    return jnp.where(is_small, dist, large)

def _band_bias_and_mask(rel_bias, seq):
    nb = seq // BLOCK
    qi = jnp.arange(BLOCK)[:, None]
    kj = jnp.arange(2 * BLOCK)[None, :]
    dist = qi - kj + BLOCK
    bucket = _rel_bucket(jnp.maximum(dist, 0))
    bias = rel_bias[bucket].astype(jnp.float32)
    bias = jnp.transpose(bias, (2, 0, 1)).reshape(N_KV_HEADS, GQA_REP, BLOCK, 2 * BLOCK)
    blk = jnp.arange(nb)[:, None, None]
    valid = (dist >= 0) & (dist < WINDOW) & (blk * BLOCK + kj - BLOCK >= 0)
    return bias, valid

def _band(t, nb):
    B = t.shape[0]
    tp = jnp.pad(t, ((0, 0), (BLOCK, 0), (0, 0), (0, 0)))
    tp = tp.reshape(B, nb + 1, BLOCK, t.shape[2], t.shape[3])
    return jnp.concatenate([tp[:, :-1], tp[:, 1:]], axis=2)

def _swa(q, k, v, band_bias, valid, sinks):
    B, S, _ = q.shape
    nb = S // BLOCK
    qb = q.reshape(B, nb, BLOCK, N_KV_HEADS, GQA_REP, HEAD_DIM)
    kb = _band(k.reshape(B, S, N_KV_HEADS, HEAD_DIM), nb)
    vb = _band(v.reshape(B, S, N_KV_HEADS, HEAD_DIM), nb)
    s = jnp.einsum('bnqgrd,bnkgd->bngrqk', qb, kb).astype(jnp.float32) * (HEAD_DIM ** -0.5)
    s = s + band_bias[None, None]
    s = jnp.where(valid[None, :, None, None], s, -1e30)
    sink = jnp.broadcast_to(sinks.astype(jnp.float32).reshape(1, 1, N_KV_HEADS, GQA_REP, 1, 1),
                            s.shape[:-1] + (1,))
    p = jax.nn.softmax(jnp.concatenate([s, sink], axis=-1), axis=-1)[..., :-1]
    o = jnp.einsum('bngrqk,bnkgd->bnqgrd', p.astype(vb.dtype), vb)
    return o.reshape(B, S, D_ATTN)

def _mixer(x, w_in, conv_dw_w, conv_dw_b, conv_ln_g, conv_ln_b, lru_conv_w, lru_conv_b,
           lru_wa, lru_ba, lru_wx, lru_bx, lru_lambda, sinks, w_out, band_bias, valid):
    u = x @ w_in
    o1 = 2 * D_CONV
    o2 = o1 + 2 * D_LRU
    o3 = o2 + D_ATTN
    o4 = o3 + KV_DIM
    u_conv, u_lru, q, k, v = jnp.split(u, [o1, o2, o3, o4], axis=-1)
    y_conv = _conv_module(u_conv, conv_dw_w, conv_dw_b, conv_ln_g, conv_ln_b)
    y_lru = _recurrent(u_lru, lru_conv_w, lru_conv_b, lru_wa, lru_ba, lru_wx, lru_bx, lru_lambda)
    y_attn = _swa(q, k, v, band_bias, valid, sinks)
    return jnp.concatenate([y_conv, y_lru, y_attn], axis=-1) @ w_out

def first_inputs(seed: int = 0) -> dict:
    key = jax.random.key(seed)
    ks = jax.random.split(key, 24)
    f32 = jnp.float32
    nrm = lambda k, shape, scale: jax.random.normal(k, shape, f32) * scale
    x = nrm(ks[0], (BATCH, SEQ, D_MODEL), 1.0)
    rel_bias = nrm(ks[1], (REL_BUCKETS, N_Q_HEADS), 0.5)
    ln_g = 1.0 + nrm(ks[2], (DEPTH, 3, D_MODEL), 0.1)
    ln_b = nrm(ks[3], (DEPTH, 3, D_MODEL), 0.02)
    ffn_w_gate = nrm(ks[4], (DEPTH, 2, D_MODEL, D_FF), D_MODEL ** -0.5)
    ffn_w_up = nrm(ks[5], (DEPTH, 2, D_MODEL, D_FF), D_MODEL ** -0.5)
    ffn_w_down = nrm(ks[6], (DEPTH, 2, D_FF, D_MODEL), BETA * D_FF ** -0.5)
    w_in = nrm(ks[7], (DEPTH, D_MODEL, D_IN), D_MODEL ** -0.5)
    conv_dw_w = nrm(ks[8], (DEPTH, CONV_KERNEL, D_CONV), CONV_KERNEL ** -0.5)
    conv_dw_b = nrm(ks[9], (DEPTH, D_CONV), 0.02)
    conv_ln_g = 1.0 + nrm(ks[10], (DEPTH, D_CONV), 0.1)
    conv_ln_b = nrm(ks[11], (DEPTH, D_CONV), 0.02)
    lru_conv_w = nrm(ks[12], (DEPTH, LRU_CONV, D_LRU), LRU_CONV ** -0.5)
    lru_conv_b = nrm(ks[13], (DEPTH, D_LRU), 0.02)
    lru_wa = nrm(ks[14], (DEPTH, LRU_HEADS, LRU_HEAD_DIM, LRU_HEAD_DIM), LRU_HEAD_DIM ** -0.5)
    lru_ba = nrm(ks[15], (DEPTH, D_LRU), 0.02)
    lru_wx = nrm(ks[16], (DEPTH, LRU_HEADS, LRU_HEAD_DIM, LRU_HEAD_DIM), LRU_HEAD_DIM ** -0.5)
    lru_bx = nrm(ks[17], (DEPTH, D_LRU), 0.02)
    a_init = jax.random.uniform(ks[18], (DEPTH, D_LRU), f32, 0.9, 0.999)
    sig = a_init ** (1.0 / LRU_C)
    lru_lambda = jnp.log(sig) - jnp.log1p(-sig)
    attn_sinks = nrm(ks[19], (DEPTH, N_Q_HEADS), 0.5)
    w_out = nrm(ks[20], (DEPTH, D_MIX, D_MODEL), BETA * D_MIX ** -0.5)
    return {'x': x, 'rel_bias': rel_bias, 'ln_g': ln_g, 'ln_b': ln_b,
            'ffn_w_gate': ffn_w_gate, 'ffn_w_up': ffn_w_up, 'ffn_w_down': ffn_w_down,
            'w_in': w_in, 'conv_dw_w': conv_dw_w, 'conv_dw_b': conv_dw_b,
            'conv_ln_g': conv_ln_g, 'conv_ln_b': conv_ln_b,
            'lru_conv_w': lru_conv_w, 'lru_conv_b': lru_conv_b,
            'lru_wa': lru_wa, 'lru_ba': lru_ba, 'lru_wx': lru_wx, 'lru_bx': lru_bx,
            'lru_lambda': lru_lambda, 'attn_sinks': attn_sinks, 'w_out': w_out}

def first_block(x, rel_bias, ln_g, ln_b, ffn_w_gate, ffn_w_up, ffn_w_down, w_in,
              conv_dw_w, conv_dw_b, conv_ln_g, conv_ln_b, lru_conv_w, lru_conv_b,
              lru_wa, lru_ba, lru_wx, lru_bx, lru_lambda, attn_sinks, w_out):
    band_bias, valid = _band_bias_and_mask(rel_bias, x.shape[1])
    for l in range(DEPTH):
        h = 0.5 * _swiglu(x, ffn_w_gate[l, 0], ffn_w_up[l, 0], ffn_w_down[l, 0])
        x = _layernorm(ALPHA * x + h, ln_g[l, 0], ln_b[l, 0])
        h = _mixer(x, w_in[l], conv_dw_w[l], conv_dw_b[l], conv_ln_g[l], conv_ln_b[l],
                   lru_conv_w[l], lru_conv_b[l], lru_wa[l], lru_ba[l], lru_wx[l], lru_bx[l],
                   lru_lambda[l], attn_sinks[l], w_out[l], band_bias, valid)
        x = _layernorm(ALPHA * x + h, ln_g[l, 1], ln_b[l, 1])
        h = 0.5 * _swiglu(x, ffn_w_gate[l, 1], ffn_w_up[l, 1], ffn_w_down[l, 1])
        x = _layernorm(ALPHA * x + h, ln_g[l, 2], ln_b[l, 2])
    return x


DEPTH_2 = 1

GRID_W = 64
CTX_LEN = 256
ATT_HEADS = 8
ATT_KV_HEADS = 2
ATT_GROUPS = ATT_HEADS // ATT_KV_HEADS
ATT_DIM = ATT_HEADS * HEAD_DIM
KV_DIM_2 = ATT_KV_HEADS * HEAD_DIM
ROPE_BASE = 10000.0
ATT_SCALE = HEAD_DIM ** -0.5
NEG_INF = -1e30
RWKV_HEADS = 8
RWKV_DIM = RWKV_HEADS * HEAD_DIM
DECAY_LORA = 64
ICL_LORA = 64
GATE_LORA = 128
GN_EPS = 64e-5
N_EXPERTS = 32
TOP_K = 4
D_EXPERT = D_MODEL
SWIGLU_LIMIT = 7.0
SWIGLU_ALPHA = 1.702
MOE_BLOCK = 128
RMS_EPS = 1e-6
ATT_COLS = ATT_DIM + 2 * KV_DIM_2
RWKV_SIZES = (RWKV_DIM, RWKV_DIM, RWKV_DIM, DECAY_LORA, DECAY_LORA, ICL_LORA, ICL_LORA, GATE_LORA)
RWKV_COLS = sum(RWKV_SIZES)
RWKV_OFFSETS = tuple(int(o) for o in np.cumsum(RWKV_SIZES)[:-1])
GATE_COLS = 2 * D_MODEL
PROJ_COLS = ATT_COLS + RWKV_COLS + GATE_COLS
F32 = jnp.float32


def rms_norm(x, g):
    xf = x.astype(F32)
    y = xf * lax.rsqrt(jnp.mean(xf * xf, axis=-1, keepdims=True) + RMS_EPS)
    return y.astype(x.dtype) * g

def modulate(h, shift, scale):
    return h * (1.0 + scale) + shift

def _rotate_half(t, ang):
    cos = jnp.cos(ang)[None, :, None, :].astype(t.dtype)
    sin = jnp.sin(ang)[None, :, None, :].astype(t.dtype)
    t1, t2 = jnp.split(t, 2, axis=-1)
    return jnp.concatenate([t1 * cos - t2 * sin, t2 * cos + t1 * sin], axis=-1)

def axial_rope(t):
    L = t.shape[1]
    n_rows = L // GRID_W
    row = jnp.repeat(jnp.arange(n_rows, dtype=F32), GRID_W, total_repeat_length=L)
    col = jnp.tile(jnp.arange(GRID_W, dtype=F32), n_rows)
    half = HEAD_DIM // 2
    inv_freq = ROPE_BASE ** (-jnp.arange(0, half, 2, dtype=F32) / half)
    t_row, t_col = jnp.split(t, 2, axis=-1)
    return jnp.concatenate([_rotate_half(t_row, row[:, None] * inv_freq[None, :]),
                            _rotate_half(t_col, col[:, None] * inv_freq[None, :])], axis=-1)

def token_shift(z, mu_prev, mu_next):
    prev = jnp.pad(z[:, :-1], ((0, 0), (1, 0), (0, 0)))
    nxt = jnp.pad(z[:, 1:], ((0, 0), (0, 1), (0, 0)))
    return z + mu_prev * (prev - z) + mu_next * (nxt - z)

def rwkv_features(z, p):
    B, L, _ = z.shape
    r, k, v, wl_f, wl_b, al_f, al_b, gl = jnp.split(z, RWKV_OFFSETS, axis=-1)

    def heads(t):
        return t.reshape(B, L, RWKV_HEADS, HEAD_DIM)

    def decay(w_low, w0, w2):
        w = (w0 + jnp.tanh(w_low) @ w2).astype(F32)
        w = -jax.nn.softplus(-w) - 0.5
        return heads(jnp.exp(-jnp.exp(w)))

    icl_f = jax.nn.sigmoid(p['a0_f'] + al_f @ p['a2_f'])
    icl_b = jax.nn.sigmoid(p['a0_b'] + al_b @ p['a2_b'])
    kk = heads(k * p['k_k']).astype(F32)
    kk = (kk / jnp.maximum(jnp.sqrt(jnp.sum(kk * kk, axis=-1, keepdims=True)), 1e-12)).astype(z.dtype)
    return dict(
        r=heads(r), v=heads(v),
        k_f=heads(k * (1.0 + (icl_f - 1.0) * p['k_a'])),
        k_b=heads(k * (1.0 + (icl_b - 1.0) * p['k_a'])),
        dec_f=decay(wl_f, p['w0_f'], p['w2_f']),
        dec_b=decay(wl_b, p['w0_b'], p['w2_b']),
        a=-kk, b_f=kk * heads(icl_f), b_b=kk * heads(icl_b),
        gate=jax.nn.sigmoid(gl) @ p['g2'])

def wkv_scan(r, w, k, v, a, b, state0, reverse):
    def step(S, inp):
        r_t, w_t, k_t, v_t, a_t, b_t = inp
        sa = jnp.einsum('bhij,bhj->bhi', S, a_t)
        S = S * w_t[:, :, None, :] + sa[..., None] * b_t[:, :, None, :] + v_t[..., None] * k_t[:, :, None, :]
        return S, jnp.einsum('bhij,bhj->bhi', S, r_t)

    xs = tuple(jnp.moveaxis(t.astype(F32), 1, 0) for t in (r, w, k, v, a, b))
    S, ys = lax.scan(step, state0, xs, reverse=reverse)
    return jnp.moveaxis(ys, 0, 1), S

def bidir_scan(f, s0_f, s0_b):
    y_f, s_f = wkv_scan(f['r'], f['dec_f'], f['k_f'], f['v'], f['a'], f['b_f'], s0_f, False)
    y_b, s_b = wkv_scan(f['r'], f['dec_b'], f['k_b'], f['v'], f['a'], f['b_b'], s0_b, True)
    return y_f + y_b, s_f, s_b

def rwkv_output(y, f, p):
    B, L = y.shape[:2]
    mean = jnp.mean(y, axis=-1, keepdims=True)
    var = jnp.mean(jnp.square(y - mean), axis=-1, keepdims=True)
    yn = ((y - mean) * lax.rsqrt(var + GN_EPS)).reshape(B, L, RWKV_DIM)
    yn = (yn * p['ln_x_w'] + p['ln_x_b']).astype(f['v'].dtype)
    bonus = jnp.sum(f['r'] * (f['k_f'] + f['k_b']) * p['r_k'], axis=-1, keepdims=True) * f['v']
    return (yn + bonus.reshape(B, L, RWKV_DIM)) * f['gate']

def project(h, p):
    B, L, _ = h.shape
    z = h @ p['w_in'] + p['b_in']
    z_att, z_rwkv, z_gate = jnp.split(z, [ATT_COLS, ATT_COLS + RWKV_COLS], axis=-1)
    q, k, v = jnp.split(z_att, [ATT_DIM, ATT_DIM + KV_DIM_2], axis=-1)
    q = q.reshape(B, L, ATT_HEADS, HEAD_DIM)
    k = k.reshape(B, L, ATT_KV_HEADS, HEAD_DIM)
    v = v.reshape(B, L, ATT_KV_HEADS, HEAD_DIM)
    feats = rwkv_features(token_shift(z_rwkv, p['mu_prev'], p['mu_next']), p)
    return q, k, v, feats, z_gate

def sink_softmax(logits, sinks):
    sink = jnp.broadcast_to(sinks.reshape(ATT_KV_HEADS, ATT_GROUPS, 1, 1).astype(F32), logits.shape[:-1] + (1,))
    return jax.nn.softmax(jnp.concatenate([logits, sink], axis=-1), axis=-1)[..., :-1]

def window_attention(q, k, v, k_ctx, v_ctx, sinks):
    B, L = q.shape[:2]
    nb = L // BLOCK
    band = BLOCK + 2 * WINDOW
    qb = jnp.moveaxis(q.reshape(B, nb, BLOCK, ATT_KV_HEADS, ATT_GROUPS, HEAD_DIM), 1, 0)
    kp = jnp.pad(k, ((0, 0), (WINDOW, WINDOW), (0, 0), (0, 0)))
    vp = jnp.pad(v, ((0, 0), (WINDOW, WINDOW), (0, 0), (0, 0)))
    k_off = jnp.arange(band) - WINDOW
    rel = k_off[None, :] - jnp.arange(BLOCK)[:, None]

    def one_block(args):
        n, q_n = args
        k_n = lax.dynamic_slice_in_dim(kp, n * BLOCK, band, axis=1)
        v_n = lax.dynamic_slice_in_dim(vp, n * BLOCK, band, axis=1)
        kpos = n * BLOCK + k_off
        valid = (jnp.abs(rel) <= WINDOW) & ((kpos >= 0) & (kpos < L))[None, :]
        s_lat = jnp.einsum('bqkgd,bskd->bkgqs', q_n, k_n).astype(F32) * ATT_SCALE
        s_lat = jnp.where(valid, s_lat, NEG_INF)
        s_ctx = jnp.einsum('bqkgd,bckd->bkgqc', q_n, k_ctx).astype(F32) * ATT_SCALE
        prob = sink_softmax(jnp.concatenate([s_lat, s_ctx], axis=-1), sinks).astype(v.dtype)
        return (jnp.einsum('bkgqs,bskd->bqkgd', prob[..., :band], v_n)
                + jnp.einsum('bkgqc,bckd->bqkgd', prob[..., band:], v_ctx))

    o = lax.map(one_block, (jnp.arange(nb), qb))
    return jnp.moveaxis(o, 0, 1).reshape(B, L, ATT_DIM)

def context_attention(q, k, v, sinks):
    B, C = q.shape[:2]
    qg = q.reshape(B, C, ATT_KV_HEADS, ATT_GROUPS, HEAD_DIM)
    s = jnp.einsum('bqkgd,bckd->bkgqc', qg, k).astype(F32) * ATT_SCALE
    prob = sink_softmax(s, sinks).astype(v.dtype)
    return jnp.einsum('bkgqc,bckd->bqkgd', prob, v).reshape(B, C, ATT_DIM)

def merge_branches(att, rwk, z_gate, p):
    g_att, g_rwkv = jnp.split(jax.nn.sigmoid(z_gate), 2, axis=-1)
    merged = g_att * (att @ p['w_up_att']) + g_rwkv * (rwk @ p['w_up_rwkv'])
    return merged @ p['w_out']

def moe_ffn(h, p):
    B, L, D = h.shape
    xt = h.reshape(-1, D)
    T = xt.shape[0]
    TK = T * TOP_K
    logits = (xt @ p['w_router'] + p['b_router']).astype(F32)
    top_val, top_idx = lax.top_k(logits, TOP_K)
    gates = jax.nn.softmax(top_val, axis=-1).astype(h.dtype)
    flat_e = top_idx.reshape(-1).astype(jnp.int32)
    flat_tok = jnp.repeat(jnp.arange(T, dtype=jnp.int32), TOP_K)
    order = jnp.argsort(flat_e)
    e_sorted = flat_e[order]
    counts = jnp.zeros((N_EXPERTS,), jnp.int32).at[flat_e].add(1)
    padded = ((counts + MOE_BLOCK - 1) // MOE_BLOCK) * MOE_BLOCK
    start = jnp.cumsum(counts) - counts
    p_end = jnp.cumsum(padded)
    p_start = p_end - padded
    dest = p_start[e_sorted] + jnp.arange(TK, dtype=jnp.int32) - start[e_sorted]
    n_blocks = -(-TK // MOE_BLOCK) + N_EXPERTS
    n_slots = n_blocks * MOE_BLOCK
    slot_tok = jnp.full((n_slots,), T, jnp.int32).at[dest].set(flat_tok[order])
    slot_g = jnp.zeros((n_slots,), h.dtype).at[dest].set(gates.reshape(-1)[order])
    block_exp = jnp.minimum(jnp.searchsorted(p_end, jnp.arange(n_blocks, dtype=jnp.int32) * MOE_BLOCK, side='right'),
                            N_EXPERTS - 1).astype(jnp.int32)
    x_pad = jnp.concatenate([xt, jnp.zeros((1, D), xt.dtype)], axis=0)
    xb = x_pad[slot_tok].reshape(n_blocks, MOE_BLOCK, D)
    w_gu, b_gu, w_dn, b_dn = p['w_gate_up'], p['b_gate_up'], p['w_down'], p['b_down']

    def expert_block(args):
        e, x_b = args
        gu = x_b @ w_gu[e] + b_gu[e]
        gate = jnp.minimum(gu[..., ::2], SWIGLU_LIMIT)
        up = jnp.clip(gu[..., 1::2], -SWIGLU_LIMIT, SWIGLU_LIMIT)
        return ((up + 1.0) * (gate * jax.nn.sigmoid(SWIGLU_ALPHA * gate))) @ w_dn[e] + b_dn[e]

    yb = lax.map(expert_block, (block_exp, xb)).reshape(n_slots, D)
    y = jnp.zeros((T + 1, D), yb.dtype).at[slot_tok].add(yb * slot_g[:, None])[:T]
    return y.reshape(B, L, D)

def second_inputs(seed: int = 0) -> dict:
    key = jax.random.key(seed)
    ks = iter(jax.random.split(key, 48))
    D = D_MODEL

    def nrm(shape, scale):
        return scale * jax.random.normal(next(ks), shape, F32)

    def gain(shape):
        return 1.0 + nrm(shape, 0.05)

    return {
        'x': nrm((BATCH, SEQ, D), 1.0),
        'c': nrm((BATCH, D), 1.0),
        'ctx': nrm((BATCH, CTX_LEN, D), 1.0),
        'c_ctx': nrm((D,), 1.0),
        'w_ada': nrm((DEPTH_2, D, 6 * D), 0.5 * D ** -0.5),
        'b_ada': nrm((DEPTH_2, 6 * D), 0.02),
        'g_pre_mix': gain((DEPTH_2, D)),
        'g_post_mix': gain((DEPTH_2, D)),
        'g_pre_ffn': gain((DEPTH_2, D)),
        'g_post_ffn': gain((DEPTH_2, D)),
        'w_in': nrm((DEPTH_2, D, PROJ_COLS), D ** -0.5),
        'b_in': nrm((DEPTH_2, PROJ_COLS), 0.02),
        'mu_prev': jax.random.uniform(next(ks), (DEPTH_2, RWKV_COLS), F32, 0.0, 0.5),
        'mu_next': jax.random.uniform(next(ks), (DEPTH_2, RWKV_COLS), F32, 0.0, 0.5),
        'att_sinks': nrm((DEPTH_2, ATT_HEADS), 0.5),
        'w0_f': jax.random.uniform(next(ks), (DEPTH_2, RWKV_DIM), F32, -5.0, 0.0),
        'w0_b': jax.random.uniform(next(ks), (DEPTH_2, RWKV_DIM), F32, -5.0, 0.0),
        'w2_f': nrm((DEPTH_2, DECAY_LORA, RWKV_DIM), 0.5 * DECAY_LORA ** -0.5),
        'w2_b': nrm((DEPTH_2, DECAY_LORA, RWKV_DIM), 0.5 * DECAY_LORA ** -0.5),
        'a0_f': nrm((DEPTH_2, RWKV_DIM), 0.5),
        'a0_b': nrm((DEPTH_2, RWKV_DIM), 0.5),
        'a2_f': nrm((DEPTH_2, ICL_LORA, RWKV_DIM), 0.5 * ICL_LORA ** -0.5),
        'a2_b': nrm((DEPTH_2, ICL_LORA, RWKV_DIM), 0.5 * ICL_LORA ** -0.5),
        'g2': nrm((DEPTH_2, GATE_LORA, RWKV_DIM), GATE_LORA ** -0.5),
        'k_k': 0.85 + nrm((DEPTH_2, RWKV_DIM), 0.05),
        'k_a': gain((DEPTH_2, RWKV_DIM)),
        'r_k': nrm((DEPTH_2, RWKV_HEADS, HEAD_DIM), 0.1),
        'ln_x_w': gain((DEPTH_2, RWKV_DIM)),
        'ln_x_b': nrm((DEPTH_2, RWKV_DIM), 0.02),
        'w_up_att': nrm((DEPTH_2, ATT_DIM, D), ATT_DIM ** -0.5),
        'w_up_rwkv': nrm((DEPTH_2, RWKV_DIM, D), RWKV_DIM ** -0.5),
        'w_out': nrm((DEPTH_2, D, D), D ** -0.5),
        'w_router': nrm((DEPTH_2, D, N_EXPERTS), D ** -0.5),
        'b_router': nrm((DEPTH_2, N_EXPERTS), 0.01),
        'w_gate_up': nrm((DEPTH_2, N_EXPERTS, D, 2 * D_EXPERT), D ** -0.5),
        'b_gate_up': nrm((DEPTH_2, N_EXPERTS, 2 * D_EXPERT), 0.02),
        'w_down': nrm((DEPTH_2, N_EXPERTS, D_EXPERT, D), D_EXPERT ** -0.5),
        'b_down': nrm((DEPTH_2, N_EXPERTS, D), 0.02),
    }

def second_block(x, c, ctx, c_ctx, w_ada, b_ada, g_pre_mix, g_post_mix, g_pre_ffn, g_post_ffn,
              w_in, b_in, mu_prev, mu_next, att_sinks, w0_f, w0_b, w2_f, w2_b, a0_f, a0_b,
              a2_f, a2_b, g2, k_k, k_a, r_k, ln_x_w, ln_x_b, w_up_att, w_up_rwkv, w_out,
              w_router, b_router, w_gate_up, b_gate_up, w_down, b_down):
    B = x.shape[0]
    silu_c = jax.nn.silu(c)
    silu_cc = jax.nn.silu(c_ctx)
    for l in range(DEPTH_2):
        p = dict(w_in=w_in[l], b_in=b_in[l], mu_prev=mu_prev[l], mu_next=mu_next[l], sinks=att_sinks[l],
                 w0_f=w0_f[l], w0_b=w0_b[l], w2_f=w2_f[l], w2_b=w2_b[l], a0_f=a0_f[l], a0_b=a0_b[l],
                 a2_f=a2_f[l], a2_b=a2_b[l], g2=g2[l], k_k=k_k[l], k_a=k_a[l], r_k=r_k[l],
                 ln_x_w=ln_x_w[l], ln_x_b=ln_x_b[l], w_up_att=w_up_att[l], w_up_rwkv=w_up_rwkv[l],
                 w_out=w_out[l], w_router=w_router[l], b_router=b_router[l], w_gate_up=w_gate_up[l],
                 b_gate_up=b_gate_up[l], w_down=w_down[l], b_down=b_down[l])
        mx = [m[:, None, :] for m in jnp.split(silu_c @ w_ada[l] + b_ada[l], 6, axis=-1)]
        mc = jnp.split(silu_cc @ w_ada[l] + b_ada[l], 6, axis=-1)
        hc = modulate(rms_norm(ctx, g_pre_mix[l]), mc[0], mc[1])
        qc, kc, vc, fc, zc_gate = project(hc, p)
        zero_state = jnp.zeros((B, RWKV_HEADS, HEAD_DIM, HEAD_DIM), F32)
        yc, sc_f, sc_b = bidir_scan(fc, zero_state, zero_state)
        hx = modulate(rms_norm(x, g_pre_mix[l]), mx[0], mx[1])
        q, k, v, fx, zx_gate = project(hx, p)
        att_x = window_attention(axial_rope(q), axial_rope(k), v, kc, vc, p['sinks'])
        yx, _, _ = bidir_scan(fx, sc_f, sc_b)
        mix_x = merge_branches(att_x, rwkv_output(yx, fx, p), zx_gate, p)
        x = x + mx[2] * rms_norm(mix_x, g_post_mix[l])
        hf = modulate(rms_norm(x, g_pre_ffn[l]), mx[3], mx[4])
        x = x + mx[5] * rms_norm(moe_ffn(hf, p), g_post_ffn[l])
        if l + 1 < DEPTH_2:
            mix_c = merge_branches(context_attention(qc, kc, vc, p['sinks']), rwkv_output(yc, fc, p), zc_gate, p)
            ctx = ctx + mc[2] * rms_norm(mix_c, g_post_mix[l])
            hcf = modulate(rms_norm(ctx, g_pre_ffn[l]), mc[3], mc[4])
            ctx = ctx + mc[5] * rms_norm(moe_ffn(hcf, p), g_post_ffn[l])
    return x


def setup_inputs(seed=0):
    out = dict(first_inputs(seed))
    for name, value in second_inputs(seed + 1).items():
        if name != "x":
            out[name + "_2"] = value
    return out


def reference(
    x, rel_bias, ln_g, ln_b, ffn_w_gate, ffn_w_up, ffn_w_down, w_in, conv_dw_w, conv_dw_b,
    conv_ln_g, conv_ln_b, lru_conv_w, lru_conv_b, lru_wa, lru_ba, lru_wx, lru_bx, lru_lambda,
    attn_sinks, w_out, c_2, ctx_2, c_ctx_2, w_ada_2, b_ada_2, g_pre_mix_2, g_post_mix_2,
    g_pre_ffn_2, g_post_ffn_2, w_in_2, b_in_2, mu_prev_2, mu_next_2, att_sinks_2, w0_f_2,
    w0_b_2, w2_f_2, w2_b_2, a0_f_2, a0_b_2, a2_f_2, a2_b_2, g2_2, k_k_2, k_a_2, r_k_2, ln_x_w_2,
    ln_x_b_2, w_up_att_2, w_up_rwkv_2, w_out_2, w_router_2, b_router_2, w_gate_up_2,
    b_gate_up_2, w_down_2, b_down_2,
):
    x = first_block(
        x, rel_bias, ln_g, ln_b, ffn_w_gate, ffn_w_up, ffn_w_down, w_in, conv_dw_w, conv_dw_b,
        conv_ln_g, conv_ln_b, lru_conv_w, lru_conv_b, lru_wa, lru_ba, lru_wx, lru_bx,
        lru_lambda, attn_sinks, w_out,
    )
    return second_block(
        x, c_2, ctx_2, c_ctx_2, w_ada_2, b_ada_2, g_pre_mix_2, g_post_mix_2, g_pre_ffn_2,
        g_post_ffn_2, w_in_2, b_in_2, mu_prev_2, mu_next_2, att_sinks_2, w0_f_2, w0_b_2, w2_f_2,
        w2_b_2, a0_f_2, a0_b_2, a2_f_2, a2_b_2, g2_2, k_k_2, k_a_2, r_k_2, ln_x_w_2, ln_x_b_2,
        w_up_att_2, w_up_rwkv_2, w_out_2, w_router_2, b_router_2, w_gate_up_2, b_gate_up_2,
        w_down_2, b_down_2,
    )


_drawn_inputs = setup_inputs


def setup_inputs(seed=0):
    import zlib

    import numpy as np

    out = dict(_drawn_inputs(seed))
    spreads = {}
    factors = {'conv_dw_b': 3.121,
     'conv_ln_b': 4.797,
     'lru_ba': 6.479,
     'lru_bx': 8.0,
     'attn_sinks': 8.0,
     'g_post_ffn_2': 4.015,
     'att_sinks_2': 8.0,
     'w2_f_2': 3.088,
     'ln_x_b_2': 3.653,
     'b_router_2': 2.857,
     'b_gate_up_2': 8.0,
     'b_down_2': 8.0}
    for name, (base, spread) in spreads.items():
        noise = np.random.default_rng([zlib.crc32(name.encode()), seed]).standard_normal(out[name].shape)
        drawn = base * np.exp(spread * noise) if base else spread * noise
        out[name] = jnp.asarray(drawn.astype(out[name].dtype))
    for name, factor in factors.items():
        out[name] = (out[name] * factor).astype(out[name].dtype)
    return out
```

```python
from contextlib import ExitStack
import math

import numpy as np
import concourse.bass as bass
from concourse import mybir

F32 = mybir.dt.float32
BF16 = mybir.dt.bfloat16
I32 = mybir.dt.int32
ALU = mybir.AluOpType
ACT = mybir.ActivationFunctionType
AX = mybir.AxisListType

P = 128
T = 256
D = 1024
KD = D // P
LAYERS = 2
F = 2816
FCH = F // 256
TAPS, LTAPS = 31, 4
HEADS = 8
BLK = 2048
RING = 6
ALPHA = (2.0 * LAYERS) ** 0.25
LN_EPS = 1e-5
RMS_EPS = 1e-6
GN_EPS = 64e-5
NEG = -1e30
EXPERTS = 32
CAP = 128
CH = 64
NSEQ = 2
ZT = 37
FFN_BLOCKS = 3 * FCH
IN_BLOCKS = 7
OUT_BLOCKS = 4
LAYER_BLOCKS = 2 * FFN_BLOCKS + IN_BLOCKS + OUT_BLOCKS
ADA_BLOCKS = 24
PROJ_BLOCKS = 19
UP_BLOCKS = 4
EXPERT_BLOCKS = 12
ADA0 = LAYERS * LAYER_BLOCKS
PROJ0 = ADA0 + ADA_BLOCKS
UP0 = PROJ0 + PROJ_BLOCKS
OUT0 = UP0 + UP_BLOCKS
MOE0 = OUT0 + OUT_BLOCKS
BLOCKS = MOE0 + EXPERTS * EXPERT_BLOCKS


def layout(entries):
    at, out = 0, {}
    for name, n in entries:
        out[name] = (at, n)
        at += n
    return out, at


VEC, NVEC = layout(
    [("ln_g", 48), ("ln_b", 48)]
    + [(f"{n}{l}", c) for l in range(LAYERS) for n, c in (
        ("dw_w", 2 * TAPS), ("dw_b", 2), ("cln_g", 2), ("cln_b", 2), ("lw", 2 * LTAPS), ("lb", 2),
        ("ba", 2), ("bx", 2), ("sink", HEADS), ("gate_w", 4 * P))]
    + [("lam", 2 * LAYERS), ("rel_bias", HEADS)]
    + [("b_in", ZT), ("mu_prev", 15), ("mu_next", 15), ("b_ada", 48), ("g_pre_mix", 8),
       ("g_post_mix", 8), ("g_pre_ffn", 8), ("g_post_ffn", 8), ("sink2", HEADS), ("w0", 8),
       ("a0", 8), ("k_k", 4), ("k_a", 4), ("r_k", 4), ("ln_x_w", 4), ("ln_x_b", 4),
       ("b_router", EXPERTS), ("c", 16), ("w2", 512), ("a2", 512), ("g2", 512),
       ("w_router", KD * EXPERTS)])
CON, NCON = layout([("ident", P), ("ones_d", P), ("ones_c", P), ("heads_mean", P),
                    ("heads_sum", P), ("before", P), ("ones", P), ("cos", T), ("sin", T),
                    ("rot", P), ("mask2", 2 * T), ("bucket", P), ("iota", P), ("mask_f", 256),
                    ("mask_b", 256), ("level_f", 6 * CH), ("level_b", 6 * CH), ("eye2", CH),
                    ("pick", 2 * EXPERTS + 1)])


def steps(*names):
    return {name: n + 1 for n, name in enumerate(names)}


def constants():
    def bucket(d):
        if d < 16:
            return d
        v = np.float32(np.log(np.float32(d) / np.float32(16))) / np.float32(math.log(8.0)) * np.float32(16)
        return min(16 + int(v), 31)

    c = np.zeros((P, NCON), np.float32)

    def put(name, a):
        at, n = CON[name]
        c[:a.shape[0], at:at + n] = a.reshape(a.shape[0], n)

    i = np.arange(P)
    put("ident", np.eye(P))
    put("ones_d", np.full((P, P), 1.0 / D))
    put("ones_c", np.full((P, P), 1.0 / 256))
    same = (i[:, None] // 64) == (i[None, :] // 64)
    put("heads_mean", same / 64.0)
    put("heads_sum", same * 1.0)
    put("before", (i[:, None] < i[None, :]) * 1.0)
    put("ones", np.ones((P, P)))
    t = np.arange(T)
    pos = np.where((i[:, None] % 64) < 32, t[None, :] // 64, t[None, :] % 64).astype(np.float32)
    inv = np.float32(10000.0) ** (-(np.arange(0, 32, 2, dtype=np.float32)) / np.float32(32))
    ang = (pos * inv[i % 16][:, None]).astype(np.float32)
    put("cos", np.cos(ang))
    put("sin", np.sin(ang))
    rot = np.zeros((P, P))
    for m in range(P):
        if m % 32 < 16:
            rot[m + 16, m] = -1.0
        else:
            rot[m - 16, m] = 1.0
    put("rot", rot)
    q = np.arange(P)[:, None, None] + P * np.arange(2)[None, :, None]
    k = np.arange(T)[None, None, :]
    put("mask2", np.where(np.abs(k - q) <= 128, 0.0, NEG))
    onehot = np.zeros((32, P))
    for d in range(P):
        onehot[bucket(P - 1 - d), d] = 1.0
    put("bucket", onehot)
    put("iota", np.broadcast_to(np.arange(P), (P, P)))
    s = (i % 64)[:, None]
    tt = np.arange(CH)[None, :]
    for name, lev, strict, incl in (("mask_f", "level_f", s < tt, s <= tt), ("mask_b", "level_b", s > tt, s >= tt)):
        both = np.concatenate([strict, incl], 1) * 1.0
        put(name, np.concatenate([both, both], 1))
        levels = []
        for n in range(6):
            size = 1 << n
            pair = (s // (2 * size)) == (tt // (2 * size))
            levels.append((strict & pair & ((s // size) != (tt // size))) * 1.0)
        put(lev, np.concatenate(levels, 1))
    put("eye2", (s == tt) * 1.0)
    e = np.arange(2 * EXPERTS + 1)
    put("pick", (((i % 32)[:, None] == e[None, :] % 32) & (i[:, None] < 96) & (e[None, :] < 64)) * 1.0)
    return c


def bass_two_blocks(nc, weights, vectors, consts, x_t, ctx_t, moe_bias, out, stop=99):
    ctx = ExitStack()
    with ctx:
        def sb(name, shape, dt=F32):
            return ctx.enter_context(nc.sbuf_tensor(name, shape, dt))

        def sem(name):
            return ctx.enter_context(nc.semaphore(name))

        ps = ctx.enter_context(nc.psum_tensor("ps", [P, 8, 512], F32))
        ring = sb("ring", [P, RING, BLK])
        vec = sb("vec", [P, NVEC])
        con = sb("con", [P, NCON])
        X = sb("X", [P, KD, T])
        EPS2 = sb("EPS2", [P, 4])
        arena = sb("arena", [P, 31000])
        rel_scratch = nc.dram_tensor("rel_scratch", [HEADS, P, 384], F32, kind="Internal").ap()

        def V(name, i=0, n=None):
            at, m = VEC[name]
            return vec[:, at + i:at + i + (1 if n is None else n)]

        def C(name):
            at, m = CON[name]
            return con[:, at:at + m]

        ident = C("ident")

        def area(start, *shape):
            n = int(np.prod(shape))
            a = arena[:, start:start + n]
            if len(shape) == 1:
                return a, start + n
            names = "abcd"[:len(shape)]
            return a.rearrange("p (" + " ".join(names) + ") -> p " + " ".join(names),
                               **{k: s for k, s in zip(names[1:], shape[1:])}), start + n

        o = 0
        XS, o = area(o, KD, T)
        ST, o = area(o, 4, 512)
        SG, o = area(o, 2, 2, T)
        HF, o = area(o, 2, 2, T)
        U, o = area(o, 14, T)
        YP, o = area(o, 2, TAPS - 1 + T)
        XB, o = area(o, 2, LTAPS - 1 + T)
        CV, o = area(o, 2, T)
        CQ, o = area(o, 2, T)
        SC, o = area(o, HEADS, 3, P)
        BT, o = area(o, HEADS, 3, P)
        PT, o = area(o, HEADS, 3, P)
        VT, o = area(o, 2, P)
        YC, o = area(o, KD, T)
        XC, o = area(o, 2, T)
        LR, o = area(o, 8, 2, T)
        M3, o = area(o, HEADS, 3)
        MM, o = area(o, HEADS, 3)
        S3, o = area(o, HEADS, 3)
        ES, o = area(o, HEADS, 2)
        DN, o = area(o, HEADS, 2)
        LC, o = area(o, 2 * LAYERS)
        LN_, o = area(o, 2 * LAYERS)
        LT, o = area(o, 6, 2 * LAYERS)
        RV, o = area(o, 384)
        ZERO, o = area(o, 640)
        first_end = o
        zero16 = ZERO[:, :].bitcast(BF16)
        zl, zr = zero16[:, 0:P], zero16[:, P:P + 512]

        H, _ = area(0, KD, NSEQ, T)
        HSQ, _ = area(4096, KD, NSEQ, T)
        SH, _ = area(0, 15, NSEQ, T)
        ZR, _ = area(8192, 15, NSEQ, T + 2)
        G, _ = area(15932, 16, T)
        o = 20028
        QA, o = area(o, 4, T)
        KA, o = area(o, NSEQ, T)
        VA, o = area(o, NSEQ, T)
        QR, o = area(o, 4, T)
        KR, o = area(o, NSEQ, T)
        VK, o = area(o, 4, P)
        assert o <= 24124
        SM, o = area(24124, 600)
        ADA = SM[:, 0:96].rearrange("p (c s) -> p c s", s=2)
        SILC = SM[:, 96:112].rearrange("p (k s) -> p k s", s=2)
        GS = SM[:, 112:128].rearrange("p (k s) -> p k s", s=2)
        GF = SM[:, 128:136]
        GP = SM[:, 136:144]
        GQ = SM[:, 144:152]
        PC = SM[:, 152:184].rearrange("p (t c) -> p t c", t=4)
        TOT = SM[:, 184:216].rearrange("p (t c) -> p t c", t=4)
        M4 = SM[:, 216:248].rearrange("p (h a) -> p h a", a=4)
        MX = SM[:, 248:256]
        ES2 = SM[:, 256:264]
        DN2 = SM[:, 264:272]
        TN = SM[:, 272:273]
        AT, o = area(o, 4, T)
        RS, o = area(o, NSEQ, T)
        S2, _ = area(8192, HEADS, 4, P)
        P2, o = area(o, HEADS, 4, P)
        KK, _ = area(8192, 4, 8 * CH)
        BF, _ = area(10240, 4, 8 * CH)
        LL, _ = area(12288, 4, 8 * CH)
        MT, _ = area(14336, 4, 4, CH)
        BK, _ = area(15360, 2, 4, CH)
        AR, _ = area(20028, 4, 8, 2, CH)
        KF, _ = area(26260, 4, 8 * CH)
        VM, _ = area(28308, 8, 4, CH)
        XZ, _ = area(30356, 2, 4, CH)
        WW, _ = area(7680, 4, CH)
        U0, _ = area(7936, 4, CH)
        UU, _ = area(25748, 4, CH)
        STT, _ = area(26004, 4, CH)
        Y = SH[:, 0:4, 0, :]
        KS = SH[:, 8:12, 0, :]
        MG, _ = area(0, KD, T)
        MH, _ = area(2048, KD, T)
        EB = sb("EB", [P, 2, 4, CH])
        RESET = sb("RESET", [P, 8, CH], BF16)
        YO, _ = area(20028, 4, T)
        YQ, _ = area(21052, 4, T)
        YB, _ = area(22076, 4, T)

        HT, _ = area(2048, 2, D)
        small, _ = area(4096, 256)
        LG = small[:, 0:64].rearrange("p (n e) -> p n e", n=2)
        MK = small[:, 64:128].rearrange("p (n e) -> p n e", n=2)
        EX = small[:, 128:192].rearrange("p (n e) -> p n e", n=2)
        RK = small[:, 192:256].rearrange("p (n e) -> p n e", n=2)
        TR, _ = area(4352, EXPERTS, EXPERTS)
        CM, _ = area(5376, EXPERTS, EXPERTS)
        CN, _ = area(6400, EXPERTS, EXPERTS)
        small2, _ = area(7424, 512)
        SLOT = small2[:, 0:130].rearrange("p (n e) -> p n e", n=2)
        GT = small2[:, 130:260].rearrange("p (n e) -> p n e", n=2)
        R2 = small2[:, 260:266]
        SS = small2[:, 266:270]
        FLAG = small2[:, 270:271].bitcast(I32)
        YT, _ = area(8192, 2, D)
        ON, _ = area(10240, 2, P)
        PTE, _ = area(10496, 2, P)
        XE, _ = area(11264, KD, P)
        AC, _ = area(13312, D)
        TG, _ = area(14336, 256)
        TU, _ = area(14592, 256)
        SGM, _ = area(14848, 256)
        AT_, _ = area(15360, KD, P)
        YBE, _ = area(16384, D)
        BR, _ = area(17408, 3 * D)
        B3a, _ = area(20480, 3 * D // 2)
        B3 = B3a[:, :].bitcast(BF16)
        T3a, _ = area(22016, 3 * D // 2)
        T3 = T3a[:, :].bitcast(BF16)
        SEa, _ = area(23552, P)
        SELG, SELD = SEa[:, 0:64].bitcast(BF16), SEa[:, 64:128].bitcast(BF16)
        XT, _ = area(26260, 2, D)
        GR, _ = area(28308, D)
        GB, _ = area(29332, KD, P)

        slot_loaded = [sem(f"slot_loaded{i}") for i in range(RING)]
        block_used = sem("block_used")
        vec_loaded, con_loaded, x_loaded = sem("vec_loaded"), sem("con_loaded"), sem("x_loaded")
        zero_ready = sem("zero_ready")
        silu_ready, hidden_ready = sem("silu_ready"), sem("hidden_ready")
        sum_ready, mean_ready, centred, squared = (sem(n) for n in ("sum_ready", "mean_ready", "centred", "squared"))
        var_ready, std_ready, x_ready = sem("var_ready"), sem("std_ready"), sem("x_ready")
        u_copied = sem("u_copied")
        vt_ready, vt_copied = sem("vt_ready"), sem("vt_copied")
        score_ready, score_read = sem("score_ready"), sem("score_read")
        score_shifted, exp_ready, prob_ready = sem("score_shifted"), sem("exp_ready"), sem("prob_ready")
        pt_ready, pt_copied = sem("pt_ready"), sem("pt_copied")
        attn_ready, attn_copied = sem("attn_ready"), sem("attn_copied")
        lru_in, lru_gates, lru_acts, lru_m2 = sem("lru_in"), sem("lru_gates"), sem("lru_acts"), sem("lru_m2")
        lru_mult, lru_done = sem("lru_mult"), sem("lru_done")
        conv_ready, cmean_ready, cc_ready, csq_ready = (sem(n) for n in ("conv_ready", "cmean_ready", "cc_ready", "csq_ready"))
        cvar_ready, cstd_ready, cnorm_ready, conv_done = (sem(n) for n in ("cvar_ready", "cstd_ready", "cnorm_ready", "conv_done"))
        lam_abs = sem("lam_abs")
        tile_done = sem("tile_done")
        glu_half, y_sum = sem("glu_half"), sem("y_sum")
        lam_exp, rel_ready, rv_ready, rv_stored, bias_loaded = (sem(n) for n in ("lam_exp", "rel_ready", "rv_ready", "rv_stored", "bias_loaded"))
        dve_chain, act_chain = sem("dve_chain"), sem("act_chain")
        ctx_loaded = sem("ctx_loaded")
        z_copied = sem("z_copied")
        s2_done, s2_read, s2_shifted, s2_exp, s2_prob = (sem(n) for n in ("s2_done", "s2_read", "s2_shifted", "s2_exp", "s2_prob"))
        p2_done, p2_copied, at_done, at_copied = (sem(n) for n in ("p2_done", "p2_copied", "at_done", "at_copied"))
        lora_done, sig_ready, ll_ready, ex_a, ex_r = sem("lora_done"), sem("sig_ready"), sem("ll_ready"), sem("ex_a"), sem("ex_r")
        ex_inv, feat_ready = sem("ex_inv"), sem("feat_ready")
        m_done, mt_ready, bk_done, bk_ready = (sem(n) for n in ("m_done", "mt_ready", "bk_done", "bk_ready"))
        e_ready, w_done, w_ready, d_done, xz_ready = (sem(n) for n in ("e_ready", "w_done", "w_ready", "d_done", "xz_ready"))
        u0_done, u0_ready, uu_done, uu_ready = (sem(n) for n in ("u0_done", "u0_ready", "uu_done", "uu_ready"))
        s_done, st_ready = sem("s_done"), sem("st_ready")
        tri_one, tri_ready, bias_in = sem("tri_one"), sem("tri_ready"), sem("bias_in")
        tok_done, tok_copied = sem("tok_done"), sem("tok_copied")
        onehot_ready, gather_done, xe_ready = sem("onehot_ready"), sem("gather_done"), sem("xe_ready")
        selg_ready, seld_ready, clipped, sigm_ready, glu_done = (sem(n) for n in ("selg_ready", "seld_ready", "clipped", "sigm_ready", "glu_done"))
        comb_done, comb_read, pt_turned, pte_ready = (sem(n) for n in ("comb_done", "comb_read", "pt_turned", "pte_ready"))
        act_turned, actt_ready, yb_ready = sem("act_turned"), sem("actt_ready"), sem("yb_ready")
        out_stored = sem("out_stored")

        pe_step = sem("pe_step")
        PE_STEP = steps("h_ms", "rot_done", "vk_done", "kk_sum", "vm_done", "y_mean", "rb_sum", "gl_done",
             "y_var", "mix_ms", "f_ms", "lg_done", "pos_done")
        act_step = sem("act_step")
        ACT_STEP = steps("silc_ready", "h_sq", "h_std", "vk_copied", "kk_sq", "tanh_ready", "kk_std",
             "vm_copied", "gl_ready", "y_sq", "y_std", "mix_copied", "mix_std", "f_sq", "f_std",
             "lg_exp", "y_root")
        dve_step = sem("dve_step")
        DVE_STEP = steps("pads_ready", "h_ready", "rot_read", "kk_raw", "kk_used", "rb_ready", "y_centred",
             "rw_ready", "mg_ready", "xm_ready", "f_ready", "gb_ready", "mask_ready", "lg_shift",
             "flag_ready", "moe_ready", "y_ss", "y_final")

        block = ctx.enter_context(nc.Block())
        LB = [l * LAYER_BLOCKS for l in range(LAYERS)]

        @block.sync
        def _(sp):
            sp.dma_start(X[:, :, :], x_t).then_inc(x_loaded, 16)
            sp.dma_start(vec[:, :], vectors).then_inc(vec_loaded, 16)
            sp.dma_start(con[:, :], consts).then_inc(con_loaded, 16)
            for s in range(RING):
                sp.dma_start(ring[:, s, :], weights[s, :, :]).then_inc(slot_loaded[s], 16)
            nblk = BLOCKS if stop > 98 else {1: FFN_BLOCKS, 2: FFN_BLOCKS + 11, 3: 154, 4: 154+24}.get(stop, MOE0)
            rounds = nblk // RING
            with sp.Fori(1, rounds) as r:
                for s in range(RING):
                    sp.wait_ge(block_used, r * RING + (s - RING + 1))
                    sp.dma_start(ring[:, s, :], weights[r * RING + s, :, :]).then_inc(slot_loaded[s], 16)
            for b in range(rounds * RING, nblk):
                sp.wait_ge(block_used, b - RING + 1)
                sp.dma_start(ring[:, b % RING, :], weights[b, :, :]).then_inc(slot_loaded[b % RING], 16)
            if stop > 98:
                sp.wait_ge(dve_step, DVE_STEP["flag_ready"])
                more = sp.value_load(FLAG[0:1, 0:1], min_val=0, max_val=1)
                with sp.If(more > 0):
                    with sp.Fori(0, EXPERTS * EXPERT_BLOCKS // RING) as r:
                        for j in range(RING):
                            b = BLOCKS + j
                            sp.wait_ge(block_used, r * RING + (b - RING + 1))
                            sp.dma_start(ring[:, b % RING, :], weights[r * RING + (MOE0 + j), :, :]).then_inc(slot_loaded[b % RING], 16)
            sp.wait_ge(out_stored, 16)

        @block.gpsimd
        def _(pool):
            pool.wait_ge(rv_ready, 1)
            pool.dma_start(rel_scratch, RV[0:HEADS, :].unsqueeze(1).broadcast_to([HEADS, P, 384])).then_inc(rv_stored, 16)
            pool.wait_ge(rv_stored, 16)
            for h in range(HEADS):
                band = bass.AP(rel_scratch.tensor, h * P * 384 + 127, [[383, P], [1, 256]])
                own = bass.AP(rel_scratch.tensor, h * P * 384 + 127 + P, [[383, P], [1, P]])
                pool.dma_start(BT[:, h, 0, :], own).then_inc(bias_loaded, 16)
                pool.dma_start(BT[:, h, 1:3, :].rearrange("p a b -> p (a b)"), band).then_inc(bias_loaded, 16)
            if stop > 3:
                pool.wait_ge(x_ready, 6)
                pool.dma_start(H[:, :, 0, :], ctx_t).then_inc(ctx_loaded, 16)
            pool.wait_ge(x_ready, 6 if stop > 2 else [1, 2][stop - 1])
            if stop > 98:
                pool.wait_ge(dve_step, DVE_STEP["f_ready"])
                pool.dma_start(BR[0:96, :], moe_bias).then_inc(bias_in, 16)
                nc.gpsimd.memset(TR[:, :, :], 1.0).then_inc(tri_one, 1)
                pool.wait_ge(tri_one, 1)
                nc.gpsimd.affine_select(out=TR[:, :, :], in_=TR[:, :, :], compare_op=ALU.is_gt, fill=0.0, base=0,
                                        pattern=[[1, EXPERTS], [-1, EXPERTS]], channel_multiplier=0).then_inc(tri_ready, 1)
                pool.wait_ge(dve_step, DVE_STEP["y_final"])
                pool.dma_start(out, YT[:, :, :].rearrange("p n d -> p (n d)")).then_inc(out_stored, 16)
            if stop in (96, 97, 98):
                pool.wait_ge(dve_step, DVE_STEP["f_ready"])
            if stop < 99:
                pool.dma_start(out.rearrange("p (a b) -> p a b", b=T), X[:, :, :]).then_inc(out_stored, 16)

        @block.tensor
        def _(pe):
            mm = nc.tensor.matmul

            def loaded(b):
                if isinstance(b, int):
                    pe.wait_ge(slot_loaded[b % RING], 16 * (b // RING + 1))

            def W(b, k):
                return ring[:, b % RING, :].rearrange("p (k n) -> p k n", k=k)

            def ffn(n, base):
                def chunk_gate_up(slot, turns, J, buf):
                    for which in range(2):
                        s = (slot + which) % RING
                        pe.wait_ge(slot_loaded[s], turns[which])
                        if which == 0 and J is not None:
                            pe.wait_ge(hidden_ready, J)
                        w = ring[:, s, :].rearrange("p (k n) -> p k n", k=KD)
                        dst = ps[:, 4 + 2 * which + buf, :].rearrange("p (f t) -> p f t", f=2)
                        for f in range(2):
                            for k in range(KD):
                                last = mm(dst[:, f, :], w[:, k, f * P:(f + 1) * P], X[:, k, :],
                                          start=(k == 0), stop=(k == KD - 1))
                        last.then_inc(block_used, 1)

                def chunk_down(slot, turn, J1, buf):
                    pe.wait_ge(slot_loaded[slot % RING], turn)
                    pe.wait_ge(hidden_ready, J1 + 1)
                    w = ring[:, slot % RING, :].rearrange("p (f n) -> p f n", f=2)
                    for f in range(2):
                        for d in range(KD):
                            last = mm(acc8[:, d, :], w[:, f, d * P:(d + 1) * P], HF[:, buf, f, :],
                                      start=False, stop=False, skip_group_check=True)
                    last.then_inc(block_used, 1)

                for b in range(4):
                    mm(ps[:, b, :], zl, zr, start=True, stop=False, skip_group_check=True)
                J0 = n * FCH

                def turn(b):
                    return 16 * (b // RING + 1)
                chunk_gate_up(base, [turn(base), turn(base + 1)], J0 if n else None, J0 % 2)
                with pe.Fori(0, (FCH - 1) // 2) as i:
                    for h in range(2):
                        b = base + 2 + 3 * h
                        chunk_gate_up(b, [i * 16 + turn(b), i * 16 + turn(b + 1)], i * 2 + (J0 + 1 + h), (J0 + 1 + h) % 2)
                        chunk_down(b + 2, i * 16 + turn(b + 2), i * 2 + (J0 + 1 + h), (J0 + h) % 2)
                chunk_down(base + 2 + 3 * (FCH - 1), turn(base + 2 + 3 * (FCH - 1)), J0 + FCH, (J0 + FCH - 1) % 2)

            acc8 = ps[:, 0:4, :].rearrange("p b (a t) -> p (b a) t", a=2)

            def ln(m):
                pe.wait_ge(sum_ready, m + 1)
                for k in range(KD):
                    last = mm(ps[:, 4, 0:T], C("ones_d"), X[:, k, :], start=(k == 0), stop=(k == KD - 1))
                last.then_inc(mean_ready, 1)
                pe.wait_ge(squared, m + 1)
                for k in range(KD):
                    last = mm(ps[:, 5, 0:T], C("ones_d"), XS[:, k, :], start=(k == 0), stop=(k == KD - 1))
                last.then_inc(var_ready, 1)
                pe.wait_ge(x_ready, m + 1)

            def mixer(l):
                base = LB[l] + FFN_BLOCKS
                for b in range(IN_BLOCKS):
                    loaded(base + b)
                    if b >= 4:
                        pe.wait_ge(u_copied, l * IN_BLOCKS + b - 3)
                    w = W(base + b, KD)
                    dst = ps[:, 4 + b % 4, :].rearrange("p (f t) -> p f t", f=2)
                    for f in range(2):
                        for k in range(KD):
                            last = mm(dst[:, f, :], w[:, k, f * P:(f + 1) * P], X[:, k, :],
                                      start=(k == 0), stop=(k == KD - 1))
                    last.then_inc(block_used, 1)
                pe.wait_ge(u_copied, (l + 1) * IN_BLOCKS)
                for n in range(2):
                    last = nc.tensor.transpose(ps[:, 4, n * P:(n + 1) * P], U[:, 13, n * P:(n + 1) * P], ident)
                last.then_inc(vt_ready, 1)
                pe.wait_ge(lru_in, l + 1)
                for which in range(2):
                    for t in range(2):
                        w = V(f"gate_w{l}", (2 * which + t) * P, P)
                        last = mm(ps[:, 6 + which, t * T:(t + 1) * T], w, XC[:, t, :], start=True, stop=True)
                last.then_inc(lru_gates, 1)
                for h in range(HEADS):
                    g, t = divmod(h, 4)
                    if h >= 4:
                        pe.wait_ge(score_read, l * HEADS + h - 3)
                    for n in range(2):
                        lo, hi = (0, P) if n == 0 else (P, 3 * P)
                        last = mm(ps[:, h % 4, lo:hi], U[g * 64:g * 64 + 64, 8 + t, n * P:(n + 1) * P],
                                  U[g * 64:g * 64 + 64, 12, 0:(n + 1) * P], start=True, stop=True)
                    last.then_inc(score_ready, 1)
                pe.wait_ge(prob_ready, l + 1)
                pe.wait_ge(vt_copied, l + 1)
                pe.wait_ge(lru_acts, l + 1)
                for q in range(6):
                    if q >= 4:
                        pe.wait_ge(pt_copied, l * 6 + q - 3)
                    for i in range(4):
                        n = 4 * q + i
                        last = nc.tensor.transpose(ps[:, 4 + q % 4, i * P:(i + 1) * P], SC[:, n // 3, n % 3, :], ident)
                    last.then_inc(pt_ready, 1)
                pe.wait_ge(pt_copied, (l + 1) * 6)
                for h in range(HEADS):
                    g, t = divmod(h, 4)
                    for n in range(2):
                        dst = ps[g * 64:g * 64 + 64, t // 2, (t % 2) * T + n * P:(t % 2) * T + (n + 1) * P]
                        for j in range(n + 1):
                            last = mm(dst, VT[:, j, g * 64:g * 64 + 64], PT[:, h, n + j, :], start=(j == 0), stop=(j == n))
                last.then_inc(attn_ready, 1)
                pe.wait_ge(conv_ready, l + 1)
                for t in range(2):
                    last = mm(ps[:, 4, 0:T], C("ones_c"), CV[:, t, :], start=(t == 0), stop=(t == 1))
                last.then_inc(cmean_ready, 1)
                pe.wait_ge(csq_ready, l + 1)
                for t in range(2):
                    last = mm(ps[:, 5, 0:T], C("ones_c"), CQ[:, t, :], start=(t == 0), stop=(t == 1))
                last.then_inc(cvar_ready, 1)
                pe.wait_ge(attn_copied, l + 1)
                pe.wait_ge(lru_done, l + 1)
                pe.wait_ge(conv_done, l + 1)
                base += IN_BLOCKS
                for b in range(OUT_BLOCKS):
                    loaded(base + b)
                    w = W(base + b, KD)
                    for f in range(2):
                        for k in range(KD):
                            last = mm(acc8[:, 2 * b + f, :], w[:, k, f * P:(f + 1) * P], YC[:, k, :],
                                      start=(k == 0), stop=(k == KD - 1))
                    last.then_inc(block_used, 1)


            def order(d):
                return list(range(8)) if d == 0 else [3, 2, 1, 0, 7, 6, 5, 4]

            def two(hp):
                return slice(hp * 64, hp * 64 + 64)

            def second():
                pe.wait_ge(act_step, ACT_STEP["silc_ready"])
                for b in range(ADA_BLOCKS):
                    loaded(ADA0 + b)
                    w = W(ADA0 + b, KD)
                    for f in range(2):
                        c = 2 * b + f
                        for k in range(KD):
                            last = mm(ps[:, 6, 2 * c:2 * c + 2], w[:, k, f * P:(f + 1) * P], SILC[:, k, :], start=(k == 0), stop=(k == KD - 1))
                    last.then_inc(block_used, 1)
                pe.wait_ge(act_step, ACT_STEP["h_sq"])
                for k in range(KD):
                    last = mm(ps[:, 7, :], C("ones_d"), HSQ[:, k, :, :].rearrange("p s t -> p (s t)"), start=(k == 0), stop=(k == KD - 1))
                last.then_inc(pe_step, 1)
                pe.wait_ge(dve_step, DVE_STEP["h_ready"])
                for b in range(PROJ_BLOCKS):
                    loaded(PROJ0 + b)
                    w = W(PROJ0 + b, KD)
                    for f in range(2):
                        c = 2 * b + f
                        if c >= ZT:
                            continue
                        if c >= 8:
                            pe.wait_ge(z_copied, c - 7)
                        dst = ps[:, c % 8, :].rearrange("p (s t) -> p s t", s=2)
                        both = 4 <= c < 6 or 10 <= c < 20
                        for k in range(KD):
                            if both:
                                last = mm(ps[:, c % 8, :], w[:, k, f * P:(f + 1) * P], H[:, k, :, :].rearrange("p s t -> p (s t)"), start=(k == 0), stop=(k == KD - 1))
                            else:
                                last = mm(dst[:, 1, :], w[:, k, f * P:(f + 1) * P], H[:, k, 1, :], start=(k == 0), stop=(k == KD - 1))
                        if f == 0:
                            last.then_inc(tile_done, 1)
                    if 2 * b + 1 < ZT:
                        last.then_inc(block_used, 1)
                    else:
                        pe.wait_ge(tile_done, PROJ_BLOCKS)
                        pe.sem_inc(block_used, 1)
                pe.wait_ge(z_copied, ZT)
                for t in range(5):
                    src = QA[:, t, :] if t < 4 else KA[:, 1, :]
                    last = mm(ps[:, t, 0:T], C("rot"), src, start=True, stop=True)
                last.then_inc(pe_step, 1)
                for j in range(4):
                    last = nc.tensor.transpose(ps[:, 5, j * P:(j + 1) * P], VA[:, j // 2, (j % 2) * P:(j % 2 + 1) * P], ident)
                last.then_inc(pe_step, 1)
                pe.wait_ge(dve_step, DVE_STEP["rot_read"])
                pe.wait_ge(act_step, ACT_STEP["vk_copied"])
                for n in range(2):
                    for h in range(HEADS):
                        g, t = divmod(h, 4)
                        if n:
                            if h == 0:
                                pe.wait_ge(at_copied, 1)
                        elif h >= 4:
                            pe.wait_ge(s2_read, h - 3)
                        if n and h >= 4:
                            pe.wait_ge(s2_read, HEADS + h - 3)
                        last = mm(ps[:, h % 4, :], QR[two(g), t, n * P:(n + 1) * P], KR[two(g), :, :].rearrange("p s t -> p (s t)"), start=True, stop=True)
                        last.then_inc(s2_done, 1)
                    pe.wait_ge(s2_prob, n + 1)
                    for q in range(8):
                        if q >= 4:
                            pe.wait_ge(p2_copied, n * 8 + q - 3)
                        for j in range(4):
                            last = nc.tensor.transpose(ps[:, 4 + q % 4, j * P:(j + 1) * P], S2[:, q, j, :], ident)
                        last.then_inc(p2_done, 1)
                    pe.wait_ge(p2_copied, n * 8 + 8)
                    for h in range(HEADS):
                        g, t = divmod(h, 4)
                        for j in range(4):
                            last = mm(ps[two(g), 0, t * P:(t + 1) * P], VK[:, j, g * 64:g * 64 + 64], P2[:, h, j, :], start=(j == 0), stop=(j == 3))
                    last.then_inc(at_done, 1)
                pe.wait_ge(act_step, ACT_STEP["kk_sq"])
                for t in range(4):
                    last = mm(ps[:, 1 + t, :], C("heads_sum"), BF[:, t, :], start=True, stop=True)
                last.then_inc(pe_step, 1)
                pe.wait_ge(act_step, ACT_STEP["kk_std"])
                for c in range(8):
                    for p in range(4):
                        for hp in range(2):
                            at = (c * 4 + p) * CH
                            last = mm(ps[two(hp), 4 + at // 512, at % 512:at % 512 + CH], SH[two(hp), 8 + p, c // 4, (c % 4) * CH:(c % 4 + 1) * CH],
                                      ident[two(hp), two(hp)], start=True, stop=True)
                last.then_inc(pe_step, 1)
                for d in range(2):
                    pe.wait_ge(act_step, ACT_STEP["tanh_ready"])
                    pe.wait_ge(act_step, ACT_STEP["vm_copied"])
                    if d:
                        pe.wait_ge(st_ready, 9)
                    for t in range(4):
                        mm(ps[:, t, :], V("w2", t * P, P)[two(d), :], SH[two(d), 12, :, :].rearrange("p s t -> p (s t)"), start=True, stop=True)
                        last = mm(ps[:, 4 + t, :], V("a2", t * P, P)[two(d), :], SH[two(d), 13, :, :].rearrange("p s t -> p (s t)"), start=True, stop=True)
                    last.then_inc(lora_done, 1)
                    pe.wait_ge(feat_ready, d + 1)
                    for i, c in enumerate(order(d)):
                        B = d * 8 + i
                        cs = slice(c * CH, (c + 1) * CH)
                        for p in range(4):
                            for hp in range(2):
                                for w, src in enumerate((BF, KF)):
                                    last = mm(ps[two(hp), p // 2, (p % 2) * 256 + w * P:(p % 2) * 256 + (w + 1) * P], src[two(hp), p, cs],
                                              AR[two(hp), p, c, :, :].rearrange("p a t -> p (a t)"), start=True, stop=True)
                        last.then_inc(m_done, 1)
                        for w, src in enumerate((BF, KF)):
                            for p in range(4):
                                for hp in range(2):
                                    last = mm(ps[two(hp), 2, (w * 4 + p) * CH:(w * 4 + p + 1) * CH], src[two(hp), p, cs], ident[two(hp), two(hp)], start=True, stop=True)
                        last.then_inc(bk_done, 1)
                        pe.wait_ge(e_ready, 6 * B + 1)
                        for p in range(4):
                            for hp in range(2):
                                last = mm(ps[two(hp), 4, p * CH:(p + 1) * CH], EB[two(hp), 0, p, :], C("eye2")[two(hp), :], start=True, stop=True)
                        last.then_inc(d_done, 1)
                        for n in range(1, 6):
                            pe.wait_ge(e_ready, 6 * B + n + 1)
                            pe.wait_ge(xz_ready, 6 * B + n)
                            for p in range(4):
                                for hp in range(2):
                                    last = mm(ps[two(hp), 4, p * CH:(p + 1) * CH], EB[two(hp), n % 2, p, :], XZ[two(hp), 0, p, :], start=True, stop=True)
                            last.then_inc(w_done, 1)
                            pe.wait_ge(w_ready, 5 * B + n)
                            for p in range(4):
                                for hp in range(2):
                                    mm(ps[two(hp), 5, p * CH:(p + 1) * CH], XZ[two(hp), 1, p, :], WW[two(hp), p, :], start=True, stop=True)
                                    last = mm(ps[two(hp), 5, 256 + p * CH:256 + (p + 1) * CH], WW[two(hp), p, :], XZ[two(hp), 1, p, :], start=True, stop=True)
                            last.then_inc(d_done, 1)
                        pe.wait_ge(st_ready, 9 * d + i + 1)
                        pe.wait_ge(mt_ready, B + 1)
                        for p in range(4):
                            for hp in range(2):
                                mm(ps[two(hp), 3, p * CH:(p + 1) * CH], AR[two(hp), p, c, 0, :], STT[two(hp), p, :], start=True, stop=False)
                                last = mm(ps[two(hp), 3, p * CH:(p + 1) * CH], MT[two(hp), p, 2, :], VM[two(hp), c, p, :], start=False, stop=True)
                        last.then_inc(u0_done, 1)
                        pe.wait_ge(u0_ready, B + 1)
                        pe.wait_ge(xz_ready, 6 * B + 6)
                        for p in range(4):
                            for hp in range(2):
                                last = mm(ps[two(hp), 3, 256 + p * CH:256 + (p + 1) * CH], XZ[two(hp), 1, p, :], U0[two(hp), p, :], start=True, stop=True)
                        last.then_inc(uu_done, 1)
                        pe.wait_ge(uu_ready, B + 1)
                        pe.wait_ge(bk_ready, B + 1)
                        if i >= 4:
                            for p in range(4):
                                for hp in range(2):
                                    dst = ps[two(hp), 6, p * CH:(p + 1) * CH]
                                    mm(dst, STT[two(hp), p, :], AR[two(hp), p, c, 1, :], start=True, stop=False)
                                    mm(dst, UU[two(hp), p, :], MT[two(hp), p, 1, :], start=False, stop=False)
                                    mm(dst, VM[two(hp), c, p, :], MT[two(hp), p, 3, :], start=False, stop=True)
                        for p in range(4):
                            for hp in range(2):
                                dst = ps[two(hp), 7, p * CH:(p + 1) * CH]
                                mm(dst, BK[two(hp), 0, p, :], UU[two(hp), p, :], start=True, stop=False)
                                last = mm(dst, BK[two(hp), 1, p, :], VM[two(hp), c, p, :], start=False, stop=True)
                        last.then_inc(s_done, 1)
                if stop == 96:
                    return
                pe.wait_ge(st_ready, 18)
                hm = C("heads_mean")
                for t in range(4):
                    last = mm(ps[:, t // 2, (t % 2) * T:(t % 2 + 1) * T], hm, YO[:, t, :], start=True, stop=True)
                last.then_inc(pe_step, 1)
                pe.wait_ge(dve_step, DVE_STEP["rb_ready"])
                for t in range(4):
                    last = mm(ps[:, 4 + t // 2, (t % 2) * T:(t % 2 + 1) * T], C("heads_sum"), YB[:, t, :], start=True, stop=True)
                last.then_inc(pe_step, 1)
                pe.wait_ge(act_step, ACT_STEP["gl_ready"])
                for t in range(4):
                    last = mm(ps[:, 6 + t // 2, (t % 2) * T:(t % 2 + 1) * T], V("g2", t * P, P), SH[:, 14, 1, :], start=True, stop=True)
                last.then_inc(pe_step, 1)
                pe.wait_ge(act_step, ACT_STEP["y_sq"])
                for t in range(4):
                    last = mm(ps[:, 2 + t // 2, (t % 2) * T:(t % 2 + 1) * T], hm, YQ[:, t, :], start=True, stop=True)
                last.then_inc(pe_step, 1)
                pe.wait_ge(dve_step, DVE_STEP["rw_ready"])
                for br, src in enumerate((AT, YO)):
                    for b in range(2):
                        blk = UP0 + 2 * br + b
                        loaded(blk)
                        w = W(blk, 4)
                        for dd in range(4):
                            dt = 4 * b + dd
                            for k in range(4):
                                last = mm(ps[:, 4 * br + dt // 2, (dt % 2) * T:(dt % 2 + 1) * T], w[:, k, dd * P:(dd + 1) * P], src[:, k, :], start=(k == 0), stop=(k == 3))
                        last.then_inc(block_used, 1)
                pe.wait_ge(dve_step, DVE_STEP["mg_ready"])
                for b in range(OUT_BLOCKS):
                    loaded(OUT0 + b)
                    w = W(OUT0 + b, KD)
                    for f in range(2):
                        for k in range(KD):
                            last = mm(acc8[:, 2 * b + f, :], w[:, k, f * P:(f + 1) * P], MG[:, k, :], start=(k == 0), stop=(k == KD - 1))
                    last.then_inc(block_used, 1)
                pe.wait_ge(act_step, ACT_STEP["mix_copied"])
                for k in range(KD):
                    last = mm(ps[:, 4, 0:T], C("ones_d"), MH[:, k, :], start=(k == 0), stop=(k == KD - 1))
                last.then_inc(pe_step, 1)
                pe.wait_ge(act_step, ACT_STEP["f_sq"])
                for k in range(KD):
                    last = mm(ps[:, 5, 0:T], C("ones_d"), MH[:, k, :], start=(k == 0), stop=(k == KD - 1))
                last.then_inc(pe_step, 1)


            def moe():
                pe.wait_ge(dve_step, DVE_STEP["f_ready"])
                for k in range(KD):
                    for n in range(2):
                        last = nc.tensor.transpose(ps[:, 2 * n + k // 4, (k % 4) * P:(k % 4 + 1) * P], MG[:, k, n * P:(n + 1) * P], ident)
                last.then_inc(tok_done, 1)
                for k in range(KD):
                    for n in range(2):
                        last = nc.tensor.transpose(ps[:, 4 + 2 * n + k // 4, (k % 4) * P:(k % 4 + 1) * P], X[:, k, n * P:(n + 1) * P], ident)
                last.then_inc(tok_done, 1)
                pe.wait_ge(tok_copied, 1)
                wr = V("w_router", 0, KD * EXPERTS).rearrange("p (k e) -> p k e", k=KD)
                for n in range(2):
                    for k in range(KD):
                        last = mm(ps[:, 0, n * EXPERTS:(n + 1) * EXPERTS], MG[:, k, n * P:(n + 1) * P], wr[:, k, :], start=(k == 0), stop=(k == KD - 1))
                last.then_inc(pe_step, 1)
                pe.wait_ge(dve_step, DVE_STEP["gb_ready"])
                for k in range(KD):
                    last = mm(ps[:, 1 + k // 4, (k % 4) * P:(k % 4 + 1) * P], GB[:, k, :], ident, start=True, stop=True)
                last.then_inc(tok_done, 1)
                pe.wait_ge(dve_step, DVE_STEP["mask_ready"])
                mm(ps[:, 3, 0:EXPERTS], C("before"), MK[:, 0, :], start=True, stop=True)
                mm(ps[:, 3, EXPERTS:2 * EXPERTS], C("ones"), MK[:, 0, :], start=True, stop=False)
                mm(ps[:, 3, EXPERTS:2 * EXPERTS], C("before"), MK[:, 1, :], start=False, stop=True)
                mm(ps[:, 3, 64:64 + EXPERTS], C("ones"), MK[:, 0, :], start=True, stop=False)
                mm(ps[:, 3, 64:64 + EXPERTS], C("ones"), MK[:, 1, :], start=False, stop=True).then_inc(pe_step, 1)
                pe.wait_ge(dve_step, DVE_STEP["moe_ready"])
                pe.wait_ge(tok_copied, 3)

                def gather(E1):
                    pe.wait_ge(onehot_ready, E1)
                    for k in range(KD):
                        for n in range(2):
                            last = mm(ps[:, 2 + k // 4, (k % 4) * P:(k % 4 + 1) * P], HT[:, n, k * P:(k + 1) * P], ON[:, n, :], start=(n == 0), stop=(n == 1))
                    last.then_inc(gather_done, 1)

                def combine(E):
                    pe.wait_ge(yb_ready, E + 1)
                    pe.wait_ge(comb_read, E * 2 + 1)
                    for n in range(2):
                        for half in range(2):
                            last = mm(ps[:, (6, 2)[n] + half, :], PTE[:, n, :], YBE[:, half * 512:(half + 1) * 512], start=True, stop=True)
                        last.then_inc(comb_done, 1)

                gather(1)

                def expert(E):
                    def products(dst, stationary, first):
                        for k in range(KD):
                            j = first + k // 4
                            b = MOE0 + j
                            if k % 4 == 0:
                                pe.wait_ge(slot_loaded[b % RING], E * 32 + 16 * (b // RING + 1))
                            last = mm(dst, stationary[:, k, :], ring[:, b % RING, (k % 4) * 512:(k % 4 + 1) * 512], start=False, stop=(k == KD - 1))
                            if k % 4 == 3:
                                last.then_inc(block_used, 1)

                    pe.wait_ge(xe_ready, E + 1)
                    pe.wait_ge(selg_ready, E + 1)
                    for c in range(4):
                        if c >= 2:
                            pe.wait_ge(clipped, E * 4 + (c - 1))
                        mm(ps[:, c % 2, :], SELG[0:96, :], B3[0:96, c * 512:(c + 1) * 512], start=True, stop=False)
                        products(ps[:, c % 2, :], XE, 2 * c)
                        if c == 0:
                            combine(E)
                        if c == 1:
                            pe.wait_ge(comb_read, E * 2 + 2)
                            for n in range(2):
                                last = nc.tensor.transpose(ps[:, 6, n * P:(n + 1) * P], ON[:, n, :], ident)
                            last.then_inc(pt_turned, 1)
                    pe.wait_ge(comb_read, E * 2 + 3)
                    gather(E + 2)
                    pe.wait_ge(glu_done, E * 4 + 5)
                    for k in range(KD):
                        last = nc.tensor.transpose(ps[:, 4 + k // 4, (k % 4) * P:(k % 4 + 1) * P], AC[:, k * P:(k + 1) * P], ident)
                    last.then_inc(act_turned, 1)
                    pe.wait_ge(actt_ready, E + 1)
                    pe.wait_ge(seld_ready, E + 1)
                    for half in range(2):
                        mm(ps[:, 4 + half, :], SELD[0:96, :], B3[0:96, 2048 + half * 512:2048 + (half + 1) * 512], start=True, stop=False)
                        products(ps[:, 4 + half, :], AT_, 8 + 2 * half)

                with pe.Fori(0, EXPERTS) as E:
                    expert(E)
                more = pe.value_load(FLAG[0:1, 0:1], min_val=0, max_val=1)
                with pe.If(more > 0):
                    with pe.Fori(EXPERTS, 2 * EXPERTS) as E:
                        expert(E)
                    combine(2 * EXPERTS)
                with pe.Else():
                    combine(EXPERTS)

            pe.wait_ge(x_loaded, 16)
            pe.wait_ge(vec_loaded, 16)
            pe.wait_ge(con_loaded, 16)
            pe.wait_ge(zero_ready, 1)
            mm(ps[0:HEADS, 7, 0:P], V("rel_bias", 0, HEADS)[0:32, :], C("bucket")[0:32, :],
               start=True, stop=True).then_inc(rel_ready, 1)
            pe.wait_ge(rv_ready, 1)
            for l in range(LAYERS):
                ffn(2 * l, LB[l])
                ln(3 * l)
                if stop == 1:
                    return
                mixer(l)
                ln(3 * l + 1)
                if stop == 2:
                    return
                ffn(2 * l + 1, LB[l] + FFN_BLOCKS + IN_BLOCKS + OUT_BLOCKS)
                ln(3 * l + 2)
            if stop > 3:
                second()
            if stop > 98:
                moe()

        @block.scalar
        def _(act):
            A = nc.scalar.activation

            def ffn(n, base):
                def silu(used, buf, prev):
                    act.wait_ge(block_used, used)
                    if prev is not None:
                        act.wait_ge(hidden_ready, prev + 1)
                    A(SG[:, buf, :, :].rearrange("p f t -> p (f t)"), ps[:, 4 + buf, :], ACT.Silu).then_inc(silu_ready, 1)
                J0 = n * FCH
                silu(base + 1, J0 % 2, J0 - 1 if n else None)
                with act.Fori(0, (FCH - 1) // 2) as i:
                    for h in range(2):
                        silu(i * 6 + (base + 3 + 3 * h), (J0 + 1 + h) % 2, i * 2 + (J0 + h))

            def ln(m):
                act.wait_ge(centred, m + 1)
                A(XS[:, :, :], X[:, :, :], ACT.Square).then_inc(squared, 1)
                act.wait_ge(var_ready, m + 1)
                A(ST[:, 0, 0:T], ps[:, 5, 0:T], ACT.Sqrt, bias=EPS2[:, 0:1]).then_inc(std_ready, 1)

            def mixer(l):
                for b in range(IN_BLOCKS):
                    act.wait_ge(block_used, LB[l] + FFN_BLOCKS + b + 1)
                    src = ps[:, 4 + b % 4, :].rearrange("p (f t) -> p f t", f=2)
                    if b == 1:
                        A(U[:, 2:4, :], src, ACT.Sigmoid).then_inc(u_copied, 1)
                    elif b == 2:
                        A(XB[:, :, LTAPS - 1:], src, ACT.Copy).then_inc(u_copied, 1)
                    else:
                        A(U[:, 2 * b:2 * b + 2, :], src, ACT.Copy).then_inc(u_copied, 1)
                act.wait_ge(vt_ready, l + 1)
                A(VT[:, :, :].rearrange("p a b -> p (a b)"), ps[:, 4, 0:2 * P], ACT.Copy).then_inc(vt_copied, 1)
                act.wait_ge(lru_gates, l + 1)
                for which, bias in ((0, "ba"), (1, "bx")):
                    for t in range(2):
                        last = A(LR[:, which, t, :], ps[:, 6 + which, t * T:(t + 1) * T], ACT.Sigmoid, bias=V(f"{bias}{l}", t))
                        last.then_inc(act_chain, 1)
                act.wait_ge(act_chain, l * 4 + 4)
                for t in range(2):
                    A(LR[:, 2, t, :], LR[:, 0, t, :], ACT.Exp, scale=LC[:, 2 * l + t:2 * l + t + 1])
                    last = A(LR[:, 3, t, :], LR[:, 0, t, :], ACT.Tanh, scale=LN_[:, 2 * l + t:2 * l + t + 1])
                A(LR[:, 7, :, :], U[:, 6:8, :], ACT.Gelu_apprx_tanh).then_inc(lru_acts, 1)
                act.wait_ge(score_shifted, l + 1)
                A(SC[:, :, :, :], SC[:, :, :, :], ACT.Exp)
                A(ES[:, :, :], ES[:, :, :], ACT.Exp).then_inc(exp_ready, 1)
                act.wait_ge(lru_m2, l + 1)
                A(LR[:, 4, :, :], LR[:, 3, :, :], ACT.Sqrt).then_inc(lru_mult, 1)
                for q in range(6):
                    act.wait_ge(pt_ready, l * 6 + q + 1)
                    A(PT[:, :, :, :].rearrange("p h a b -> p (h a b)")[:, q * 512:(q + 1) * 512], ps[:, 4 + q % 4, :],
                      ACT.Copy).then_inc(pt_copied, 1)
                act.wait_ge(attn_ready, l + 1)
                A(YC[:, 4:8, :].rearrange("p (b a) t -> p b (a t)", a=2), ps[:, 0:2, :], ACT.Copy).then_inc(attn_copied, 1)
                act.wait_ge(cc_ready, l + 1)
                A(CQ[:, :, :], CV[:, :, :], ACT.Square).then_inc(csq_ready, 1)
                act.wait_ge(cvar_ready, l + 1)
                A(ST[:, 1, 0:T], ps[:, 5, 0:T], ACT.Sqrt, bias=EPS2[:, 0:1]).then_inc(cstd_ready, 1)
                act.wait_ge(cnorm_ready, l + 1)
                for t in range(2):
                    last = A(YC[:, t, :], CV[:, t, :], ACT.Silu, scale=V(f"cln_g{l}", t), bias=V(f"cln_b{l}", t))
                last.then_inc(conv_done, 1)


            def second():
                act.wait_ge(x_ready, 6)
                A(SILC[:, :, :], V("c", 0, 16).rearrange("p (k s) -> p k s", s=2), ACT.Silu).then_inc(act_step, 1)
                act.wait_ge(ctx_loaded, 16)
                for s_, src in enumerate((H[:, :, 0, :], X[:, :, :])):
                    last = A(HSQ[:, :, s_, :], src, ACT.Square)
                last.then_inc(act_step, 1)
                act.wait_ge(pe_step, PE_STEP["h_ms"])
                A(RS[:, :, :].rearrange("p s t -> p (s t)"), ps[:, 7, :], ACT.Sqrt, bias=EPS2[:, 1:2]).then_inc(act_step, 1)
                for c in range(ZT):
                    if c % 2 == 0:
                        act.wait_ge(tile_done, c // 2 + 1)
                    else:
                        act.wait_ge(block_used, PROJ0 + c // 2 + 1)
                    if c == 0:
                        act.wait_ge(dve_step, DVE_STEP["pads_ready"])
                    src = ps[:, c % 8, :].rearrange("p (s t) -> p s t", s=2)
                    b = V("b_in", c)
                    if c < 4:
                        A(QA[:, c, :], src[:, 1, :], ACT.Identity, bias=b).then_inc(z_copied, 1)
                    elif c < 6:
                        A((KA, VA)[c - 4][:, :, :], src, ACT.Identity, bias=b).then_inc(z_copied, 1)
                    elif c < 21:
                        s0 = 0 if 10 <= c < 20 else 1
                        A(ZR[:, c - 6, s0:2, 1:T + 1], src[:, s0:2, :], ACT.Identity, bias=b).then_inc(z_copied, 1)
                    else:
                        A(G[:, c - 21, :], src[:, 1, :], ACT.Sigmoid, bias=b).then_inc(z_copied, 1)
                act.wait_ge(pe_step, PE_STEP["vk_done"])
                A(VK[:, :, :].rearrange("p a b -> p (a b)"), ps[:, 5, :], ACT.Copy).then_inc(act_step, 1)
                for n in range(2):
                    act.wait_ge(s2_shifted, n + 1)
                    A(S2[:, :, :, :], S2[:, :, :, :], ACT.Exp)
                    A(ES2, ES2, ACT.Exp).then_inc(s2_exp, 1)
                    for q in range(8):
                        act.wait_ge(p2_done, n * 8 + q + 1)
                        if n and q == 0:
                            act.wait_ge(at_done, 1)
                        A(P2[:, q, :, :].rearrange("p a b -> p (a b)"), ps[:, 4 + q % 4, :], ACT.Copy).then_inc(p2_copied, 1)
                    act.wait_ge(at_done, n + 1)
                    A(AT[:, :, n * P:(n + 1) * P], ps[:, 0, :].rearrange("p (a b) -> p a b", a=4), ACT.Copy).then_inc(at_copied, 1)
                act.wait_ge(dve_step, DVE_STEP["kk_raw"])
                A(BF[:, :, :], KK[:, :, :], ACT.Square).then_inc(act_step, 1)
                A(SH[:, 12, :, :], SH[:, 12, :, :], ACT.Tanh).then_inc(act_step, 1)
                act.wait_ge(pe_step, PE_STEP["kk_sum"])
                A(BF[:, :, :], ps[:, 1:5, :], ACT.Sqrt).then_inc(act_step, 1)
                act.wait_ge(pe_step, PE_STEP["vm_done"])
                A(VM[:, :, :, :].rearrange("p (b c) d e -> p b (c d e)", b=4), ps[:, 4:8, :], ACT.Copy).then_inc(act_step, 1)
                for d in range(2):
                    act.wait_ge(lora_done, d + 1)
                    act.wait_ge(dve_step, DVE_STEP["kk_used"])
                    for t in range(4):
                        A(KF[:, t, :], ps[:, t, :], ACT.Sigmoid, bias=V("w0", 4 * d + t))
                        last = A(BF[:, t, :], ps[:, 4 + t, :], ACT.Sigmoid, bias=V("a0", 4 * d + t))
                    last.then_inc(sig_ready, 1)
                    act.wait_ge(ll_ready, d + 1)
                    l8 = LL[:, :, :].rearrange("p t (c e) -> p (t c) e", e=CH)
                    ar = AR[:, :, :, :, :].rearrange("p t c a e -> p (t c) a e")
                    A(PC[:, :, :], TOT[:, :, :], ACT.Exp)
                    A(ar[:, :, 0, :], ar[:, :, 0, :], ACT.Exp).then_inc(ex_a, 1)
                    A(ar[:, :, 1, :], l8, ACT.Exp).then_inc(ex_r, 1)
                    act.wait_ge(ex_r, d + 1)
                    A(LL[:, :, :], LL[:, :, :], ACT.Exp, scale=-1.0).then_inc(ex_inv, 1)
                    for i in range(8):
                        B = d * 8 + i
                        act.wait_ge(bk_done, B + 1)
                        if B:
                            act.wait_ge(s_done, B)
                        A(BK[:, :, :, :].rearrange("p w a b -> p (w a b)"), ps[:, 2, :], ACT.Copy).then_inc(bk_ready, 1)
                        for n in range(1, 6):
                            act.wait_ge(w_done, 5 * B + n)
                            A(WW[:, :, :].rearrange("p a b -> p (a b)"), ps[:, 4, 0:256], ACT.Copy).then_inc(w_ready, 1)
                        act.wait_ge(u0_done, B + 1)
                        A(U0[:, :, :].rearrange("p a b -> p (a b)"), ps[:, 3, 0:256], ACT.Copy).then_inc(u0_ready, 1)
                        act.wait_ge(uu_done, B + 1)
                        A(UU[:, :, :].rearrange("p a b -> p (a b)"), ps[:, 3, 256:512], ACT.Copy).then_inc(uu_ready, 1)
                if stop == 96:
                    return
                A(SH[:, 14, 1, :], SH[:, 14, 1, :], ACT.Sigmoid).then_inc(act_step, 1)
                act.wait_ge(dve_step, DVE_STEP["y_centred"])
                A(YQ[:, :, :], YO[:, :, :], ACT.Square).then_inc(act_step, 1)
                act.wait_ge(pe_step, PE_STEP["y_var"])
                A(YQ[:, :, :].rearrange("p (b a) t -> p b (a t)", b=2), ps[:, 2:4, :], ACT.Sqrt, bias=EPS2[:, 2:3]).then_inc(act_step, 1)
                act.wait_ge(block_used, OUT0 + OUT_BLOCKS)
                A(MH[:, :, :].rearrange("p (b a) t -> p b (a t)", a=2), ps[:, 0:4, :], ACT.Square).then_inc(act_step, 1)
                act.wait_ge(pe_step, PE_STEP["mix_ms"])
                A(RS[:, 0, :], ps[:, 4, 0:T], ACT.Sqrt, bias=EPS2[:, 1:2]).then_inc(act_step, 1)
                act.wait_ge(dve_step, DVE_STEP["xm_ready"])
                A(MH[:, :, :], X[:, :, :], ACT.Square).then_inc(act_step, 1)
                act.wait_ge(pe_step, PE_STEP["f_ms"])
                A(RS[:, 1, :], ps[:, 5, 0:T], ACT.Sqrt, bias=EPS2[:, 1:2]).then_inc(act_step, 1)


            def moe():
                act.wait_ge(tok_done, 1)
                A(HT[:, :, :].rearrange("p n d -> p (n d)"), ps[:, 0:4, :].rearrange("p b n -> p (b n)"), ACT.Copy).then_inc(tok_copied, 1)
                act.wait_ge(tok_done, 2)
                A(XT[:, :, :].rearrange("p n d -> p (n d)"), ps[:, 4:8, :].rearrange("p b n -> p (b n)"), ACT.Copy).then_inc(tok_copied, 1)
                act.wait_ge(tok_done, 3)
                A(GR[:, :], ps[:, 1:3, :].rearrange("p b n -> p (b n)"), ACT.Copy).then_inc(tok_copied, 1)
                act.wait_ge(dve_step, DVE_STEP["lg_shift"])
                A(EX[:, :, :], EX[:, :, :], ACT.Exp).then_inc(act_step, 1)

                def tokens(E1):
                    act.wait_ge(gather_done, E1)
                    A(XE[:, :, :].rearrange("p k n -> p (k n)"), ps[:, 2:4, :].rearrange("p b n -> p (b n)"), ACT.Copy).then_inc(xe_ready, 1)

                act.sem_inc(yb_ready, 1)
                tokens(1)

                def expert(E, used):
                    for c in range(4):
                        act.wait_ge(clipped, E * 4 + (c + 1))
                        if c:
                            act.wait_ge(glu_done, E * 4 + (c + 1))
                        A(SGM[:, :], TG[:, :], ACT.Sigmoid, scale=1.702).then_inc(sigm_ready, 1)
                        if c == 1:
                            act.wait_ge(pt_turned, E + 1)
                            A(PTE[:, :, :].rearrange("p n s -> p (n s)"), ps[:, 6, 0:2 * P], ACT.Copy).then_inc(pte_ready, 1)
                    tokens(E + 2)
                    act.wait_ge(act_turned, E + 1)
                    A(AT_[:, :, :].rearrange("p k n -> p (k n)"), ps[:, 4:6, :].rearrange("p b n -> p (b n)"), ACT.Copy).then_inc(actt_ready, 1)
                    act.wait_ge(block_used, used + EXPERT_BLOCKS)
                    A(YBE[:, :], ps[:, 4:6, :].rearrange("p b n -> p (b n)"), ACT.Copy).then_inc(yb_ready, 1)

                with act.Fori(0, EXPERTS) as E:
                    expert(E, E * EXPERT_BLOCKS + MOE0)
                more = act.value_load(FLAG[0:1, 0:1], min_val=0, max_val=1)
                with act.If(more > 0):
                    with act.Fori(EXPERTS, 2 * EXPERTS) as E:
                        expert(E, E * EXPERT_BLOCKS + MOE0)
                act.wait_ge(dve_step, DVE_STEP["y_ss"])
                for n in range(2):
                    last = A(SS[:, n:n + 1], SS[:, n:n + 1], ACT.Sqrt, bias=EPS2[:, 1:2], scale=1.0 / D)
                last.then_inc(act_step, 1)

            act.wait_ge(vec_loaded, 16)
            act.wait_ge(zero_ready, 1)
            A(LT[:, 0, :], V("lam", 0, 2 * LAYERS), ACT.Abs).then_inc(lam_abs, 1)
            act.wait_ge(lam_abs, 1)
            A(LT[:, 1, :], LT[:, 0, :], ACT.Exp, scale=-1.0).then_inc(lam_exp, 1)
            act.wait_ge(lam_exp, 1)
            for l in range(LAYERS):
                ffn(2 * l, LB[l])
                ln(3 * l)
                if stop == 1:
                    return
                mixer(l)
                ln(3 * l + 1)
                if stop == 2:
                    return
                ffn(2 * l + 1, LB[l] + FFN_BLOCKS + IN_BLOCKS + OUT_BLOCKS)
                ln(3 * l + 2)
            if stop > 3:
                second()
            if stop > 98:
                moe()

        @block.vector
        def _(dve):
            v = nc.vector
            chain = [0]

            def link(ins):
                chain[0] += 1
                ins.then_inc(dve_chain, 1)
                dve.wait_ge(dve_chain, chain[0])

            acc8 = ps[:, 0:4, :].rearrange("p b (a t) -> p (b a) t", a=2)

            def ffn(n, base):
                def hidden(J1, buf, used):
                    dve.wait_ge(silu_ready, J1)
                    dve.wait_ge(block_used, used)
                    v.tensor_tensor(HF[:, buf, :, :].rearrange("p f t -> p (f t)"), ps[:, 6 + buf, :],
                                    SG[:, buf, :, :].rearrange("p f t -> p (f t)"), ALU.mult).then_inc(hidden_ready, 1)
                J0 = n * FCH
                hidden(J0 + 1, J0 % 2, base + 2)
                with dve.Fori(0, (FCH - 1) // 2) as i:
                    for h in range(2):
                        hidden(i * 2 + (J0 + 2 + h), (J0 + 1 + h) % 2, i * 6 + (base + 4 + 3 * h))

            def ln(m, scale, used):
                dve.wait_ge(block_used, used)
                link(v.tensor_scalar(XS[:, :, :], acc8, scale, None, ALU.mult))
                v.scalar_tensor_tensor(out=X[:, :, :], in0=X[:, :, :], scalar=ALPHA, in1=XS[:, :, :],
                                       op0=ALU.mult, op1=ALU.add).then_inc(sum_ready, 1)
                dve.wait_ge(mean_ready, m + 1)
                link(v.tensor_copy(ST[:, 2, 0:T], ps[:, 4, 0:T]))
                v.tensor_tensor(X[:, :, :], X[:, :, :], ST[:, 2, 0:T].unsqueeze(1).broadcast_to([P, KD, T]),
                                ALU.subtract).then_inc(centred, 1)
                dve.wait_ge(std_ready, m + 1)
                link(v.reciprocal(ST[:, 3, 0:T], ST[:, 0, 0:T]))
                dve.wait_ge(squared, m + 1)
                link(v.tensor_tensor(X[:, :, :], X[:, :, :], ST[:, 3, 0:T].unsqueeze(1).broadcast_to([P, KD, T]), ALU.mult))
                for k in range(KD):
                    last = v.tensor_scalar(X[:, k, :], X[:, k, :], V("ln_g", m * KD + k), V("ln_b", m * KD + k), ALU.mult, ALU.add)
                last.then_inc(x_ready, 1)

            def mixer(l):
                dve.wait_ge(u_copied, l * IN_BLOCKS + 3)
                for t in range(2):
                    for j in range(LTAPS):
                        w = V(f"lw{l}", t * LTAPS + j)
                        if j == 0:
                            ins = v.tensor_scalar(XC[:, t, :], XB[:, t, 0:T], w, V(f"lb{l}", t), ALU.mult, ALU.add)
                        else:
                            ins = v.scalar_tensor_tensor(out=XC[:, t, :], in0=XB[:, t, j:j + T], scalar=w, in1=XC[:, t, :], op0=ALU.mult, op1=ALU.add)
                        link(ins)
                dve.sem_inc(lru_in, 1)
                dve.wait_ge(bias_loaded, 16 * 2 * HEADS)
                for h in range(HEADS):
                    dve.wait_ge(score_ready, l * HEADS + h + 1)
                    v.scalar_tensor_tensor(out=SC[:, h, :, :].rearrange("p a b -> p (a b)"), in0=ps[:, h % 4, 0:3 * P], scalar=0.125,
                                           in1=BT[:, h, :, :].rearrange("p a b -> p (a b)"),
                                           op0=ALU.mult, op1=ALU.add).then_inc(score_read, 1)
                dve.wait_ge(score_read, (l + 1) * HEADS)
                sink = V(f"sink{l}", 0, HEADS)
                link(v.tensor_reduce(M3[:, :, :], SC[:, :, :, :], AX.X, ALU.max))
                link(v.tensor_tensor(MM[:, :, 1], M3[:, :, 1], M3[:, :, 2], ALU.max))
                v.tensor_tensor(MM[:, :, 0], M3[:, :, 0], sink, ALU.max)
                link(v.tensor_tensor(MM[:, :, 1], MM[:, :, 1], sink, ALU.max))
                link(v.tensor_copy(MM[:, :, 2], MM[:, :, 1]))
                v.tensor_tensor(ES[:, :, :], sink.unsqueeze(2).broadcast_to([P, HEADS, 2]), MM[:, :, 0:2], ALU.subtract)
                v.tensor_tensor(SC[:, :, :, :].rearrange("p h a b -> p (h a) b"), SC[:, :, :, :].rearrange("p h a b -> p (h a) b"),
                                MM[:, :, :].rearrange("p h a -> p (h a)").unsqueeze(2).broadcast_to([P, HEADS * 3, P]),
                                ALU.subtract).then_inc(score_shifted, 1)
                dve.wait_ge(exp_ready, l + 1)
                link(v.tensor_reduce(S3[:, :, :], SC[:, :, :, :], AX.X, ALU.add))
                link(v.tensor_tensor(S3[:, :, 1], S3[:, :, 1], S3[:, :, 2], ALU.add))
                link(v.tensor_tensor(DN[:, :, :], S3[:, :, 0:2], ES[:, :, :], ALU.add))
                link(v.reciprocal(S3[:, :, 0:2], DN[:, :, :]))
                link(v.tensor_copy(S3[:, :, 2], S3[:, :, 1]))
                v.tensor_tensor(SC[:, :, :, :].rearrange("p h a b -> p (h a) b"), SC[:, :, :, :].rearrange("p h a b -> p (h a) b"),
                                S3[:, :, :].rearrange("p h a -> p (h a)").unsqueeze(2).broadcast_to([P, HEADS * 3, P]),
                                ALU.mult).then_inc(prob_ready, 1)
                dve.wait_ge(lru_acts, l + 1)
                link(v.tensor_tensor(LR[:, 5, :, :], LR[:, 2, :, :], LR[:, 2, :, :], ALU.mult))
                v.scalar_tensor_tensor(out=LR[:, 3, :, :], in0=LR[:, 5, :, :], scalar=1.0, in1=LR[:, 3, :, :],
                                       op0=ALU.add, op1=ALU.mult).then_inc(lru_m2, 1)
                link(v.tensor_tensor(LR[:, 1, :, :], LR[:, 1, :, :], XC[:, :, :], ALU.mult))
                dve.wait_ge(lru_mult, l + 1)
                link(v.tensor_tensor(LR[:, 1, :, :], LR[:, 1, :, :], LR[:, 4, :, :], ALU.mult))
                for t in range(2):
                    last = v.tensor_tensor_scan(LR[:, 6, t, :], LR[:, 2, t, :], LR[:, 1, t, :], 0.0, ALU.mult, ALU.add)
                link(last)
                v.tensor_tensor(YC[:, 2:4, :], LR[:, 6, :, :], LR[:, 7, :, :], ALU.mult).then_inc(lru_done, 1)
                link(v.tensor_tensor(YP[:, :, TAPS - 1:], U[:, 0:2, :], U[:, 2:4, :], ALU.mult))
                for j in range(TAPS):
                    for t in range(2):
                        w = V(f"dw_w{l}", t * TAPS + j)
                        if j == 0:
                            last = v.tensor_scalar(CV[:, t, :], YP[:, t, 0:T], w, V(f"dw_b{l}", t), ALU.mult, ALU.add)
                        else:
                            last = v.scalar_tensor_tensor(out=CV[:, t, :], in0=YP[:, t, j:j + T], scalar=w, in1=CV[:, t, :], op0=ALU.mult, op1=ALU.add)
                    link(last)
                dve.sem_inc(conv_ready, 1)
                dve.wait_ge(cmean_ready, l + 1)
                link(v.tensor_copy(ST[:, 2, 0:T], ps[:, 4, 0:T]))
                v.tensor_tensor(CV[:, :, :], CV[:, :, :], ST[:, 2, 0:T].unsqueeze(1).broadcast_to([P, 2, T]), ALU.subtract).then_inc(cc_ready, 1)
                dve.wait_ge(cstd_ready, l + 1)
                link(v.reciprocal(ST[:, 3, 0:T], ST[:, 1, 0:T]))
                v.tensor_tensor(CV[:, :, :], CV[:, :, :], ST[:, 3, 0:T].unsqueeze(1).broadcast_to([P, 2, T]), ALU.mult).then_inc(cnorm_ready, 1)

            dve.sem_inc(hidden_ready, 1)

            def second():
                dve.wait_ge(x_ready, 6)
                v.memset(ZR[:, :, :, 0:1], 0.0)
                v.memset(ZR[:, :, :, T + 1:T + 2], 0.0).then_inc(dve_step, 1)
                link(v.memset(RESET[:, :, :], 1.0))
                v.memset(RESET[:, :, 0:1], 0.0)
                dve.wait_ge(block_used, ADA0 + ADA_BLOCKS)
                link(v.tensor_tensor(ADA[:, :, :], ps[:, 6, 0:96].rearrange("p (c s) -> p c s", s=2),
                                     V("b_ada", 0, 48).unsqueeze(2).broadcast_to([P, 48, 2]), ALU.add))
                for s_ in range(2):
                    link(v.scalar_tensor_tensor(out=GS[:, :, s_], in0=ADA[:, 8:16, s_], scalar=1.0, in1=V("g_pre_mix", 0, 8), op0=ALU.add, op1=ALU.mult))
                link(v.tensor_tensor(GP, ADA[:, 16:24, 1], V("g_post_mix", 0, 8), ALU.mult))
                link(v.scalar_tensor_tensor(out=GF, in0=ADA[:, 32:40, 1], scalar=1.0, in1=V("g_pre_ffn", 0, 8), op0=ALU.add, op1=ALU.mult))
                link(v.tensor_tensor(GQ, ADA[:, 40:48, 1], V("g_post_ffn", 0, 8), ALU.mult))
                dve.wait_ge(act_step, ACT_STEP["h_std"])
                link(v.reciprocal(RS[:, :, :], RS[:, :, :]))
                v.tensor_tensor(H[:, :, 0, :], H[:, :, 0, :], RS[:, 0, :].unsqueeze(1).broadcast_to([P, KD, T]), ALU.mult)
                link(v.tensor_tensor(H[:, :, 1, :], X[:, :, :], RS[:, 1, :].unsqueeze(1).broadcast_to([P, KD, T]), ALU.mult))
                for k in range(KD):
                    for s_ in range(2):
                        last = v.tensor_scalar(H[:, k, s_, :], H[:, k, s_, :], GS[:, k, s_:s_ + 1], ADA[:, k, s_:s_ + 1], ALU.mult, ALU.add)
                last.then_inc(dve_step, 1)
                dve.wait_ge(pe_step, PE_STEP["rot_done"])
                for t in range(5):
                    src, dst = (QA[:, t, :], QR[:, t, :]) if t < 4 else (KA[:, 1, :], KR[:, 1, :])
                    link(v.tensor_tensor(dst, ps[:, t, 0:T], C("sin"), ALU.mult))
                    link(v.tensor_tensor(src, src, C("cos"), ALU.mult))
                    link(v.tensor_tensor(dst, dst, src, ALU.add))
                v.tensor_copy(KR[:, 0, :], KA[:, 0, :]).then_inc(dve_step, 1)
                for c in range(15):
                    s0 = 0 if 4 <= c < 14 else 1
                    z = ZR[:, c, s0:2, :]
                    dst = SH[:, c, s0:2, :]
                    link(v.tensor_tensor(dst, z[:, :, 0:T], z[:, :, 1:T + 1], ALU.subtract))
                    link(v.scalar_tensor_tensor(out=dst, in0=dst, scalar=V("mu_prev", c), in1=z[:, :, 1:T + 1], op0=ALU.mult, op1=ALU.add))
                    link(v.scalar_tensor_tensor(out=dst, in0=z[:, :, 2:T + 2], scalar=V("mu_next", c), in1=dst, op0=ALU.mult, op1=ALU.add))
                    link(v.tensor_scalar(TN, V("mu_next", c), -1.0, None, ALU.mult))
                    link(v.scalar_tensor_tensor(out=dst, in0=z[:, :, 1:T + 1], scalar=TN, in1=dst, op0=ALU.mult, op1=ALU.add))
                for n in range(2):
                    m2 = C("mask2")[:, n * T:(n + 1) * T]
                    for h in range(HEADS):
                        dve.wait_ge(s2_done, n * HEADS + h + 1)
                        if n == 1 and h == 0:
                            dve.wait_ge(at_copied, 1)
                        v.tensor_scalar(S2[:, h, 0:2, :].rearrange("p a b -> p (a b)"), ps[:, h % 4, 0:T], 0.125, None, ALU.mult)
                        v.scalar_tensor_tensor(out=S2[:, h, 2:4, :].rearrange("p a b -> p (a b)"), in0=ps[:, h % 4, T:2 * T], scalar=0.125,
                                               in1=m2, op0=ALU.mult, op1=ALU.add).then_inc(s2_read, 1)
                    dve.wait_ge(s2_read, (n + 1) * HEADS)
                    s3 = S2[:, :, :, :].rearrange("p h a b -> p h (a b)")
                    link(v.tensor_reduce(MX, s3, AX.X, ALU.max))
                    link(v.tensor_tensor(MX, MX, V("sink2", 0, HEADS), ALU.max))
                    v.tensor_tensor(ES2, V("sink2", 0, HEADS), MX, ALU.subtract)
                    v.tensor_tensor(s3, s3, MX.unsqueeze(2).broadcast_to([P, HEADS, 512]), ALU.subtract).then_inc(s2_shifted, 1)
                    dve.wait_ge(s2_exp, n + 1)
                    link(v.tensor_reduce(DN2, s3, AX.X, ALU.add))
                    link(v.tensor_tensor(DN2, DN2, ES2, ALU.add))
                    link(v.reciprocal(DN2, DN2))
                    v.tensor_tensor(s3, s3, DN2.unsqueeze(2).broadcast_to([P, HEADS, 512]), ALU.mult).then_inc(s2_prob, 1)
                dve.wait_ge(at_done, 2)
                for t in range(4):
                    last = v.tensor_scalar(KK[:, t, :], SH[:, 4 + t, :, :].rearrange("p s t -> p (s t)"), V("k_k", t), None, ALU.mult)
                last.then_inc(dve_step, 1)
                dve.wait_ge(act_step, ACT_STEP["kk_std"])
                link(v.tensor_scalar(BF[:, :, :], BF[:, :, :], 1e-12, None, ALU.max))
                link(v.reciprocal(BF[:, :, :], BF[:, :, :]))
                link(v.tensor_tensor(KK[:, :, :], KK[:, :, :], BF[:, :, :], ALU.mult))
                dve.sem_inc(dve_step, 1)
                r4, k4 = SH[:, 0:4, 1, :], SH[:, 4:8, :, :].rearrange("p t s e -> p t (s e)")
                for d in range(2):
                    dve.wait_ge(sig_ready, d + 1)
                    if d:
                        dve.wait_ge(s_done, 8)
                    link(v.tensor_scalar(KF[:, :, :], KF[:, :, :], -math.exp(-0.5), None, ALU.mult))
                    for t in range(4):
                        last = v.tensor_tensor_scan(LL[:, t, :], RESET[:, :, :].rearrange("p c e -> p (c e)"), KF[:, t, :], 0.0, ALU.mult, ALU.add)
                    link(last)
                    l8 = LL[:, :, :].rearrange("p t (c e) -> p (t c) e", e=CH)
                    f8 = KF[:, :, :].rearrange("p t (c e) -> p (t c) e", e=CH)
                    ar = AR[:, :, :, :, :].rearrange("p t c a e -> p (t c) a e")
                    tot = TOT[:, :, :].rearrange("p t c -> p (t c)")
                    link(v.tensor_copy(tot, l8[:, :, CH - 1]))
                    if d:
                        link(v.tensor_tensor(l8, f8, l8, ALU.subtract))
                        link(v.tensor_tensor(l8, l8, tot.unsqueeze(2).broadcast_to([P, 32, CH]), ALU.add))
                    v.tensor_tensor(ar[:, :, 0, :], l8, f8, ALU.subtract).then_inc(ll_ready, 1)
                    dve.wait_ge(ex_a, d + 1)
                    kk8 = KK[:, :, :].rearrange("p t (c e) -> p (t c) e", e=CH)
                    v.scalar_tensor_tensor(out=ar[:, :, 0, :], in0=ar[:, :, 0, :], scalar=-1.0, in1=kk8, op0=ALU.mult, op1=ALU.mult)
                    dve.wait_ge(ex_r, d + 1)
                    for t in range(4):
                        v.tensor_tensor(AR[:, t, 4:8, 1, :], AR[:, t, 4:8, 1, :], SH[:, t, 1, :].rearrange("p (c e) -> p c e", e=CH), ALU.mult)
                    for t in range(4):
                        last = v.tensor_scalar(KF[:, t, :], BF[:, t, :], -1.0, V("k_a", t), ALU.add, ALU.mult)
                    link(last)
                    link(v.scalar_tensor_tensor(out=KF[:, :, :], in0=KF[:, :, :], scalar=1.0, in1=k4, op0=ALU.add, op1=ALU.mult))
                    if d == 0:
                        v.tensor_copy(KS, KF[:, :, T:2 * T])
                        link(v.memset(STT[:, :, :], 0.0))
                    else:
                        v.tensor_tensor(KS, KS, KF[:, :, T:2 * T], ALU.add)
                        link(v.memset(STT[:, :, :], 0.0))
                    dve.sem_inc(st_ready, 1)
                    dve.wait_ge(ex_inv, d + 1)
                    v.tensor_tensor(KF[:, :, :], KF[:, :, :], LL[:, :, :], ALU.mult)
                    link(v.tensor_tensor(BF[:, :, :], BF[:, :, :], KK[:, :, :], ALU.mult))
                    v.tensor_tensor(BF[:, :, :], BF[:, :, :], LL[:, :, :], ALU.mult).then_inc(feat_ready, 1)
                    mask = C("mask_f" if d == 0 else "mask_b")
                    level = C("level_f" if d == 0 else "level_b").rearrange("p (n e) -> p n e", n=6)
                    eye = C("eye2")

                    def over(a):
                        return a.unsqueeze(1).broadcast_to([P, 4, CH])

                    chunks = list(range(8)) if d == 0 else [3, 2, 1, 0, 7, 6, 5, 4]
                    for i, c in enumerate(chunks):
                        B = d * 8 + i
                        dve.wait_ge(m_done, B + 1)
                        if B:
                            dve.wait_ge(s_done, B)
                        link(v.tensor_tensor(MT[:, :, :, :].rearrange("p a b c -> p a (b c)"),
                                             ps[:, 0:2, :].rearrange("p a (b c) -> p (a b) c", b=2),
                                             mask.unsqueeze(1).broadcast_to([P, 4, 256]), ALU.mult))
                        dve.sem_inc(mt_ready, 1)

                        def edge(n):
                            v.tensor_tensor(EB[:, n % 2, :, :], MT[:, :, 0, :], over(level[:, n, :]), ALU.mult).then_inc(e_ready, 1)

                        edge(0)
                        dve.wait_ge(e_ready, 6 * B + 1)
                        link(v.tensor_tensor(XZ[:, 1, :, :], EB[:, 0, :, :], over(eye), ALU.add))
                        edge(1)
                        dve.wait_ge(d_done, 6 * B + 1)
                        v.tensor_tensor(XZ[:, 0, :, :], ps[:, 4, 0:256].rearrange("p (a b) -> p a b", a=4), over(eye), ALU.add).then_inc(xz_ready, 1)
                        for n in range(1, 6):
                            if n < 5:
                                edge(n + 1)
                            dve.wait_ge(d_done, 6 * B + n + 1)
                            dve.wait_ge(xz_ready, 6 * B + n)
                            v.tensor_tensor(XZ[:, :, :, :].rearrange("p s a b -> p (s a b)"), XZ[:, :, :, :].rearrange("p s a b -> p (s a b)"), ps[:, 5, :], ALU.add).then_inc(xz_ready, 1)
                        dve.wait_ge(s_done, B + 1)
                        if i >= 4:
                            dst = YO_at(c)
                            y = ps[:, 6, 0:256].rearrange("p (a b) -> p a b", a=4)
                            if d == 0:
                                v.tensor_copy(dst, y)
                            else:
                                v.tensor_tensor(dst, dst, y, ALU.add)
                        link(v.tensor_tensor(STT[:, :, :], STT[:, :, :], ps[:, 7, 0:256].rearrange("p (a b) -> p a b", a=4), ALU.add))
                        link(v.tensor_tensor(STT[:, :, :], STT[:, :, :], PC[:, :, c].unsqueeze(2).broadcast_to([P, 4, CH]), ALU.mult))
                        if B == 15:
                            v.tensor_copy(YO[:, :, :], Y)
                            link(v.tensor_copy(STT[:, 0, 0:1], STT[:, 0, 0:1]))
                        dve.sem_inc(st_ready, 1)
                if stop == 96:
                    return
                dve.wait_ge(st_ready, 18)
                link(v.tensor_tensor(YB[:, :, :], r4, KS, ALU.mult))
                for t in range(4):
                    last = v.tensor_scalar(YB[:, t, :], YB[:, t, :], V("r_k", t), None, ALU.mult)
                last.then_inc(dve_step, 1)
                dve.wait_ge(pe_step, PE_STEP["y_mean"])
                y2 = YO[:, :, :].rearrange("p (b a) t -> p b (a t)", b=2)
                link(v.tensor_tensor(y2, y2, ps[:, 0:2, :], ALU.subtract))
                dve.sem_inc(dve_step, 1)
                dve.wait_ge(act_step, ACT_STEP["y_std"])
                link(v.reciprocal(YQ[:, :, :], YQ[:, :, :]))
                link(v.tensor_tensor(YO[:, :, :], YO[:, :, :], YQ[:, :, :], ALU.mult))
                for t in range(4):
                    last = v.tensor_scalar(YO[:, t, :], YO[:, t, :], V("ln_x_w", t), V("ln_x_b", t), ALU.mult, ALU.add)
                link(last)
                dve.wait_ge(pe_step, PE_STEP["rb_sum"])
                link(v.tensor_tensor(YB[:, :, :], SH[:, 8:12, 1, :], ps[:, 4:6, :].rearrange("p b (a t) -> p (b a) t", a=2), ALU.mult))
                link(v.tensor_tensor(YO[:, :, :], YO[:, :, :], YB[:, :, :], ALU.add))
                dve.wait_ge(pe_step, PE_STEP["gl_done"])
                v.tensor_tensor(y2, y2, ps[:, 6:8, :], ALU.mult).then_inc(dve_step, 1)
                dve.wait_ge(block_used, OUT0)
                g2 = G[:, :, :].rearrange("p (b a) t -> p b (a t)", a=2)
                v.tensor_tensor(MG[:, :, :].rearrange("p (b a) t -> p b (a t)", a=2), g2[:, 0:4, :], ps[:, 0:4, :], ALU.mult)
                link(v.tensor_tensor(MH[:, :, :].rearrange("p (b a) t -> p b (a t)", a=2), g2[:, 4:8, :], ps[:, 4:8, :], ALU.mult))
                v.tensor_tensor(MG[:, :, :], MG[:, :, :], MH[:, :, :], ALU.add).then_inc(dve_step, 1)
                dve.wait_ge(act_step, ACT_STEP["mix_std"])
                link(v.reciprocal(RS[:, 0, :], RS[:, 0, :]))
                link(v.tensor_tensor(MG[:, :, :], acc8, RS[:, 0, :].unsqueeze(1).broadcast_to([P, KD, T]), ALU.mult))
                for k in range(KD):
                    last = v.scalar_tensor_tensor(out=X[:, k, :], in0=MG[:, k, :], scalar=GP[:, k:k + 1], in1=X[:, k, :], op0=ALU.mult, op1=ALU.add)
                last.then_inc(dve_step, 1)
                dve.wait_ge(act_step, ACT_STEP["f_std"])
                link(v.reciprocal(RS[:, 1, :], RS[:, 1, :]))
                link(v.tensor_tensor(MG[:, :, :], X[:, :, :], RS[:, 1, :].unsqueeze(1).broadcast_to([P, KD, T]), ALU.mult))
                for k in range(KD):
                    last = v.tensor_scalar(MG[:, k, :], MG[:, k, :], GF[:, k:k + 1], ADA[:, 24 + k, 1:2], ALU.mult, ALU.add)
                last.then_inc(dve_step, 1)

            def YO_at(c):
                return SH[:, 0:4, 0, (c % 4) * CH:(c % 4 + 1) * CH]


            def moe():
                link(v.tensor_copy(GB[:, :, :], GQ.unsqueeze(2).broadcast_to([P, KD, P])))
                dve.sem_inc(dve_step, 1)
                dve.wait_ge(tri_ready, 1)
                dve.wait_ge(pe_step, PE_STEP["lg_done"])
                link(v.tensor_tensor(LG[:, :, :], ps[:, 0, 0:64].rearrange("p (n e) -> p n e", n=2),
                                     V("b_router", 0, EXPERTS).unsqueeze(1).broadcast_to([P, 2, EXPERTS]), ALU.add))
                for n in range(2):
                    other = LG[:, n, :].unsqueeze(1).broadcast_to([P, EXPERTS, EXPERTS])
                    own = LG[:, n, :].unsqueeze(2).broadcast_to([P, EXPERTS, EXPERTS])
                    link(v.tensor_tensor(CM[:, :, :], other, own, ALU.is_gt))
                    link(v.tensor_tensor(CN[:, :, :], other, own, ALU.is_equal))
                    link(v.tensor_tensor(CN[:, :, :], CN[:, :, :], TR[:, :, :], ALU.mult))
                    link(v.tensor_tensor(CM[:, :, :], CM[:, :, :], CN[:, :, :], ALU.add))
                    link(v.tensor_reduce(RK[:, n, :], CM[:, :, :], AX.X, ALU.add))
                v.tensor_scalar(MK[:, :, :], RK[:, :, :], 3.5, None, ALU.is_lt).then_inc(dve_step, 1)
                link(v.tensor_reduce(R2[:, 0:2], LG[:, :, :], AX.X, ALU.max))
                v.tensor_tensor(EX[:, :, :], LG[:, :, :], R2[:, 0:2].unsqueeze(2).broadcast_to([P, 2, EXPERTS]), ALU.subtract).then_inc(dve_step, 1)
                dve.wait_ge(act_step, ACT_STEP["lg_exp"])
                dve.wait_ge(dve_step, DVE_STEP["mask_ready"])
                link(v.tensor_tensor(EX[:, :, :], EX[:, :, :], MK[:, :, :], ALU.mult))
                link(v.tensor_reduce(R2[:, 2:4], EX[:, :, :], AX.X, ALU.add))
                link(v.reciprocal(R2[:, 4:6], R2[:, 2:4]))
                v.memset(GT[:, :, 0:1], 0.0)
                for r in range(2):
                    last = v.tensor_tensor(GT[:, :, 1 + r * EXPERTS:1 + (r + 1) * EXPERTS], EX[:, :, :], R2[:, 4:6].unsqueeze(2).broadcast_to([P, 2, EXPERTS]), ALU.mult)
                link(last)
                dve.wait_ge(pe_step, PE_STEP["pos_done"])
                link(v.scalar_tensor_tensor(out=RK[:, :, :], in0=ps[:, 3, 0:64].rearrange("p (n e) -> p n e", n=2), scalar=1.0, in1=MK[:, :, :], op0=ALU.add, op1=ALU.mult))
                v.tensor_scalar(SLOT[:, :, 0:EXPERTS], RK[:, :, :], -1.0, None, ALU.add)
                v.tensor_scalar(SLOT[:, :, EXPERTS:2 * EXPERTS], RK[:, :, :], -1.0 - CAP, None, ALU.add)
                link(v.memset(SLOT[:, :, 2 * EXPERTS:], -1.0))
                link(v.tensor_reduce(SS[:, 2:3], ps[:, 3, 64:64 + EXPERTS], AX.X, ALU.max))
                link(v.tensor_scalar(SS[:, 3:4], SS[:, 2:3], CAP + 0.5, None, ALU.is_gt))
                v.tensor_copy(FLAG, SS[:, 3:4]).then_inc(dve_step, 1)
                v.memset(YT[:, :, :], 0.0)
                v.memset(YBE[:, :], 0.0)
                link(v.memset(PTE[:, :, :], 0.0))
                dve.wait_ge(bias_in, 16)
                link(v.tensor_copy(T3[0:96, :], BR[0:96, :]))
                v.tensor_copy(B3[0:32, :], T3[0:32, :])
                link(v.tensor_tensor(BR[0:96, :], BR[0:96, :], T3[0:96, :], ALU.subtract))
                link(v.tensor_copy(T3[0:96, :], BR[0:96, :]))
                v.tensor_copy(B3[32:64, :], T3[32:64, :])
                link(v.tensor_tensor(BR[0:96, :], BR[0:96, :], T3[0:96, :], ALU.subtract))
                link(v.tensor_copy(B3[64:96, :], BR[64:96, :]))
                dve.sem_inc(dve_step, 1)
                pick = C("pick")

                def onehot(E):
                    for n in range(2):
                        last = v.tensor_scalar(ON[:, n, :], C("iota"), SLOT[:, n, bass.ds(E, 1)], None, ALU.is_equal)
                    last.then_inc(onehot_ready, 1)

                def select(dst, E, done):
                    v.tensor_copy(dst[0:96, :], pick[0:96, bass.ds(E, 1)].broadcast_to([96, P])).then_inc(done, 1)

                def add_expert(E):
                    for n in range(2):
                        dve.wait_ge(comb_done, E * 2 + (n + 1))
                        y = YT[:, n, :]
                        b = (6, 2)[n]
                        v.scalar_tensor_tensor(out=y, in0=ps[:, b:b + 2, :].rearrange("p b n -> p (b n)"), scalar=GT[:, n, bass.ds(E, 1)], in1=y,
                                               op0=ALU.mult, op1=ALU.add).then_inc(comb_read, 1)

                dve.sem_inc(comb_read, 1)
                dve.sem_inc(glu_done, 1)
                onehot(0)
                select(SELG, 0, selg_ready)

                def expert(E, used):
                    dve.wait_ge(block_used, used)
                    select(SELD, E, seld_ready)
                    for c in range(4):
                        dve.wait_ge(block_used, used + (2 * c + 2))
                        pair = ps[:, c % 2, :].rearrange("p (n a) -> p n a", a=2)
                        dve.wait_ge(glu_done, E * 4 + (c + 1))
                        v.tensor_scalar(TU[:, :], pair[:, :, 1], 7.0, -7.0, ALU.min, ALU.max)
                        v.tensor_scalar(TG[:, :], pair[:, :, 0], 7.0, None, ALU.min).then_inc(clipped, 1)
                        dve.wait_ge(sigm_ready, E * 4 + (c + 1))
                        v.tensor_tensor(TG[:, :], TG[:, :], SGM[:, :], ALU.mult).then_inc(glu_half, 1)
                        dve.wait_ge(glu_half, E * 4 + (c + 1))
                        v.scalar_tensor_tensor(out=AC[:, c * 256:(c + 1) * 256], in0=TU[:, :], scalar=1.0, in1=TG[:, :], op0=ALU.add, op1=ALU.mult).then_inc(glu_done, 1)
                        if c == 0:
                            add_expert(E)
                        if c == 1:
                            dve.wait_ge(pt_turned, E + 1)
                            onehot(E + 1)
                    select(SELG, E + 1, selg_ready)

                with dve.Fori(0, EXPERTS) as E:
                    expert(E, E * EXPERT_BLOCKS + MOE0)
                more = dve.value_load(FLAG[0:1, 0:1], min_val=0, max_val=1)
                with dve.If(more > 0):
                    with dve.Fori(EXPERTS, 2 * EXPERTS) as E:
                        expert(E, E * EXPERT_BLOCKS + MOE0)
                    add_expert(2 * EXPERTS)
                with dve.Else():
                    add_expert(EXPERTS)
                dve.wait_ge(comb_read, EXPERTS * 2 + 3)
                for n in range(2):
                    v.tensor_tensor_reduce(out=HT[:, n, :], in0=YT[:, n, :], in1=YT[:, n, :], scale=1.0, scalar=0.0, op0=ALU.mult, op1=ALU.add, accum_out=SS[:, n:n + 1]).then_inc(y_sum, 1)
                dve.wait_ge(y_sum, 2)
                dve.sem_inc(dve_step, 1)
                dve.wait_ge(act_step, ACT_STEP["y_root"])
                link(v.reciprocal(SS[:, 2:4], SS[:, 0:2]))
                for n in range(2):
                    last = v.scalar_tensor_tensor(out=YT[:, n, :], in0=YT[:, n, :], scalar=SS[:, 2 + n:3 + n], in1=GR[:, :], op0=ALU.mult, op1=ALU.mult)
                link(last)
                v.tensor_tensor(YT[:, :, :], YT[:, :, :], XT[:, :, :], ALU.add).then_inc(dve_step, 1)

            v.memset(EPS2[:, 0:1], LN_EPS)
            v.memset(EPS2[:, 1:2], RMS_EPS)
            v.memset(EPS2[:, 2:3], GN_EPS)
            v.memset(YP[:, :, 0:TAPS - 1], 0.0)
            v.memset(XB[:, :, 0:LTAPS - 1], 0.0)
            v.memset(RV[0:HEADS, :], NEG)
            link(v.memset(ZERO[:, :], 0.0))
            dve.sem_inc(zero_ready, 1)
            dve.wait_ge(lam_exp, 1)
            link(v.tensor_scalar(LT[:, 2, :], LT[:, 1, :], 2.0, None, ALU.add))
            link(v.reciprocal(LT[:, 2, :], LT[:, 2, :]))
            link(v.tensor_tensor(LT[:, 2, :], LT[:, 2, :], LT[:, 1, :], ALU.mult))
            link(v.tensor_tensor(LT[:, 3, :], LT[:, 2, :], LT[:, 2, :], ALU.mult))
            link(v.memset(LT[:, 4, :], 1.0 / 17))
            for n in range(15, 0, -2):
                link(v.tensor_tensor(LT[:, 4, :], LT[:, 4, :], LT[:, 3, :], ALU.mult))
                link(v.tensor_scalar(LT[:, 4, :], LT[:, 4, :], 1.0 / n, None, ALU.add))
            link(v.tensor_tensor(LT[:, 4, :], LT[:, 4, :], LT[:, 2, :], ALU.mult))
            link(v.tensor_scalar(LT[:, 5, :], V("lam", 0, 2 * LAYERS), -1.0, 0.0, ALU.mult, ALU.max))
            link(v.scalar_tensor_tensor(out=LT[:, 5, :], in0=LT[:, 4, :], scalar=2.0, in1=LT[:, 5, :], op0=ALU.mult, op1=ALU.add))
            link(v.tensor_scalar(LC[:, :], LT[:, 5, :], -8.0, None, ALU.mult))
            link(v.tensor_scalar(LN_[:, :], LT[:, 5, :], 8.0, None, ALU.mult))
            dve.wait_ge(rel_ready, 1)
            v.tensor_copy(RV[0:HEADS, P:2 * P], ps[0:HEADS, 7, 0:P]).then_inc(rv_ready, 1)
            for l in range(LAYERS):
                ffn(2 * l, LB[l])
                ln(3 * l, 0.5, LB[l] + FFN_BLOCKS)
                if stop == 1:
                    return
                mixer(l)
                ln(3 * l + 1, 1.0, LB[l] + FFN_BLOCKS + IN_BLOCKS + OUT_BLOCKS)
                if stop == 2:
                    return
                ffn(2 * l + 1, LB[l] + FFN_BLOCKS + IN_BLOCKS + OUT_BLOCKS)
                ln(3 * l + 2, 0.5, LB[l + 1] if l + 1 < LAYERS else ADA0)
            if stop > 3:
                second()
            if stop > 98:
                moe()


def _lay_out(inputs):
    f = {k: np.asarray(v) for k, v in inputs.items()}

    def cols(a):
        a = np.ascontiguousarray(a).reshape(-1, P)
        return a.T

    def rows(a):
        a = np.asarray(a).reshape(1, -1)
        return np.broadcast_to(a, (P, a.shape[1]))

    def top(a):
        z = np.zeros((P,) + a.shape[1:], a.dtype)
        z[:a.shape[0]] = a
        return z

    def by_k(w):
        k = w.shape[0] // P
        return w.reshape(k, P, w.shape[1]).transpose(1, 0, 2).reshape(P, -1)

    vec = np.zeros((P, NVEC), np.float32)

    def put(name, a):
        at, n = VEC[name]
        vec[:, at:at + n] = a

    put("ln_g", cols(f["ln_g"]))
    put("ln_b", cols(f["ln_b"]))
    for l in range(LAYERS):
        put(f"dw_w{l}", f["conv_dw_w"][l].reshape(TAPS, 2, P).transpose(2, 1, 0).reshape(P, -1))
        put(f"dw_b{l}", cols(f["conv_dw_b"][l]))
        put(f"cln_g{l}", cols(f["conv_ln_g"][l]))
        put(f"cln_b{l}", cols(f["conv_ln_b"][l]))
        put(f"lw{l}", f["lru_conv_w"][l].reshape(LTAPS, 2, P).transpose(2, 1, 0).reshape(P, -1))
        put(f"lb{l}", cols(f["lru_conv_b"][l]))
        put(f"ba{l}", cols(f["lru_ba"][l]))
        put(f"bx{l}", cols(f["lru_bx"][l]))
        put(f"sink{l}", rows(f["attn_sinks"][l]))
        g = np.zeros((P, 4, P), np.float32)
        for which, w in ((0, f["lru_wa"][l]), (1, f["lru_wx"][l])):
            for t in range(2):
                for h in range(2):
                    g[h * 64:h * 64 + 64, 2 * which + t, h * 64:h * 64 + 64] = w[2 * t + h]
        put(f"gate_w{l}", g.reshape(P, -1))
    put("lam", cols(f["lru_lambda"]))
    put("rel_bias", top(f["rel_bias"]))

    heads = np.concatenate([np.r_[t * 64:t * 64 + 64, (4 + t) * 64:(4 + t) * 64 + 64] for t in range(4)])
    perm_in = np.r_[0:1024, 1024 + heads, 1536:1792]
    perm_out = np.r_[0:512, 512 + heads]

    W = np.zeros((BLOCKS, P, BLK), np.float32)
    at = 0

    def cols_block(w, c):
        return by_k(w[:, c * 256:(c + 1) * 256])

    for l in range(LAYERS):
        for i in range(2):
            g, u, d = f["ffn_w_gate"][l, i], f["ffn_w_up"][l, i], f["ffn_w_down"][l, i]
            for j in range(FCH):
                W[at], W[at + 1] = cols_block(g, j), cols_block(u, j)
                at += 2
                if j:
                    W[at] = by_k(d[(j - 1) * 256:j * 256])
                    at += 1
            W[at] = by_k(d[(FCH - 1) * 256:])
            at += 1
            if i == 0:
                w = f["w_in"][l][:, perm_in]
                for b in range(IN_BLOCKS):
                    W[at] = cols_block(w, b)
                    at += 1
                w = f["w_out"][l][perm_out]
                for b in range(OUT_BLOCKS):
                    W[at] = cols_block(w, b)
                    at += 1
    _second(f, W, at, put, cols, rows, top, by_k, cols_block, heads)
    con = constants()
    x_t = f["x"][0].T.reshape(KD, P, T).transpose(1, 0, 2)
    ctx_t = f["ctx_2"][0].T.reshape(KD, P, T).transpose(1, 0, 2)
    b = np.concatenate([f["b_gate_up_2"][0], f["b_down_2"][0]], 1)
    bias = np.concatenate([b, b, b], 0)
    return {"weights": W, "vectors": vec, "consts": con, "x_t": np.ascontiguousarray(x_t),
            "ctx_t": np.ascontiguousarray(ctx_t), "moe_bias": bias}


def _second(f, W, at, put, cols, rows, top, by_k, cols_block, heads):
    for name in ("g_pre_mix", "g_post_mix", "g_pre_ffn", "g_post_ffn", "k_k", "k_a", "r_k", "ln_x_w", "ln_x_b", "mu_prev", "mu_next", "b_ada"):
        put(name, cols(f[name + "_2"][0]))
    zero = np.zeros(P, np.float32)
    perm = np.r_[heads, 512:4736]
    put("b_in", cols(f["b_in_2"][0][perm]))
    put("sink2", rows(f["att_sinks_2"][0]))
    put("w0", np.concatenate([cols(f["w0_f_2"][0]), cols(f["w0_b_2"][0])], 1))
    put("a0", np.concatenate([cols(f["a0_f_2"][0]), cols(f["a0_b_2"][0])], 1))
    put("b_router", rows(f["b_router_2"][0]))
    put("c", np.stack([cols(f["c_ctx_2"]), cols(f["c_2"][0])], 2).reshape(P, 16))
    put("w2", np.concatenate([f["w2_f_2"][0], f["w2_b_2"][0]], 0))
    put("a2", np.concatenate([f["a2_f_2"][0], f["a2_b_2"][0]], 0))
    put("g2", f["g2_2"][0])
    put("w_router", by_k(f["w_router_2"][0]))
    assert at == ADA0
    for b in range(ADA_BLOCKS):
        W[ADA0 + b] = cols_block(f["w_ada_2"][0], b)
    w = f["w_in_2"][0][:, perm]
    w = np.concatenate([w, np.zeros((D, P), np.float32)], 1)
    for b in range(PROJ_BLOCKS):
        W[PROJ0 + b] = cols_block(w, b)
    for b in range(2):
        W[UP0 + b] = by_k(f["w_up_att_2"][0][heads][:, b * 512:(b + 1) * 512])
        W[UP0 + 2 + b] = by_k(f["w_up_rwkv_2"][0][:, b * 512:(b + 1) * 512])
    for b in range(OUT_BLOCKS):
        W[OUT0 + b] = cols_block(f["w_out_2"][0], b)
    for e in range(EXPERTS):
        at = MOE0 + e * EXPERT_BLOCKS
        for n in range(4):
            for k in range(2):
                W[at] = by_k(f["w_gate_up_2"][0, e][k * 512:(k + 1) * 512, n * 512:(n + 1) * 512])
                at += 1
        for n in range(2):
            for k in range(2):
                W[at] = by_k(f["w_down_2"][0, e][k * 512:(k + 1) * 512, n * 512:(n + 1) * 512])
                at += 1


def _program(nc, arrays, stop=99):
    args = {n: nc.dram_tensor(n, a.shape, mybir.dt.from_np(a.dtype), kind="ExternalInput").ap()
            for n, a in arrays.items()}
    out = nc.dram_tensor("out", (P, 2048), F32, kind="ExternalOutput").ap()
    bass_two_blocks(nc, args["weights"], args["vectors"], args["consts"], args["x_t"], args["ctx_t"],
                    args["moe_bias"], out, stop)


def kernel(**inputs):
    import concourse.bacc as _bacc
    from concourse.bass_utils import run_bass_kernel_spmd as _run

    arrays = _lay_out(inputs)
    nc = _bacc.Bacc("TRN2", target_bir_lowering=False, num_devices=1)
    _program(nc, arrays)
    r = _run(nc, [arrays], core_ids=[0])
    return r.results[0]["out"].reshape(P, 2, D).transpose(1, 0, 2).reshape(1, T, D)
```

```python
from contextlib import ExitStack
import math

import numpy as np
import concourse.bass as bass
from concourse import mybir

F32 = mybir.dt.float32
BF16 = mybir.dt.bfloat16
I32 = mybir.dt.int32
ALU = mybir.AluOpType
ACT = mybir.ActivationFunctionType
AX = mybir.AxisListType

P = 128
T = 256
D = 1024
KD = D // P
LAYERS = 2
F = 2816
FCH = F // 256
TAPS, LTAPS = 31, 4
HEADS = 8
BLK = 2048
RING = 6
ALPHA = (2.0 * LAYERS) ** 0.25
LN_EPS = 1e-5
RMS_EPS = 1e-6
GN_EPS = 64e-5
NEG = -1e30
EXPERTS = 32
CAP = 64
PASSES = T // CAP
EXTRA = 16
CH = 64
NSEQ = 2
ZT = 37
FFN_BLOCKS = 3 * FCH
IN_BLOCKS = 7
OUT_BLOCKS = 4
LAYER_BLOCKS = 2 * FFN_BLOCKS + IN_BLOCKS + OUT_BLOCKS
ADA_BLOCKS = 24
PROJ_BLOCKS = 19
UP_BLOCKS = 4
EXPERT_BLOCKS = 12
ADA0 = LAYERS * LAYER_BLOCKS
PROJ0 = ADA0 + ADA_BLOCKS
UP0 = PROJ0 + PROJ_BLOCKS
OUT0 = UP0 + UP_BLOCKS
MOE0 = OUT0 + OUT_BLOCKS
BLOCKS = MOE0 + EXPERTS * EXPERT_BLOCKS


def layout(entries):
    at, out = 0, {}
    for name, n in entries:
        out[name] = (at, n)
        at += n
    return out, at


VEC, NVEC = layout(
    [("ln_g", 48), ("ln_b", 48)]
    + [(f"{n}{l}", c) for l in range(LAYERS) for n, c in (
        ("dw_w", 2 * TAPS), ("dw_b", 2), ("cln_g", 2), ("cln_b", 2), ("lw", 2 * LTAPS), ("lb", 2),
        ("ba", 2), ("bx", 2), ("sink", HEADS), ("gate_w", 4 * P))]
    + [("lam", 2 * LAYERS), ("rel_bias", HEADS)]
    + [("b_in", ZT), ("mu_prev", 15), ("mu_next", 15), ("b_ada", 48), ("g_pre_mix", 8),
       ("g_post_mix", 8), ("g_pre_ffn", 8), ("g_post_ffn", 8), ("sink2", HEADS), ("w0", 8),
       ("a0", 8), ("k_k", 4), ("k_a", 4), ("r_k", 4), ("ln_x_w", 4), ("ln_x_b", 4),
       ("b_router", EXPERTS), ("c", 16), ("w2", 512), ("a2", 512), ("g2", 512),
       ("w_router", KD * EXPERTS)])
CON, NCON = layout([("ident", P), ("ones_d", P), ("ones_c", P), ("heads_mean", P),
                    ("heads_sum", P), ("before", P), ("ones", P), ("cos", T), ("sin", T),
                    ("rot", P), ("mask2", 2 * T), ("bucket", P), ("iota", P), ("mask_f", 256),
                    ("mask_b", 256), ("level_f", 6 * CH), ("level_b", 6 * CH), ("eye2", CH),
                    ("pick", EXPERTS)])


def steps(*names):
    return {name: n + 1 for n, name in enumerate(names)}


def constants():
    def bucket(d):
        if d < 16:
            return d
        v = np.float32(np.log(np.float32(d) / np.float32(16))) / np.float32(math.log(8.0)) * np.float32(16)
        return min(16 + int(v), 31)

    c = np.zeros((P, NCON), np.float32)

    def put(name, a):
        at, n = CON[name]
        c[:a.shape[0], at:at + n] = a.reshape(a.shape[0], n)

    i = np.arange(P)
    put("ident", np.eye(P))
    put("ones_d", np.full((P, P), 1.0 / D))
    put("ones_c", np.full((P, P), 1.0 / 256))
    same = (i[:, None] // 64) == (i[None, :] // 64)
    put("heads_mean", same / 64.0)
    put("heads_sum", same * 1.0)
    put("before", (i[:, None] < i[None, :]) * 1.0)
    put("ones", np.ones((P, P)))
    t = np.arange(T)
    pos = np.where((i[:, None] % 64) < 32, t[None, :] // 64, t[None, :] % 64).astype(np.float32)
    inv = np.float32(10000.0) ** (-(np.arange(0, 32, 2, dtype=np.float32)) / np.float32(32))
    ang = (pos * inv[i % 16][:, None]).astype(np.float32)
    put("cos", np.cos(ang))
    put("sin", np.sin(ang))
    rot = np.zeros((P, P))
    for m in range(P):
        if m % 32 < 16:
            rot[m + 16, m] = -1.0
        else:
            rot[m - 16, m] = 1.0
    put("rot", rot)
    q = np.arange(P)[:, None, None] + P * np.arange(2)[None, :, None]
    k = np.arange(T)[None, None, :]
    put("mask2", np.where(np.abs(k - q) <= 128, 0.0, NEG))
    onehot = np.zeros((32, P))
    for d in range(P):
        onehot[bucket(P - 1 - d), d] = 1.0
    put("bucket", onehot)
    slot = np.arange(P) % 64
    put("iota", np.broadcast_to(np.where(slot < CAP, slot, 1e9), (P, P)))
    s = (i % 64)[:, None]
    tt = np.arange(CH)[None, :]
    for name, lev, strict, incl in (("mask_f", "level_f", s < tt, s <= tt), ("mask_b", "level_b", s > tt, s >= tt)):
        both = np.concatenate([strict, incl], 1) * 1.0
        put(name, np.concatenate([both, both], 1))
        levels = []
        for n in range(6):
            size = 1 << n
            pair = (s // (2 * size)) == (tt // (2 * size))
            levels.append((strict & pair & ((s // size) != (tt // size))) * 1.0)
        put(lev, np.concatenate(levels, 1))
    put("eye2", (s == tt) * 1.0)
    e = np.arange(EXPERTS)
    put("pick", (((i % 32)[:, None] == e[None, :] % 32) & (i[:, None] < 96)) * 1.0)
    return c


def bass_two_blocks(nc, weights, vectors, consts, x_t, ctx_t, moe_bias, out, stop=99):
    ctx = ExitStack()
    with ctx:
        def sb(name, shape, dt=F32):
            return ctx.enter_context(nc.sbuf_tensor(name, shape, dt))

        def sem(name):
            return ctx.enter_context(nc.semaphore(name))

        ps = ctx.enter_context(nc.psum_tensor("ps", [P, 8, 512], F32))
        ring = sb("ring", [P, RING, BLK])
        vec = sb("vec", [P, NVEC])
        con = sb("con", [P, NCON])
        X = sb("X", [P, KD, T])
        EPS2 = sb("EPS2", [P, 4])
        arena = sb("arena", [P, 30868])
        rel_scratch = nc.dram_tensor("rel_scratch", [HEADS, P, 384], F32, kind="Internal").ap()

        def V(name, i=0, n=None):
            at, m = VEC[name]
            return vec[:, at + i:at + i + (1 if n is None else n)]

        def C(name):
            at, m = CON[name]
            return con[:, at:at + m]

        ident = C("ident")

        def area(start, *shape):
            n = int(np.prod(shape))
            a = arena[:, start:start + n]
            if len(shape) == 1:
                return a, start + n
            names = "abcd"[:len(shape)]
            return a.rearrange("p (" + " ".join(names) + ") -> p " + " ".join(names),
                               **{k: s for k, s in zip(names[1:], shape[1:])}), start + n

        o = 0
        XS, o = area(o, KD, T)
        ST, o = area(o, 4, 512)
        SG, o = area(o, 2, 2, T)
        HF, o = area(o, 2, 2, T)
        U, o = area(o, 14, T)
        YP, o = area(o, 2, TAPS - 1 + T)
        XB, o = area(o, 2, LTAPS - 1 + T)
        CV, o = area(o, 2, T)
        CQ, o = area(o, 2, T)
        SC, o = area(o, HEADS, 3, P)
        BT, o = area(o, HEADS, 3, P)
        PT, o = area(o, HEADS, 3, P)
        VT, o = area(o, 2, P)
        YC, o = area(o, KD, T)
        XC, o = area(o, 2, T)
        LR, o = area(o, 8, 2, T)
        M3, o = area(o, HEADS, 3)
        MM, o = area(o, HEADS, 3)
        S3, o = area(o, HEADS, 3)
        ES, o = area(o, HEADS, 2)
        DN, o = area(o, HEADS, 2)
        LC, o = area(o, 2 * LAYERS)
        LN_, o = area(o, 2 * LAYERS)
        LT, o = area(o, 6, 2 * LAYERS)
        RV, o = area(o, 384)
        ZERO, o = area(o, 640)
        first_end = o
        zero16 = ZERO[:, :].bitcast(BF16)
        zl, zr = zero16[:, 0:P], zero16[:, P:P + 512]

        H, _ = area(0, KD, NSEQ, T)
        HSQ, _ = area(4096, KD, NSEQ, T)
        SH, _ = area(0, 15, NSEQ, T)
        ZR, _ = area(8192, 15, NSEQ, T + 2)
        G, _ = area(15932, 16, T)
        o = 20028
        QA, o = area(o, 4, T)
        KA, o = area(o, NSEQ, T)
        VA, o = area(o, NSEQ, T)
        QR, o = area(o, 4, T)
        KR, o = area(o, NSEQ, T)
        VK, o = area(o, 4, P)
        assert o <= 24124
        SM, o = area(24124, 600)
        ADA = SM[:, 0:96].rearrange("p (c s) -> p c s", s=2)
        SILC = SM[:, 96:112].rearrange("p (k s) -> p k s", s=2)
        GS = SM[:, 112:128].rearrange("p (k s) -> p k s", s=2)
        GF = SM[:, 128:136]
        GP = SM[:, 136:144]
        GQ = SM[:, 144:152]
        PC = SM[:, 152:184].rearrange("p (t c) -> p t c", t=4)
        TOT = SM[:, 184:216].rearrange("p (t c) -> p t c", t=4)
        M4 = SM[:, 216:248].rearrange("p (h a) -> p h a", a=4)
        MX = SM[:, 248:256]
        ES2 = SM[:, 256:264]
        DN2 = SM[:, 264:272]
        TN = SM[:, 272:273]
        AT, o = area(o, 4, T)
        RS, o = area(o, NSEQ, T)
        S2, _ = area(8192, HEADS, 4, P)
        P2, o = area(o, HEADS, 4, P)
        KK, _ = area(8192, 4, 8 * CH)
        BF, _ = area(10240, 4, 8 * CH)
        LL, _ = area(12288, 4, 8 * CH)
        MT0, _ = area(14336, 4, 4, CH)
        BK0, _ = area(15360, 2, 4, CH)
        MT1, _ = area(12288, 4, 4, CH)
        BK1, _ = area(13312, 2, 4, CH)
        XZ1, _ = area(13824, 2, 4, CH)
        AR, _ = area(20028, 4, 8, 2, CH)
        KF, _ = area(26260, 4, 8 * CH)
        VM, _ = area(28308, 8, 4, CH)
        XZ0, _ = area(30356, 2, 4, CH)
        WW0, _ = area(7680, 4, CH)
        WW1 = V("gate_w1", 0, 4 * CH).rearrange("p (a b) -> p a b", a=4)
        EB1 = V("gate_w0", 0, 8 * CH).rearrange("p (s a b) -> p s a b", s=2, a=4)
        U0, _ = area(7936, 4, CH)
        UU, _ = area(25748, 4, CH)
        STT, _ = area(26004, 4, CH)
        Y = SH[:, 0:4, 0, :]
        KS = SH[:, 8:12, 0, :]
        MG, _ = area(0, KD, T)
        MH, _ = area(2048, KD, T)
        EB0 = sb("EB", [P, 2, 4, CH])
        MTS, BKS, XZS, WWS, EBS = (MT0, MT1), (BK0, BK1), (XZ0, XZ1), (WW0, WW1), (EB0, EB1)
        RESET = sb("RESET", [P, 8, CH], BF16)
        YO, _ = area(20028, 4, T)
        YQ, _ = area(21052, 4, T)
        YB, _ = area(22076, 4, T)

        HT, _ = area(2048, 2, D)
        small, _ = area(4096, 256)
        LG = small[:, 0:64].rearrange("p (n e) -> p n e", n=2)
        MK = small[:, 64:128].rearrange("p (n e) -> p n e", n=2)
        EX = small[:, 128:192].rearrange("p (n e) -> p n e", n=2)
        RK = small[:, 192:256].rearrange("p (n e) -> p n e", n=2)
        TR, _ = area(4352, EXPERTS, EXPERTS)
        CM, _ = area(5376, EXPERTS, EXPERTS)
        CN, _ = area(6400, EXPERTS, EXPERTS)
        small2, _ = area(7424, 768)
        turns = EXPERTS + EXTRA + 1
        SLOT = small2[:, 0:2 * turns].rearrange("p (n e) -> p n e", n=2)
        GT = small2[:, 2 * turns:4 * turns].rearrange("p (n e) -> p n e", n=2)
        R2 = small2[:, 4 * turns:4 * turns + 6]
        SS = small2[:, 4 * turns + 6:4 * turns + 10]
        FLAG = small2[:, 4 * turns + 10:4 * turns + 11].bitcast(I32)
        WHO = small2[:, 4 * turns + 12:4 * turns + 12 + EXTRA].bitcast(I32)
        PICK = small2[:, 4 * turns + 40:5 * turns + 40]
        small3, _ = area(24724, 1024)
        PART = small3[:, 0:192].rearrange("p (n a) -> p n a", n=2)
        OVER = small3[:, 192:288].rearrange("p (a e) -> p a e", e=EXPERTS)
        TURN = small3[:, 288:384].rearrange("p (a e) -> p a e", e=EXPERTS)
        MORE = small3[:, 384:416]
        UPTO = small3[:, 416:448]
        GATE3 = small3[:, 448:640].rearrange("p (n a) -> p n a", n=2)
        PICK3 = small3[:, 640:736]
        WHO3 = small3[:, 736:832]
        WHOF = small3[:, 832:848]
        SELJ, _ = area(17408, EXTRA, 96)
        PROD, _ = area(18944, EXTRA, 96)
        YT, _ = area(8192, 2, D)
        ON, _ = area(10240, 2, P)
        PTE, _ = area(10496, 2, P)
        XE, _ = area(11264, KD, P)
        AC, _ = area(13312, 2, 256)
        TG, _ = area(14336, 256)
        TU, _ = area(14592, 256)
        SGM, _ = area(14848, 256)
        AT_, _ = area(15360, 4, P)
        YBE, _ = area(16384, 512)
        BR, _ = area(17408, 3 * D)
        B3a, _ = area(20480, 3 * D // 2)
        B3 = B3a[:, :].bitcast(BF16)
        T3a, _ = area(22016, 3 * D // 2)
        T3 = T3a[:, :].bitcast(BF16)
        SEa, _ = area(23552, P)
        SELG, SELD = SEa[:, 0:32].bitcast(BF16), SEa[:, 64:96].bitcast(BF16)
        XT, _ = area(26260, 2, D)
        GR, _ = area(28308, D)
        GB, _ = area(29332, KD, P)

        slot_loaded = [sem(f"slot_loaded{i}") for i in range(RING)]
        block_used = sem("block_used")
        vec_loaded, con_loaded, x_loaded = sem("vec_loaded"), sem("con_loaded"), sem("x_loaded")
        zero_ready = sem("zero_ready")
        silu_ready, hidden_ready = sem("silu_ready"), sem("hidden_ready")
        sum_ready, mean_ready, centred, squared = (sem(n) for n in ("sum_ready", "mean_ready", "centred", "squared"))
        var_ready, std_ready, x_ready = sem("var_ready"), sem("std_ready"), sem("x_ready")
        u_copied = sem("u_copied")
        vt_ready, vt_copied = sem("vt_ready"), sem("vt_copied")
        score_ready, score_read = sem("score_ready"), sem("score_read")
        score_shifted, exp_ready, prob_ready = sem("score_shifted"), sem("exp_ready"), sem("prob_ready")
        pt_ready, pt_copied = sem("pt_ready"), sem("pt_copied")
        attn_ready, attn_copied = sem("attn_ready"), sem("attn_copied")
        lru_in, lru_gates, lru_acts, lru_m2 = sem("lru_in"), sem("lru_gates"), sem("lru_acts"), sem("lru_m2")
        lru_mult, lru_done = sem("lru_mult"), sem("lru_done")
        conv_ready, cmean_ready, cc_ready, csq_ready = (sem(n) for n in ("conv_ready", "cmean_ready", "cc_ready", "csq_ready"))
        cvar_ready, cstd_ready, cnorm_ready, conv_done = (sem(n) for n in ("cvar_ready", "cstd_ready", "cnorm_ready", "conv_done"))
        lam_abs = sem("lam_abs")
        tile_done = sem("tile_done")
        glu_half, y_sum, y_all = sem("glu_half"), sem("y_sum"), sem("y_all")
        extra_ready = sem("extra_ready")
        lam_exp, rel_ready, rv_ready, rv_stored, bias_loaded = (sem(n) for n in ("lam_exp", "rel_ready", "rv_ready", "rv_stored", "bias_loaded"))
        dve_chain, act_chain = sem("dve_chain"), sem("act_chain")
        ctx_loaded = sem("ctx_loaded")
        z_copied = sem("z_copied")
        s2_done, s2_read, s2_shifted, s2_exp, s2_prob = (sem(n) for n in ("s2_done", "s2_read", "s2_shifted", "s2_exp", "s2_prob"))
        p2_done, p2_copied, at_done, at_copied = (sem(n) for n in ("p2_done", "p2_copied", "at_done", "at_copied"))
        lora_done, sig_ready, ll_ready, ex_a, ex_r = sem("lora_done"), sem("sig_ready"), sem("ll_ready"), sem("ex_a"), sem("ex_r")
        ex_inv, feat_ready = sem("ex_inv"), sem("feat_ready")
        m_done, mt_ready, bk_done, bk_ready = (sem(n) for n in ("m_done", "mt_ready", "bk_done", "bk_ready"))
        e_ready, w_done, w_ready, d_done, xz_ready = (sem(n) for n in ("e_ready", "w_done", "w_ready", "d_done", "xz_ready"))
        u0_done, u0_ready, uu_done, uu_ready = (sem(n) for n in ("u0_done", "u0_ready", "uu_done", "uu_ready"))
        s_done, st_ready = sem("s_done"), sem("st_ready")
        tri_one, tri_ready, bias_in = sem("tri_one"), sem("tri_ready"), sem("bias_in")
        tok_done, tok_copied = sem("tok_done"), sem("tok_copied")
        flag_ready = sem("flag_ready")
        onehot_ready, gather_done, xe_ready = sem("onehot_ready"), sem("gather_done"), sem("xe_ready")
        selg_ready, seld_ready, clipped, sigm_ready, glu_done = (sem(n) for n in ("selg_ready", "seld_ready", "clipped", "sigm_ready", "glu_done"))
        comb_done, comb_read, pt_turned, pte_ready = (sem(n) for n in ("comb_done", "comb_read", "pt_turned", "pte_ready"))
        act_turned, actt_ready, yb_ready = sem("act_turned"), sem("actt_ready"), sem("yb_ready")
        out_stored = sem("out_stored")

        pe_step = sem("pe_step")
        PE_STEP = steps("h_ms", "rot_done", "vk_done", "kk_sum", "vm_done", "y_mean", "rb_sum", "gl_done",
             "y_var", "mix_ms", "f_ms", "lg_done", "pos_done")
        act_step = sem("act_step")
        ACT_STEP = steps("silc_ready", "h_sq", "h_std", "vk_copied", "kk_sq", "tanh_ready", "kk_std",
             "vm_copied", "gl_ready", "y_sq", "y_std", "mix_copied", "mix_std", "f_sq", "f_std",
             "lg_exp", "y_root")
        dve_step = sem("dve_step")
        DVE_STEP = steps("pads_ready", "h_ready", "rot_read", "kk_raw", "kk_used", "rb_ready", "y_centred",
             "rw_ready", "mg_ready", "xm_ready", "f_ready", "gb_ready", "mask_ready", "lg_shift",
             "moe_ready", "y_ss", "y_final")

        block = ctx.enter_context(nc.Block())
        LB = [l * LAYER_BLOCKS for l in range(LAYERS)]

        @block.sync
        def _(sp):
            sp.dma_start(X[:, :, :], x_t).then_inc(x_loaded, 16)
            sp.dma_start(vec[:, :], vectors).then_inc(vec_loaded, 16)
            sp.dma_start(con[:, :], consts).then_inc(con_loaded, 16)
            for s in range(RING):
                sp.dma_start(ring[:, s, :], weights[s, :, :]).then_inc(slot_loaded[s], 16)
            nblk = BLOCKS if stop > 98 else {1: FFN_BLOCKS, 2: FFN_BLOCKS + 11, 3: 154, 4: 154+24}.get(stop, MOE0)
            rounds = nblk // RING
            with sp.Fori(1, rounds) as r:
                for s in range(RING):
                    sp.wait_ge(block_used, r * RING + (s - RING + 1))
                    sp.dma_start(ring[:, s, :], weights[r * RING + s, :, :]).then_inc(slot_loaded[s], 16)
            for b in range(rounds * RING, nblk):
                sp.wait_ge(block_used, b - RING + 1)
                sp.dma_start(ring[:, b % RING, :], weights[b, :, :]).then_inc(slot_loaded[b % RING], 16)
            if stop > 98:
                sp.wait_ge(extra_ready, 1)
                extra = sp.value_load(FLAG[0:1, 0:1], min_val=0, max_val=EXTRA - 1)
                with sp.If(extra > 0):
                    with sp.Fori(0, extra) as t:
                        who = sp.value_load(WHO[0:1, bass.ds(t, 1)], min_val=0, max_val=EXPERTS - 1)
                        for j in range(EXPERT_BLOCKS):
                            b = BLOCKS + j
                            sp.wait_ge(block_used, t * EXPERT_BLOCKS + (b - RING + 1))
                            sp.dma_start(ring[:, b % RING, :], weights[who * EXPERT_BLOCKS + (MOE0 + j), :, :]).then_inc(slot_loaded[b % RING], 16)
            sp.wait_ge(out_stored, 16)

        @block.gpsimd
        def _(pool):
            pool.wait_ge(rv_ready, 1)
            pool.dma_start(rel_scratch, RV[0:HEADS, :].unsqueeze(1).broadcast_to([HEADS, P, 384])).then_inc(rv_stored, 16)
            pool.wait_ge(rv_stored, 16)
            for h in range(HEADS):
                band = bass.AP(rel_scratch.tensor, h * P * 384 + 127, [[383, P], [1, 256]])
                own = bass.AP(rel_scratch.tensor, h * P * 384 + 127 + P, [[383, P], [1, P]])
                pool.dma_start(BT[:, h, 0, :], own).then_inc(bias_loaded, 16)
                pool.dma_start(BT[:, h, 1:3, :].rearrange("p a b -> p (a b)"), band).then_inc(bias_loaded, 16)
            if stop > 3:
                pool.wait_ge(x_ready, 6)
                pool.dma_start(H[:, :, 0, :], ctx_t).then_inc(ctx_loaded, 16)
            pool.wait_ge(x_ready, 6 if stop > 2 else [1, 2][stop - 1])
            if stop > 98:
                pool.wait_ge(dve_step, DVE_STEP["f_ready"])
                pool.dma_start(BR[0:96, :], moe_bias).then_inc(bias_in, 16)
                nc.gpsimd.memset(TR[:, :, :], 1.0).then_inc(tri_one, 1)
                pool.wait_ge(tri_one, 1)
                nc.gpsimd.affine_select(out=TR[:, :, :], in_=TR[:, :, :], compare_op=ALU.is_gt, fill=0.0, base=0,
                                        pattern=[[1, EXPERTS], [-1, EXPERTS]], channel_multiplier=0).then_inc(tri_ready, 1)
                pool.wait_ge(dve_step, DVE_STEP["y_final"])
                pool.dma_start(out, YT[:, :, :].rearrange("p n d -> p (n d)")).then_inc(out_stored, 16)
            if stop in (96, 97, 98):
                pool.wait_ge(dve_step, DVE_STEP["f_ready"])
            if stop < 99:
                pool.dma_start(out.rearrange("p (a b) -> p a b", b=T), X[:, :, :]).then_inc(out_stored, 16)

        @block.tensor
        def _(pe):
            mm = nc.tensor.matmul

            def loaded(b):
                if isinstance(b, int):
                    pe.wait_ge(slot_loaded[b % RING], 16 * (b // RING + 1))

            def W(b, k):
                return ring[:, b % RING, :].rearrange("p (k n) -> p k n", k=k)

            def ffn(n, base):
                def chunk_gate_up(slot, turns, J, buf):
                    for which in range(2):
                        s = (slot + which) % RING
                        pe.wait_ge(slot_loaded[s], turns[which])
                        if which == 0 and J is not None:
                            pe.wait_ge(hidden_ready, J)
                        w = ring[:, s, :].rearrange("p (k n) -> p k n", k=KD)
                        dst = ps[:, 4 + 2 * which + buf, :].rearrange("p (f t) -> p f t", f=2)
                        for f in range(2):
                            for k in range(KD):
                                last = mm(dst[:, f, :], w[:, k, f * P:(f + 1) * P], X[:, k, :],
                                          start=(k == 0), stop=(k == KD - 1))
                        last.then_inc(block_used, 1)

                def chunk_down(slot, turn, J1, buf):
                    pe.wait_ge(slot_loaded[slot % RING], turn)
                    pe.wait_ge(hidden_ready, J1 + 1)
                    w = ring[:, slot % RING, :].rearrange("p (f n) -> p f n", f=2)
                    for f in range(2):
                        for d in range(KD):
                            last = mm(acc8[:, d, :], w[:, f, d * P:(d + 1) * P], HF[:, buf, f, :],
                                      start=False, stop=False, skip_group_check=True)
                    last.then_inc(block_used, 1)

                for b in range(4):
                    mm(ps[:, b, :], zl, zr, start=True, stop=False, skip_group_check=True)
                J0 = n * FCH

                def turn(b):
                    return 16 * (b // RING + 1)
                chunk_gate_up(base, [turn(base), turn(base + 1)], J0 if n else None, J0 % 2)
                with pe.Fori(0, (FCH - 1) // 2) as i:
                    for h in range(2):
                        b = base + 2 + 3 * h
                        chunk_gate_up(b, [i * 16 + turn(b), i * 16 + turn(b + 1)], i * 2 + (J0 + 1 + h), (J0 + 1 + h) % 2)
                        chunk_down(b + 2, i * 16 + turn(b + 2), i * 2 + (J0 + 1 + h), (J0 + h) % 2)
                chunk_down(base + 2 + 3 * (FCH - 1), turn(base + 2 + 3 * (FCH - 1)), J0 + FCH, (J0 + FCH - 1) % 2)

            acc8 = ps[:, 0:4, :].rearrange("p b (a t) -> p (b a) t", a=2)

            def ln(m):
                pe.wait_ge(sum_ready, m + 1)
                for k in range(KD):
                    last = mm(ps[:, 4, 0:T], C("ones_d"), X[:, k, :], start=(k == 0), stop=(k == KD - 1))
                last.then_inc(mean_ready, 1)
                pe.wait_ge(squared, m + 1)
                for k in range(KD):
                    last = mm(ps[:, 5, 0:T], C("ones_d"), XS[:, k, :], start=(k == 0), stop=(k == KD - 1))
                last.then_inc(var_ready, 1)
                pe.wait_ge(x_ready, m + 1)

            def mixer(l):
                base = LB[l] + FFN_BLOCKS
                for b in range(IN_BLOCKS):
                    loaded(base + b)
                    if b >= 4:
                        pe.wait_ge(u_copied, l * IN_BLOCKS + b - 3)
                    w = W(base + b, KD)
                    dst = ps[:, 4 + b % 4, :].rearrange("p (f t) -> p f t", f=2)
                    for f in range(2):
                        for k in range(KD):
                            last = mm(dst[:, f, :], w[:, k, f * P:(f + 1) * P], X[:, k, :],
                                      start=(k == 0), stop=(k == KD - 1))
                    last.then_inc(block_used, 1)
                pe.wait_ge(u_copied, (l + 1) * IN_BLOCKS)
                for n in range(2):
                    last = nc.tensor.transpose(ps[:, 4, n * P:(n + 1) * P], U[:, 13, n * P:(n + 1) * P], ident)
                last.then_inc(vt_ready, 1)
                pe.wait_ge(lru_in, l + 1)
                for which in range(2):
                    for t in range(2):
                        w = V(f"gate_w{l}", (2 * which + t) * P, P)
                        last = mm(ps[:, 6 + which, t * T:(t + 1) * T], w, XC[:, t, :], start=True, stop=True)
                last.then_inc(lru_gates, 1)
                for h in range(HEADS):
                    g, t = divmod(h, 4)
                    if h >= 4:
                        pe.wait_ge(score_read, l * HEADS + h - 3)
                    for n in range(2):
                        lo, hi = (0, P) if n == 0 else (P, 3 * P)
                        last = mm(ps[:, h % 4, lo:hi], U[g * 64:g * 64 + 64, 8 + t, n * P:(n + 1) * P],
                                  U[g * 64:g * 64 + 64, 12, 0:(n + 1) * P], start=True, stop=True)
                    last.then_inc(score_ready, 1)
                pe.wait_ge(prob_ready, l + 1)
                pe.wait_ge(vt_copied, l + 1)
                pe.wait_ge(lru_acts, l + 1)
                for q in range(6):
                    if q >= 4:
                        pe.wait_ge(pt_copied, l * 6 + q - 3)
                    for i in range(4):
                        n = 4 * q + i
                        last = nc.tensor.transpose(ps[:, 4 + q % 4, i * P:(i + 1) * P], SC[:, n // 3, n % 3, :], ident)
                    last.then_inc(pt_ready, 1)
                pe.wait_ge(pt_copied, (l + 1) * 6)
                for h in range(HEADS):
                    g, t = divmod(h, 4)
                    for n in range(2):
                        dst = ps[g * 64:g * 64 + 64, t // 2, (t % 2) * T + n * P:(t % 2) * T + (n + 1) * P]
                        for j in range(n + 1):
                            last = mm(dst, VT[:, j, g * 64:g * 64 + 64], PT[:, h, n + j, :], start=(j == 0), stop=(j == n))
                last.then_inc(attn_ready, 1)
                pe.wait_ge(conv_ready, l + 1)
                for t in range(2):
                    last = mm(ps[:, 4, 0:T], C("ones_c"), CV[:, t, :], start=(t == 0), stop=(t == 1))
                last.then_inc(cmean_ready, 1)
                pe.wait_ge(csq_ready, l + 1)
                for t in range(2):
                    last = mm(ps[:, 5, 0:T], C("ones_c"), CQ[:, t, :], start=(t == 0), stop=(t == 1))
                last.then_inc(cvar_ready, 1)
                pe.wait_ge(attn_copied, l + 1)
                pe.wait_ge(lru_done, l + 1)
                pe.wait_ge(conv_done, l + 1)
                base += IN_BLOCKS
                for b in range(OUT_BLOCKS):
                    loaded(base + b)
                    w = W(base + b, KD)
                    for f in range(2):
                        for k in range(KD):
                            last = mm(acc8[:, 2 * b + f, :], w[:, k, f * P:(f + 1) * P], YC[:, k, :],
                                      start=(k == 0), stop=(k == KD - 1))
                    last.then_inc(block_used, 1)


            def order(d):
                return list(range(8)) if d == 0 else [3, 2, 1, 0, 7, 6, 5, 4]

            def two(hp):
                return slice(hp * 64, hp * 64 + 64)

            def second():
                pe.wait_ge(act_step, ACT_STEP["silc_ready"])
                for b in range(ADA_BLOCKS):
                    loaded(ADA0 + b)
                    w = W(ADA0 + b, KD)
                    for f in range(2):
                        c = 2 * b + f
                        for k in range(KD):
                            last = mm(ps[:, 6, 2 * c:2 * c + 2], w[:, k, f * P:(f + 1) * P], SILC[:, k, :], start=(k == 0), stop=(k == KD - 1))
                    last.then_inc(block_used, 1)
                pe.wait_ge(act_step, ACT_STEP["h_sq"])
                for k in range(KD):
                    last = mm(ps[:, 7, :], C("ones_d"), HSQ[:, k, :, :].rearrange("p s t -> p (s t)"), start=(k == 0), stop=(k == KD - 1))
                last.then_inc(pe_step, 1)
                pe.wait_ge(dve_step, DVE_STEP["h_ready"])
                for b in range(PROJ_BLOCKS):
                    loaded(PROJ0 + b)
                    w = W(PROJ0 + b, KD)
                    for f in range(2):
                        c = 2 * b + f
                        if c >= ZT:
                            continue
                        if c >= 8:
                            pe.wait_ge(z_copied, c - 7)
                        dst = ps[:, c % 8, :].rearrange("p (s t) -> p s t", s=2)
                        both = 4 <= c < 6 or 10 <= c < 20
                        for k in range(KD):
                            if both:
                                last = mm(ps[:, c % 8, :], w[:, k, f * P:(f + 1) * P], H[:, k, :, :].rearrange("p s t -> p (s t)"), start=(k == 0), stop=(k == KD - 1))
                            else:
                                last = mm(dst[:, 1, :], w[:, k, f * P:(f + 1) * P], H[:, k, 1, :], start=(k == 0), stop=(k == KD - 1))
                        if f == 0:
                            last.then_inc(tile_done, 1)
                    if 2 * b + 1 < ZT:
                        last.then_inc(block_used, 1)
                    else:
                        pe.wait_ge(tile_done, PROJ_BLOCKS)
                        pe.sem_inc(block_used, 1)
                pe.wait_ge(z_copied, ZT)
                for t in range(5):
                    src = QA[:, t, :] if t < 4 else KA[:, 1, :]
                    last = mm(ps[:, t, 0:T], C("rot"), src, start=True, stop=True)
                last.then_inc(pe_step, 1)
                for j in range(4):
                    last = nc.tensor.transpose(ps[:, 5, j * P:(j + 1) * P], VA[:, j // 2, (j % 2) * P:(j % 2 + 1) * P], ident)
                last.then_inc(pe_step, 1)
                pe.wait_ge(dve_step, DVE_STEP["rot_read"])
                pe.wait_ge(act_step, ACT_STEP["vk_copied"])
                for n in range(2):
                    for h in range(HEADS):
                        g, t = divmod(h, 4)
                        if n:
                            if h == 0:
                                pe.wait_ge(at_copied, 1)
                        elif h >= 4:
                            pe.wait_ge(s2_read, h - 3)
                        if n and h >= 4:
                            pe.wait_ge(s2_read, HEADS + h - 3)
                        last = mm(ps[:, h % 4, :], QR[two(g), t, n * P:(n + 1) * P], KR[two(g), :, :].rearrange("p s t -> p (s t)"), start=True, stop=True)
                        last.then_inc(s2_done, 1)
                    pe.wait_ge(s2_prob, n + 1)
                    for q in range(8):
                        if q >= 4:
                            pe.wait_ge(p2_copied, n * 8 + q - 3)
                        for j in range(4):
                            last = nc.tensor.transpose(ps[:, 4 + q % 4, j * P:(j + 1) * P], S2[:, q, j, :], ident)
                        last.then_inc(p2_done, 1)
                    pe.wait_ge(p2_copied, n * 8 + 8)
                    for h in range(HEADS):
                        g, t = divmod(h, 4)
                        for j in range(4):
                            last = mm(ps[two(g), 0, t * P:(t + 1) * P], VK[:, j, g * 64:g * 64 + 64], P2[:, h, j, :], start=(j == 0), stop=(j == 3))
                    last.then_inc(at_done, 1)
                pe.wait_ge(act_step, ACT_STEP["kk_sq"])
                for t in range(4):
                    last = mm(ps[:, 1 + t, :], C("heads_sum"), BF[:, t, :], start=True, stop=True)
                last.then_inc(pe_step, 1)
                pe.wait_ge(act_step, ACT_STEP["kk_std"])
                for c in range(8):
                    for p in range(4):
                        for hp in range(2):
                            at = (c * 4 + p) * CH
                            last = mm(ps[two(hp), 4 + at // 512, at % 512:at % 512 + CH], SH[two(hp), 8 + p, c // 4, (c % 4) * CH:(c % 4 + 1) * CH],
                                      ident[two(hp), two(hp)], start=True, stop=True)
                last.then_inc(pe_step, 1)
                for d in range(2):
                    pe.wait_ge(act_step, ACT_STEP["tanh_ready"])
                    pe.wait_ge(act_step, ACT_STEP["vm_copied"])
                    if d:
                        pe.wait_ge(st_ready, 9)
                    for t in range(4):
                        mm(ps[:, t, :], V("w2", t * P, P)[two(d), :], SH[two(d), 12, :, :].rearrange("p s t -> p (s t)"), start=True, stop=True)
                        last = mm(ps[:, 4 + t, :], V("a2", t * P, P)[two(d), :], SH[two(d), 13, :, :].rearrange("p s t -> p (s t)"), start=True, stop=True)
                    last.then_inc(lora_done, 1)
                    pe.wait_ge(feat_ready, d + 1)
                    for m in range(4):
                        Q = 4 * d + m
                        pair = order(d)[2 * m:2 * m + 2]
                        for x, c in enumerate(pair):
                            cs = slice(c * CH, (c + 1) * CH)
                            if x:
                                pe.wait_ge(mt_ready, 2 * Q + 1)
                            for p in range(4):
                                for w, src in enumerate((BF, KF)):
                                    for hp in range(2):
                                        last = mm(ps[two(hp), p // 2, (p % 2) * 256 + w * P:(p % 2) * 256 + (w + 1) * P], src[two(hp), p, cs],
                                                  AR[two(hp), p, c, :, :].rearrange("p a t -> p (a t)"), start=True, stop=True)
                            last.then_inc(m_done, 1)
                            if x:
                                pe.wait_ge(bk_ready, 2 * Q + 1)
                            for w, src in enumerate((BF, KF)):
                                for p in range(4):
                                    for hp in range(2):
                                        last = mm(ps[two(hp), 2, (w * 4 + p) * CH:(w * 4 + p + 1) * CH], src[two(hp), p, cs], ident[two(hp), two(hp)], start=True, stop=True)
                            last.then_inc(bk_done, 1)
                        for x in range(2):
                            pe.wait_ge(e_ready, 12 * Q + x + 1)
                            for p in range(4):
                                for hp in range(2):
                                    at = p * CH
                                    last = mm(ps[two(hp), (4, 1)[x], at:at + CH], EBS[x][two(hp), 0, p, :], C("eye2")[two(hp), :], start=True, stop=True)
                            last.then_inc(d_done, 1)
                        for n in range(1, 6):
                            for x in range(2):
                                pe.wait_ge(e_ready, 12 * Q + 2 * n + x + 1)
                                pe.wait_ge(xz_ready, 12 * Q + 2 * (n - 1) + x + 1)
                                for p in range(4):
                                    for hp in range(2):
                                        at = p * CH
                                        last = mm(ps[two(hp), (4, 1)[x], at:at + CH], EBS[x][two(hp), n % 2, p, :], XZS[x][two(hp), 0, p, :], start=True, stop=True)
                                last.then_inc(w_done, 1)
                            for x in range(2):
                                pe.wait_ge(w_ready, 10 * Q + 2 * (n - 1) + x + 1)
                                bank = (5, 0)[x]
                                if n < 5:
                                    for p in range(4):
                                        for hp in range(2):
                                            mm(ps[two(hp), bank, p * CH:(p + 1) * CH], XZS[x][two(hp), 1, p, :], WWS[x][two(hp), p, :], start=True, stop=True)
                                for p in range(4):
                                    for hp in range(2):
                                        last = mm(ps[two(hp), bank, 256 + p * CH:256 + (p + 1) * CH], WWS[x][two(hp), p, :], XZS[x][two(hp), 1, p, :], start=True, stop=True)
                                last.then_inc(d_done, 1)
                        for x, c in enumerate(pair):
                            i = 2 * m + x
                            B = d * 8 + i
                            MT, BK, XZ = MTS[x], BKS[x], XZS[x]
                            pe.wait_ge(st_ready, 9 * d + i + 1)
                            pe.wait_ge(mt_ready, B + 1)
                            for p in range(4):
                                for hp in range(2):
                                    mm(ps[two(hp), 3, p * CH:(p + 1) * CH], AR[two(hp), p, c, 0, :], STT[two(hp), p, :], start=True, stop=False)
                                    last = mm(ps[two(hp), 3, p * CH:(p + 1) * CH], MT[two(hp), p, 2, :], VM[two(hp), c, p, :], start=False, stop=True)
                            last.then_inc(u0_done, 1)
                            pe.wait_ge(u0_ready, B + 1)
                            pe.wait_ge(xz_ready, 12 * Q + 10 + x + 1)
                            for p in range(4):
                                for hp in range(2):
                                    last = mm(ps[two(hp), 3, 256 + p * CH:256 + (p + 1) * CH], XZ[two(hp), 1, p, :], U0[two(hp), p, :], start=True, stop=True)
                            last.then_inc(uu_done, 1)
                            pe.wait_ge(uu_ready, B + 1)
                            pe.wait_ge(bk_ready, B + 1)
                            for p in range(4):
                                for hp in range(2):
                                    dst = ps[two(hp), 7, p * CH:(p + 1) * CH]
                                    mm(dst, BK[two(hp), 0, p, :], UU[two(hp), p, :], start=True, stop=False)
                                    last = mm(dst, BK[two(hp), 1, p, :], VM[two(hp), c, p, :], start=False, stop=True)
                            if i >= 4:
                                for p in range(4):
                                    for hp in range(2):
                                        dst = ps[two(hp), 6, p * CH:(p + 1) * CH]
                                        mm(dst, STT[two(hp), p, :], AR[two(hp), p, c, 1, :], start=True, stop=False)
                                        mm(dst, UU[two(hp), p, :], MT[two(hp), p, 1, :], start=False, stop=False)
                                        last = mm(dst, VM[two(hp), c, p, :], MT[two(hp), p, 3, :], start=False, stop=True)
                            last.then_inc(s_done, 1)
                if stop == 96:
                    return
                pe.wait_ge(st_ready, 18)
                hm = C("heads_mean")
                for t in range(4):
                    last = mm(ps[:, t // 2, (t % 2) * T:(t % 2 + 1) * T], hm, YO[:, t, :], start=True, stop=True)
                last.then_inc(pe_step, 1)
                pe.wait_ge(dve_step, DVE_STEP["rb_ready"])
                for t in range(4):
                    last = mm(ps[:, 4 + t // 2, (t % 2) * T:(t % 2 + 1) * T], C("heads_sum"), YB[:, t, :], start=True, stop=True)
                last.then_inc(pe_step, 1)
                pe.wait_ge(act_step, ACT_STEP["gl_ready"])
                for t in range(4):
                    last = mm(ps[:, 6 + t // 2, (t % 2) * T:(t % 2 + 1) * T], V("g2", t * P, P), SH[:, 14, 1, :], start=True, stop=True)
                last.then_inc(pe_step, 1)
                pe.wait_ge(act_step, ACT_STEP["y_sq"])
                for t in range(4):
                    last = mm(ps[:, 2 + t // 2, (t % 2) * T:(t % 2 + 1) * T], hm, YQ[:, t, :], start=True, stop=True)
                last.then_inc(pe_step, 1)
                pe.wait_ge(dve_step, DVE_STEP["rw_ready"])
                for br, src in enumerate((AT, YO)):
                    for b in range(2):
                        blk = UP0 + 2 * br + b
                        loaded(blk)
                        w = W(blk, 4)
                        for dd in range(4):
                            dt = 4 * b + dd
                            for k in range(4):
                                last = mm(ps[:, 4 * br + dt // 2, (dt % 2) * T:(dt % 2 + 1) * T], w[:, k, dd * P:(dd + 1) * P], src[:, k, :], start=(k == 0), stop=(k == 3))
                        last.then_inc(block_used, 1)
                pe.wait_ge(dve_step, DVE_STEP["mg_ready"])
                for b in range(OUT_BLOCKS):
                    loaded(OUT0 + b)
                    w = W(OUT0 + b, KD)
                    for f in range(2):
                        for k in range(KD):
                            last = mm(acc8[:, 2 * b + f, :], w[:, k, f * P:(f + 1) * P], MG[:, k, :], start=(k == 0), stop=(k == KD - 1))
                    last.then_inc(block_used, 1)
                pe.wait_ge(act_step, ACT_STEP["mix_copied"])
                for k in range(KD):
                    last = mm(ps[:, 4, 0:T], C("ones_d"), MH[:, k, :], start=(k == 0), stop=(k == KD - 1))
                last.then_inc(pe_step, 1)
                pe.wait_ge(act_step, ACT_STEP["f_sq"])
                for k in range(KD):
                    last = mm(ps[:, 5, 0:T], C("ones_d"), MH[:, k, :], start=(k == 0), stop=(k == KD - 1))
                last.then_inc(pe_step, 1)


            def moe():
                pe.wait_ge(dve_step, DVE_STEP["f_ready"])
                for k in range(KD):
                    for n in range(2):
                        last = nc.tensor.transpose(ps[:, 2 * n + k // 4, (k % 4) * P:(k % 4 + 1) * P], MG[:, k, n * P:(n + 1) * P], ident)
                last.then_inc(tok_done, 1)
                for k in range(KD):
                    for n in range(2):
                        last = nc.tensor.transpose(ps[:, 4 + 2 * n + k // 4, (k % 4) * P:(k % 4 + 1) * P], X[:, k, n * P:(n + 1) * P], ident)
                last.then_inc(tok_done, 1)
                pe.wait_ge(tok_copied, 1)
                wr = V("w_router", 0, KD * EXPERTS).rearrange("p (k e) -> p k e", k=KD)
                for n in range(2):
                    for k in range(KD):
                        last = mm(ps[:, 0, n * EXPERTS:(n + 1) * EXPERTS], MG[:, k, n * P:(n + 1) * P], wr[:, k, :], start=(k == 0), stop=(k == KD - 1))
                last.then_inc(pe_step, 1)
                pe.wait_ge(dve_step, DVE_STEP["gb_ready"])
                for k in range(KD):
                    last = mm(ps[:, 1 + k // 4, (k % 4) * P:(k % 4 + 1) * P], GB[:, k, :], ident, start=True, stop=True)
                last.then_inc(tok_done, 1)
                pe.wait_ge(dve_step, DVE_STEP["mask_ready"])
                mm(ps[:, 3, 0:EXPERTS], C("before"), MK[:, 0, :], start=True, stop=True)
                mm(ps[:, 3, EXPERTS:2 * EXPERTS], C("ones"), MK[:, 0, :], start=True, stop=False)
                mm(ps[:, 3, EXPERTS:2 * EXPERTS], C("before"), MK[:, 1, :], start=False, stop=True)
                mm(ps[:, 3, 64:64 + EXPERTS], C("ones"), MK[:, 0, :], start=True, stop=False)
                mm(ps[:, 3, 64:64 + EXPERTS], C("ones"), MK[:, 1, :], start=False, stop=True).then_inc(pe_step, 1)
                pe.wait_ge(dve_step, DVE_STEP["moe_ready"])
                pe.wait_ge(tok_copied, 3)

                def gather(E1):
                    pe.wait_ge(onehot_ready, E1)
                    for k in range(KD):
                        for n in range(2):
                            last = mm(ps[:, 2 + k // 4, (k % 4) * P:(k % 4 + 1) * P], HT[:, n, k * P:(k + 1) * P], ON[:, n, :], start=(n == 0), stop=(n == 1))
                    last.then_inc(gather_done, 1)

                def combine(E):
                    pe.wait_ge(yb_ready, E + 1)
                    pe.wait_ge(comb_read, E * 2 + 1)
                    for n in range(2):
                        for half in range(2):
                            last = mm(ps[:, (6, 2)[n] + half, :], PTE[two(half), n, :], YBE[two(half), :], start=True, stop=True)
                        last.then_inc(comb_done, 1)

                gather(1)

                def expert(E):
                    def products(bank, stationary, chooser, column, first):
                        for half in range(2):
                            c = column + half * 512
                            mm(ps[two(half), bank, :], chooser[0:96, :], B3[0:96, c:c + 512], start=True, stop=False)
                        for k in range(KD):
                            for half in range(2):
                                b = MOE0 + first + 2 * (k // 4) + half
                                if k % 4 == 0:
                                    pe.wait_ge(slot_loaded[b % RING], E * 32 + 16 * (b // RING + 1))
                                last = mm(ps[two(half), bank, :], stationary(k), ring[:, b % RING, (k % 4) * 512:(k % 4 + 1) * 512],
                                          start=False, stop=(k == KD - 1))
                                if k % 4 == 3:
                                    last.then_inc(block_used, 1)

                    pe.wait_ge(xe_ready, E + 1)
                    pe.wait_ge(selg_ready, E + 1)
                    for c in range(2):
                        products(c, lambda k: XE[:, k, 0:64], SELG, 1024 * c, 4 * c)
                        if c == 0:
                            combine(E)
                            pe.wait_ge(comb_read, E * 2 + 2)
                            for n in range(2):
                                last = nc.tensor.transpose(ps[:, 6, n * P:(n + 1) * P], ON[:, n, :], ident)
                            last.then_inc(pt_turned, 1)
                    pe.wait_ge(comb_read, E * 2 + 3)
                    gather(E + 2)
                    pe.wait_ge(glu_done, E * 2 + 3)
                    for q in range(4):
                        last = nc.tensor.transpose(ps[:, 4, q * P:(q + 1) * P], AC[:, q // 2, (q % 2) * P:(q % 2 + 1) * P], ident)
                    last.then_inc(act_turned, 1)
                    pe.wait_ge(actt_ready, E + 1)
                    pe.wait_ge(seld_ready, E + 1)
                    products(5, lambda k: AT_[:, 2 * (k // 4) + k % 2, two((k // 2) % 2)], SELD, 2048, 8)

                with pe.Fori(0, EXPERTS) as E:
                    expert(E)
                pe.wait_ge(extra_ready, 1)
                extra = pe.value_load(FLAG[0:1, 0:1], min_val=0, max_val=EXTRA - 1)
                with pe.If(extra > 0):
                    with pe.Fori(EXPERTS, extra + EXPERTS) as E:
                        expert(E)
                    combine(extra + EXPERTS)
                with pe.Else():
                    combine(EXPERTS)

            pe.wait_ge(x_loaded, 16)
            pe.wait_ge(vec_loaded, 16)
            pe.wait_ge(con_loaded, 16)
            pe.wait_ge(zero_ready, 1)
            mm(ps[0:HEADS, 7, 0:P], V("rel_bias", 0, HEADS)[0:32, :], C("bucket")[0:32, :],
               start=True, stop=True).then_inc(rel_ready, 1)
            pe.wait_ge(rv_ready, 1)
            for l in range(LAYERS):
                ffn(2 * l, LB[l])
                ln(3 * l)
                if stop == 1:
                    return
                mixer(l)
                ln(3 * l + 1)
                if stop == 2:
                    return
                ffn(2 * l + 1, LB[l] + FFN_BLOCKS + IN_BLOCKS + OUT_BLOCKS)
                ln(3 * l + 2)
            if stop > 3:
                second()
            if stop > 98:
                moe()

        @block.scalar
        def _(act):
            A = nc.scalar.activation

            def ffn(n, base):
                def silu(used, buf, prev):
                    act.wait_ge(block_used, used)
                    if prev is not None:
                        act.wait_ge(hidden_ready, prev + 1)
                    A(SG[:, buf, :, :].rearrange("p f t -> p (f t)"), ps[:, 4 + buf, :], ACT.Silu).then_inc(silu_ready, 1)
                J0 = n * FCH
                silu(base + 1, J0 % 2, J0 - 1 if n else None)
                with act.Fori(0, (FCH - 1) // 2) as i:
                    for h in range(2):
                        silu(i * 6 + (base + 3 + 3 * h), (J0 + 1 + h) % 2, i * 2 + (J0 + h))

            def ln(m):
                act.wait_ge(centred, m + 1)
                A(XS[:, :, :], X[:, :, :], ACT.Square).then_inc(squared, 1)
                act.wait_ge(var_ready, m + 1)
                A(ST[:, 0, 0:T], ps[:, 5, 0:T], ACT.Sqrt, bias=EPS2[:, 0:1]).then_inc(std_ready, 1)

            def mixer(l):
                for b in range(IN_BLOCKS):
                    act.wait_ge(block_used, LB[l] + FFN_BLOCKS + b + 1)
                    src = ps[:, 4 + b % 4, :].rearrange("p (f t) -> p f t", f=2)
                    if b == 1:
                        A(U[:, 2:4, :], src, ACT.Sigmoid).then_inc(u_copied, 1)
                    elif b == 2:
                        A(XB[:, :, LTAPS - 1:], src, ACT.Copy).then_inc(u_copied, 1)
                    else:
                        A(U[:, 2 * b:2 * b + 2, :], src, ACT.Copy).then_inc(u_copied, 1)
                act.wait_ge(vt_ready, l + 1)
                A(VT[:, :, :].rearrange("p a b -> p (a b)"), ps[:, 4, 0:2 * P], ACT.Copy).then_inc(vt_copied, 1)
                act.wait_ge(lru_gates, l + 1)
                for which, bias in ((0, "ba"), (1, "bx")):
                    for t in range(2):
                        last = A(LR[:, which, t, :], ps[:, 6 + which, t * T:(t + 1) * T], ACT.Sigmoid, bias=V(f"{bias}{l}", t))
                        last.then_inc(act_chain, 1)
                act.wait_ge(act_chain, l * 4 + 4)
                for t in range(2):
                    A(LR[:, 2, t, :], LR[:, 0, t, :], ACT.Exp, scale=LC[:, 2 * l + t:2 * l + t + 1])
                    last = A(LR[:, 3, t, :], LR[:, 0, t, :], ACT.Tanh, scale=LN_[:, 2 * l + t:2 * l + t + 1])
                A(LR[:, 7, :, :], U[:, 6:8, :], ACT.Gelu_apprx_tanh).then_inc(lru_acts, 1)
                act.wait_ge(score_shifted, l + 1)
                A(SC[:, :, :, :], SC[:, :, :, :], ACT.Exp)
                A(ES[:, :, :], ES[:, :, :], ACT.Exp).then_inc(exp_ready, 1)
                act.wait_ge(lru_m2, l + 1)
                A(LR[:, 4, :, :], LR[:, 3, :, :], ACT.Sqrt).then_inc(lru_mult, 1)
                for q in range(6):
                    act.wait_ge(pt_ready, l * 6 + q + 1)
                    A(PT[:, :, :, :].rearrange("p h a b -> p (h a b)")[:, q * 512:(q + 1) * 512], ps[:, 4 + q % 4, :],
                      ACT.Copy).then_inc(pt_copied, 1)
                act.wait_ge(attn_ready, l + 1)
                A(YC[:, 4:8, :].rearrange("p (b a) t -> p b (a t)", a=2), ps[:, 0:2, :], ACT.Copy).then_inc(attn_copied, 1)
                act.wait_ge(cc_ready, l + 1)
                A(CQ[:, :, :], CV[:, :, :], ACT.Square).then_inc(csq_ready, 1)
                act.wait_ge(cvar_ready, l + 1)
                A(ST[:, 1, 0:T], ps[:, 5, 0:T], ACT.Sqrt, bias=EPS2[:, 0:1]).then_inc(cstd_ready, 1)
                act.wait_ge(cnorm_ready, l + 1)
                for t in range(2):
                    last = A(YC[:, t, :], CV[:, t, :], ACT.Silu, scale=V(f"cln_g{l}", t), bias=V(f"cln_b{l}", t))
                last.then_inc(conv_done, 1)


            def second():
                act.wait_ge(x_ready, 6)
                A(SILC[:, :, :], V("c", 0, 16).rearrange("p (k s) -> p k s", s=2), ACT.Silu).then_inc(act_step, 1)
                act.wait_ge(ctx_loaded, 16)
                for s_, src in enumerate((H[:, :, 0, :], X[:, :, :])):
                    last = A(HSQ[:, :, s_, :], src, ACT.Square)
                last.then_inc(act_step, 1)
                act.wait_ge(pe_step, PE_STEP["h_ms"])
                A(RS[:, :, :].rearrange("p s t -> p (s t)"), ps[:, 7, :], ACT.Sqrt, bias=EPS2[:, 1:2]).then_inc(act_step, 1)
                for c in range(ZT):
                    if c % 2 == 0:
                        act.wait_ge(tile_done, c // 2 + 1)
                    else:
                        act.wait_ge(block_used, PROJ0 + c // 2 + 1)
                    if c == 0:
                        act.wait_ge(dve_step, DVE_STEP["pads_ready"])
                    src = ps[:, c % 8, :].rearrange("p (s t) -> p s t", s=2)
                    b = V("b_in", c)
                    if c < 4:
                        A(QA[:, c, :], src[:, 1, :], ACT.Identity, bias=b).then_inc(z_copied, 1)
                    elif c < 6:
                        A((KA, VA)[c - 4][:, :, :], src, ACT.Identity, bias=b).then_inc(z_copied, 1)
                    elif c < 21:
                        s0 = 0 if 10 <= c < 20 else 1
                        A(ZR[:, c - 6, s0:2, 1:T + 1], src[:, s0:2, :], ACT.Identity, bias=b).then_inc(z_copied, 1)
                    else:
                        A(G[:, c - 21, :], src[:, 1, :], ACT.Sigmoid, bias=b).then_inc(z_copied, 1)
                act.wait_ge(pe_step, PE_STEP["vk_done"])
                A(VK[:, :, :].rearrange("p a b -> p (a b)"), ps[:, 5, :], ACT.Copy).then_inc(act_step, 1)
                for n in range(2):
                    act.wait_ge(s2_shifted, n + 1)
                    A(S2[:, :, :, :], S2[:, :, :, :], ACT.Exp)
                    A(ES2, ES2, ACT.Exp).then_inc(s2_exp, 1)
                    for q in range(8):
                        act.wait_ge(p2_done, n * 8 + q + 1)
                        if n and q == 0:
                            act.wait_ge(at_done, 1)
                        A(P2[:, q, :, :].rearrange("p a b -> p (a b)"), ps[:, 4 + q % 4, :], ACT.Copy).then_inc(p2_copied, 1)
                    act.wait_ge(at_done, n + 1)
                    A(AT[:, :, n * P:(n + 1) * P], ps[:, 0, :].rearrange("p (a b) -> p a b", a=4), ACT.Copy).then_inc(at_copied, 1)
                act.wait_ge(dve_step, DVE_STEP["kk_raw"])
                A(BF[:, :, :], KK[:, :, :], ACT.Square).then_inc(act_step, 1)
                A(SH[:, 12, :, :], SH[:, 12, :, :], ACT.Tanh).then_inc(act_step, 1)
                act.wait_ge(pe_step, PE_STEP["kk_sum"])
                A(BF[:, :, :], ps[:, 1:5, :], ACT.Sqrt).then_inc(act_step, 1)
                act.wait_ge(pe_step, PE_STEP["vm_done"])
                A(VM[:, :, :, :].rearrange("p (b c) d e -> p b (c d e)", b=4), ps[:, 4:8, :], ACT.Copy).then_inc(act_step, 1)
                for d in range(2):
                    act.wait_ge(lora_done, d + 1)
                    act.wait_ge(dve_step, DVE_STEP["kk_used"])
                    for t in range(4):
                        A(KF[:, t, :], ps[:, t, :], ACT.Sigmoid, bias=V("w0", 4 * d + t))
                        last = A(BF[:, t, :], ps[:, 4 + t, :], ACT.Sigmoid, bias=V("a0", 4 * d + t))
                    last.then_inc(sig_ready, 1)
                    act.wait_ge(ll_ready, d + 1)
                    l8 = LL[:, :, :].rearrange("p t (c e) -> p (t c) e", e=CH)
                    ar = AR[:, :, :, :, :].rearrange("p t c a e -> p (t c) a e")
                    A(PC[:, :, :], TOT[:, :, :], ACT.Exp)
                    A(ar[:, :, 0, :], ar[:, :, 0, :], ACT.Exp).then_inc(ex_a, 1)
                    A(ar[:, :, 1, :], l8, ACT.Exp).then_inc(ex_r, 1)
                    act.wait_ge(ex_r, d + 1)
                    A(LL[:, :, :], LL[:, :, :], ACT.Exp, scale=-1.0).then_inc(ex_inv, 1)
                    for m in range(4):
                        Q = 4 * d + m
                        for x in range(2):
                            act.wait_ge(bk_done, 2 * Q + x + 1)
                            if Q:
                                act.wait_ge(s_done, 2 * Q)
                            A(BKS[x][:, :, :, :].rearrange("p w a b -> p (w a b)"), ps[:, 2, :], ACT.Copy).then_inc(bk_ready, 1)
                        for n in range(1, 6):
                            for x in range(2):
                                act.wait_ge(w_done, 10 * Q + 2 * (n - 1) + x + 1)
                                A(WWS[x][:, :, :].rearrange("p a b -> p (a b)"), ps[:, (4, 1)[x], 0:256], ACT.Copy).then_inc(w_ready, 1)
                        for x in range(2):
                            B = 2 * Q + x
                            act.wait_ge(u0_done, B + 1)
                            A(U0[:, :, :].rearrange("p a b -> p (a b)"), ps[:, 3, 0:256], ACT.Copy).then_inc(u0_ready, 1)
                            act.wait_ge(uu_done, B + 1)
                            A(UU[:, :, :].rearrange("p a b -> p (a b)"), ps[:, 3, 256:512], ACT.Copy).then_inc(uu_ready, 1)
                if stop == 96:
                    return
                A(SH[:, 14, 1, :], SH[:, 14, 1, :], ACT.Sigmoid).then_inc(act_step, 1)
                act.wait_ge(dve_step, DVE_STEP["y_centred"])
                A(YQ[:, :, :], YO[:, :, :], ACT.Square).then_inc(act_step, 1)
                act.wait_ge(pe_step, PE_STEP["y_var"])
                A(YQ[:, :, :].rearrange("p (b a) t -> p b (a t)", b=2), ps[:, 2:4, :], ACT.Sqrt, bias=EPS2[:, 2:3]).then_inc(act_step, 1)
                act.wait_ge(block_used, OUT0 + OUT_BLOCKS)
                A(MH[:, :, :].rearrange("p (b a) t -> p b (a t)", a=2), ps[:, 0:4, :], ACT.Square).then_inc(act_step, 1)
                act.wait_ge(pe_step, PE_STEP["mix_ms"])
                A(RS[:, 0, :], ps[:, 4, 0:T], ACT.Sqrt, bias=EPS2[:, 1:2]).then_inc(act_step, 1)
                act.wait_ge(dve_step, DVE_STEP["xm_ready"])
                A(MH[:, :, :], X[:, :, :], ACT.Square).then_inc(act_step, 1)
                act.wait_ge(pe_step, PE_STEP["f_ms"])
                A(RS[:, 1, :], ps[:, 5, 0:T], ACT.Sqrt, bias=EPS2[:, 1:2]).then_inc(act_step, 1)


            def moe():
                act.wait_ge(tok_done, 1)
                A(HT[:, :, :].rearrange("p n d -> p (n d)"), ps[:, 0:4, :].rearrange("p b n -> p (b n)"), ACT.Copy).then_inc(tok_copied, 1)
                act.wait_ge(tok_done, 2)
                A(XT[:, :, :].rearrange("p n d -> p (n d)"), ps[:, 4:8, :].rearrange("p b n -> p (b n)"), ACT.Copy).then_inc(tok_copied, 1)
                act.wait_ge(tok_done, 3)
                A(GR[:, :], ps[:, 1:3, :].rearrange("p b n -> p (b n)"), ACT.Copy).then_inc(tok_copied, 1)
                act.wait_ge(dve_step, DVE_STEP["lg_shift"])
                A(EX[:, :, :], EX[:, :, :], ACT.Exp).then_inc(act_step, 1)

                def tokens(E1):
                    act.wait_ge(gather_done, E1)
                    A(XE[:, :, :].rearrange("p k n -> p (k n)"), ps[:, 2:4, :].rearrange("p b n -> p (b n)"), ACT.Copy).then_inc(xe_ready, 1)

                act.sem_inc(yb_ready, 1)
                tokens(1)

                def expert(E, used):
                    for c in range(2):
                        act.wait_ge(clipped, E * 2 + (c + 1))
                        act.wait_ge(glu_done, E * 2 + (c + 1))
                        A(SGM[:, :], TG[:, :], ACT.Sigmoid, scale=1.702).then_inc(sigm_ready, 1)
                        if c == 0:
                            act.wait_ge(pt_turned, E + 1)
                            A(PTE[:, :, :].rearrange("p n s -> p (n s)"), ps[:, 6, 0:2 * P], ACT.Copy).then_inc(pte_ready, 1)
                    tokens(E + 2)
                    act.wait_ge(act_turned, E + 1)
                    A(AT_[:, :, :].rearrange("p k n -> p (k n)"), ps[:, 4, :], ACT.Copy).then_inc(actt_ready, 1)
                    act.wait_ge(block_used, used + EXPERT_BLOCKS)
                    A(YBE[:, :], ps[:, 5, :], ACT.Copy).then_inc(yb_ready, 1)

                with act.Fori(0, EXPERTS) as E:
                    expert(E, E * EXPERT_BLOCKS + MOE0)
                act.wait_ge(extra_ready, 1)
                extra = act.value_load(FLAG[0:1, 0:1], min_val=0, max_val=EXTRA - 1)
                with act.If(extra > 0):
                    with act.Fori(EXPERTS, extra + EXPERTS) as E:
                        expert(E, E * EXPERT_BLOCKS + MOE0)
                act.wait_ge(dve_step, DVE_STEP["y_ss"])
                for n in range(2):
                    last = A(SS[:, n:n + 1], SS[:, n:n + 1], ACT.Sqrt, bias=EPS2[:, 1:2], scale=1.0 / D)
                last.then_inc(act_step, 1)

            act.wait_ge(vec_loaded, 16)
            act.wait_ge(zero_ready, 1)
            A(LT[:, 0, :], V("lam", 0, 2 * LAYERS), ACT.Abs).then_inc(lam_abs, 1)
            act.wait_ge(lam_abs, 1)
            A(LT[:, 1, :], LT[:, 0, :], ACT.Exp, scale=-1.0).then_inc(lam_exp, 1)
            act.wait_ge(lam_exp, 1)
            for l in range(LAYERS):
                ffn(2 * l, LB[l])
                ln(3 * l)
                if stop == 1:
                    return
                mixer(l)
                ln(3 * l + 1)
                if stop == 2:
                    return
                ffn(2 * l + 1, LB[l] + FFN_BLOCKS + IN_BLOCKS + OUT_BLOCKS)
                ln(3 * l + 2)
            if stop > 3:
                second()
            if stop > 98:
                moe()

        @block.vector
        def _(dve):
            v = nc.vector
            chain = [0]

            def link(ins):
                chain[0] += 1
                ins.then_inc(dve_chain, 1)
                dve.wait_ge(dve_chain, chain[0])

            acc8 = ps[:, 0:4, :].rearrange("p b (a t) -> p (b a) t", a=2)

            def ffn(n, base):
                def hidden(J1, buf, used):
                    dve.wait_ge(silu_ready, J1)
                    dve.wait_ge(block_used, used)
                    v.tensor_tensor(HF[:, buf, :, :].rearrange("p f t -> p (f t)"), ps[:, 6 + buf, :],
                                    SG[:, buf, :, :].rearrange("p f t -> p (f t)"), ALU.mult).then_inc(hidden_ready, 1)
                J0 = n * FCH
                hidden(J0 + 1, J0 % 2, base + 2)
                with dve.Fori(0, (FCH - 1) // 2) as i:
                    for h in range(2):
                        hidden(i * 2 + (J0 + 2 + h), (J0 + 1 + h) % 2, i * 6 + (base + 4 + 3 * h))

            def ln(m, scale, used):
                dve.wait_ge(block_used, used)
                link(v.tensor_scalar(XS[:, :, :], acc8, scale, None, ALU.mult))
                v.scalar_tensor_tensor(out=X[:, :, :], in0=X[:, :, :], scalar=ALPHA, in1=XS[:, :, :],
                                       op0=ALU.mult, op1=ALU.add).then_inc(sum_ready, 1)
                dve.wait_ge(mean_ready, m + 1)
                link(v.tensor_copy(ST[:, 2, 0:T], ps[:, 4, 0:T]))
                v.tensor_tensor(X[:, :, :], X[:, :, :], ST[:, 2, 0:T].unsqueeze(1).broadcast_to([P, KD, T]),
                                ALU.subtract).then_inc(centred, 1)
                dve.wait_ge(std_ready, m + 1)
                link(v.reciprocal(ST[:, 3, 0:T], ST[:, 0, 0:T]))
                dve.wait_ge(squared, m + 1)
                link(v.tensor_tensor(X[:, :, :], X[:, :, :], ST[:, 3, 0:T].unsqueeze(1).broadcast_to([P, KD, T]), ALU.mult))
                for k in range(KD):
                    last = v.tensor_scalar(X[:, k, :], X[:, k, :], V("ln_g", m * KD + k), V("ln_b", m * KD + k), ALU.mult, ALU.add)
                last.then_inc(x_ready, 1)

            def mixer(l):
                dve.wait_ge(u_copied, l * IN_BLOCKS + 3)
                for t in range(2):
                    for j in range(LTAPS):
                        w = V(f"lw{l}", t * LTAPS + j)
                        if j == 0:
                            ins = v.tensor_scalar(XC[:, t, :], XB[:, t, 0:T], w, V(f"lb{l}", t), ALU.mult, ALU.add)
                        else:
                            ins = v.scalar_tensor_tensor(out=XC[:, t, :], in0=XB[:, t, j:j + T], scalar=w, in1=XC[:, t, :], op0=ALU.mult, op1=ALU.add)
                        link(ins)
                dve.sem_inc(lru_in, 1)
                dve.wait_ge(bias_loaded, 16 * 2 * HEADS)
                for h in range(HEADS):
                    dve.wait_ge(score_ready, l * HEADS + h + 1)
                    v.scalar_tensor_tensor(out=SC[:, h, :, :].rearrange("p a b -> p (a b)"), in0=ps[:, h % 4, 0:3 * P], scalar=0.125,
                                           in1=BT[:, h, :, :].rearrange("p a b -> p (a b)"),
                                           op0=ALU.mult, op1=ALU.add).then_inc(score_read, 1)
                dve.wait_ge(score_read, (l + 1) * HEADS)
                sink = V(f"sink{l}", 0, HEADS)
                link(v.tensor_reduce(M3[:, :, :], SC[:, :, :, :], AX.X, ALU.max))
                link(v.tensor_tensor(MM[:, :, 1], M3[:, :, 1], M3[:, :, 2], ALU.max))
                v.tensor_tensor(MM[:, :, 0], M3[:, :, 0], sink, ALU.max)
                link(v.tensor_tensor(MM[:, :, 1], MM[:, :, 1], sink, ALU.max))
                link(v.tensor_copy(MM[:, :, 2], MM[:, :, 1]))
                v.tensor_tensor(ES[:, :, :], sink.unsqueeze(2).broadcast_to([P, HEADS, 2]), MM[:, :, 0:2], ALU.subtract)
                v.tensor_tensor(SC[:, :, :, :].rearrange("p h a b -> p (h a) b"), SC[:, :, :, :].rearrange("p h a b -> p (h a) b"),
                                MM[:, :, :].rearrange("p h a -> p (h a)").unsqueeze(2).broadcast_to([P, HEADS * 3, P]),
                                ALU.subtract).then_inc(score_shifted, 1)
                dve.wait_ge(exp_ready, l + 1)
                link(v.tensor_reduce(S3[:, :, :], SC[:, :, :, :], AX.X, ALU.add))
                link(v.tensor_tensor(S3[:, :, 1], S3[:, :, 1], S3[:, :, 2], ALU.add))
                link(v.tensor_tensor(DN[:, :, :], S3[:, :, 0:2], ES[:, :, :], ALU.add))
                link(v.reciprocal(S3[:, :, 0:2], DN[:, :, :]))
                link(v.tensor_copy(S3[:, :, 2], S3[:, :, 1]))
                v.tensor_tensor(SC[:, :, :, :].rearrange("p h a b -> p (h a) b"), SC[:, :, :, :].rearrange("p h a b -> p (h a) b"),
                                S3[:, :, :].rearrange("p h a -> p (h a)").unsqueeze(2).broadcast_to([P, HEADS * 3, P]),
                                ALU.mult).then_inc(prob_ready, 1)
                dve.wait_ge(lru_acts, l + 1)
                link(v.tensor_tensor(LR[:, 5, :, :], LR[:, 2, :, :], LR[:, 2, :, :], ALU.mult))
                v.scalar_tensor_tensor(out=LR[:, 3, :, :], in0=LR[:, 5, :, :], scalar=1.0, in1=LR[:, 3, :, :],
                                       op0=ALU.add, op1=ALU.mult).then_inc(lru_m2, 1)
                link(v.tensor_tensor(LR[:, 1, :, :], LR[:, 1, :, :], XC[:, :, :], ALU.mult))
                dve.wait_ge(lru_mult, l + 1)
                link(v.tensor_tensor(LR[:, 1, :, :], LR[:, 1, :, :], LR[:, 4, :, :], ALU.mult))
                for t in range(2):
                    last = v.tensor_tensor_scan(LR[:, 6, t, :], LR[:, 2, t, :], LR[:, 1, t, :], 0.0, ALU.mult, ALU.add)
                link(last)
                v.tensor_tensor(YC[:, 2:4, :], LR[:, 6, :, :], LR[:, 7, :, :], ALU.mult).then_inc(lru_done, 1)
                link(v.tensor_tensor(YP[:, :, TAPS - 1:], U[:, 0:2, :], U[:, 2:4, :], ALU.mult))
                for j in range(TAPS):
                    for t in range(2):
                        w = V(f"dw_w{l}", t * TAPS + j)
                        if j == 0:
                            last = v.tensor_scalar(CV[:, t, :], YP[:, t, 0:T], w, V(f"dw_b{l}", t), ALU.mult, ALU.add)
                        else:
                            last = v.scalar_tensor_tensor(out=CV[:, t, :], in0=YP[:, t, j:j + T], scalar=w, in1=CV[:, t, :], op0=ALU.mult, op1=ALU.add)
                    link(last)
                dve.sem_inc(conv_ready, 1)
                dve.wait_ge(cmean_ready, l + 1)
                link(v.tensor_copy(ST[:, 2, 0:T], ps[:, 4, 0:T]))
                v.tensor_tensor(CV[:, :, :], CV[:, :, :], ST[:, 2, 0:T].unsqueeze(1).broadcast_to([P, 2, T]), ALU.subtract).then_inc(cc_ready, 1)
                dve.wait_ge(cstd_ready, l + 1)
                link(v.reciprocal(ST[:, 3, 0:T], ST[:, 1, 0:T]))
                v.tensor_tensor(CV[:, :, :], CV[:, :, :], ST[:, 3, 0:T].unsqueeze(1).broadcast_to([P, 2, T]), ALU.mult).then_inc(cnorm_ready, 1)

            dve.sem_inc(hidden_ready, 1)

            def second():
                dve.wait_ge(x_ready, 6)
                v.memset(ZR[:, :, :, 0:1], 0.0)
                v.memset(ZR[:, :, :, T + 1:T + 2], 0.0).then_inc(dve_step, 1)
                link(v.memset(RESET[:, :, :], 1.0))
                v.memset(RESET[:, :, 0:1], 0.0)
                dve.wait_ge(block_used, ADA0 + ADA_BLOCKS)
                link(v.tensor_tensor(ADA[:, :, :], ps[:, 6, 0:96].rearrange("p (c s) -> p c s", s=2),
                                     V("b_ada", 0, 48).unsqueeze(2).broadcast_to([P, 48, 2]), ALU.add))
                for s_ in range(2):
                    link(v.scalar_tensor_tensor(out=GS[:, :, s_], in0=ADA[:, 8:16, s_], scalar=1.0, in1=V("g_pre_mix", 0, 8), op0=ALU.add, op1=ALU.mult))
                link(v.tensor_tensor(GP, ADA[:, 16:24, 1], V("g_post_mix", 0, 8), ALU.mult))
                link(v.scalar_tensor_tensor(out=GF, in0=ADA[:, 32:40, 1], scalar=1.0, in1=V("g_pre_ffn", 0, 8), op0=ALU.add, op1=ALU.mult))
                link(v.tensor_tensor(GQ, ADA[:, 40:48, 1], V("g_post_ffn", 0, 8), ALU.mult))
                dve.wait_ge(act_step, ACT_STEP["h_std"])
                link(v.reciprocal(RS[:, :, :], RS[:, :, :]))
                v.tensor_tensor(H[:, :, 0, :], H[:, :, 0, :], RS[:, 0, :].unsqueeze(1).broadcast_to([P, KD, T]), ALU.mult)
                link(v.tensor_tensor(H[:, :, 1, :], X[:, :, :], RS[:, 1, :].unsqueeze(1).broadcast_to([P, KD, T]), ALU.mult))
                for k in range(KD):
                    for s_ in range(2):
                        last = v.tensor_scalar(H[:, k, s_, :], H[:, k, s_, :], GS[:, k, s_:s_ + 1], ADA[:, k, s_:s_ + 1], ALU.mult, ALU.add)
                last.then_inc(dve_step, 1)
                dve.wait_ge(pe_step, PE_STEP["rot_done"])
                for t in range(5):
                    src, dst = (QA[:, t, :], QR[:, t, :]) if t < 4 else (KA[:, 1, :], KR[:, 1, :])
                    link(v.tensor_tensor(dst, ps[:, t, 0:T], C("sin"), ALU.mult))
                    link(v.tensor_tensor(src, src, C("cos"), ALU.mult))
                    link(v.tensor_tensor(dst, dst, src, ALU.add))
                v.tensor_copy(KR[:, 0, :], KA[:, 0, :]).then_inc(dve_step, 1)
                for c in range(15):
                    s0 = 0 if 4 <= c < 14 else 1
                    z = ZR[:, c, s0:2, :]
                    dst = SH[:, c, s0:2, :]
                    link(v.tensor_tensor(dst, z[:, :, 0:T], z[:, :, 1:T + 1], ALU.subtract))
                    link(v.scalar_tensor_tensor(out=dst, in0=dst, scalar=V("mu_prev", c), in1=z[:, :, 1:T + 1], op0=ALU.mult, op1=ALU.add))
                    link(v.scalar_tensor_tensor(out=dst, in0=z[:, :, 2:T + 2], scalar=V("mu_next", c), in1=dst, op0=ALU.mult, op1=ALU.add))
                    link(v.tensor_scalar(TN, V("mu_next", c), -1.0, None, ALU.mult))
                    link(v.scalar_tensor_tensor(out=dst, in0=z[:, :, 1:T + 1], scalar=TN, in1=dst, op0=ALU.mult, op1=ALU.add))
                for n in range(2):
                    m2 = C("mask2")[:, n * T:(n + 1) * T]
                    for h in range(HEADS):
                        dve.wait_ge(s2_done, n * HEADS + h + 1)
                        if n == 1 and h == 0:
                            dve.wait_ge(at_copied, 1)
                        v.tensor_scalar(S2[:, h, 0:2, :].rearrange("p a b -> p (a b)"), ps[:, h % 4, 0:T], 0.125, None, ALU.mult)
                        v.scalar_tensor_tensor(out=S2[:, h, 2:4, :].rearrange("p a b -> p (a b)"), in0=ps[:, h % 4, T:2 * T], scalar=0.125,
                                               in1=m2, op0=ALU.mult, op1=ALU.add).then_inc(s2_read, 1)
                    dve.wait_ge(s2_read, (n + 1) * HEADS)
                    s3 = S2[:, :, :, :].rearrange("p h a b -> p h (a b)")
                    link(v.tensor_reduce(MX, s3, AX.X, ALU.max))
                    link(v.tensor_tensor(MX, MX, V("sink2", 0, HEADS), ALU.max))
                    v.tensor_tensor(ES2, V("sink2", 0, HEADS), MX, ALU.subtract)
                    v.tensor_tensor(s3, s3, MX.unsqueeze(2).broadcast_to([P, HEADS, 512]), ALU.subtract).then_inc(s2_shifted, 1)
                    dve.wait_ge(s2_exp, n + 1)
                    link(v.tensor_reduce(DN2, s3, AX.X, ALU.add))
                    link(v.tensor_tensor(DN2, DN2, ES2, ALU.add))
                    link(v.reciprocal(DN2, DN2))
                    v.tensor_tensor(s3, s3, DN2.unsqueeze(2).broadcast_to([P, HEADS, 512]), ALU.mult).then_inc(s2_prob, 1)
                dve.wait_ge(at_done, 2)
                for t in range(4):
                    last = v.tensor_scalar(KK[:, t, :], SH[:, 4 + t, :, :].rearrange("p s t -> p (s t)"), V("k_k", t), None, ALU.mult)
                last.then_inc(dve_step, 1)
                dve.wait_ge(act_step, ACT_STEP["kk_std"])
                link(v.tensor_scalar(BF[:, :, :], BF[:, :, :], 1e-12, None, ALU.max))
                link(v.reciprocal(BF[:, :, :], BF[:, :, :]))
                link(v.tensor_tensor(KK[:, :, :], KK[:, :, :], BF[:, :, :], ALU.mult))
                dve.sem_inc(dve_step, 1)
                r4, k4 = SH[:, 0:4, 1, :], SH[:, 4:8, :, :].rearrange("p t s e -> p t (s e)")
                for d in range(2):
                    dve.wait_ge(sig_ready, d + 1)
                    if d:
                        dve.wait_ge(s_done, 8)
                    link(v.tensor_scalar(KF[:, :, :], KF[:, :, :], -math.exp(-0.5), None, ALU.mult))
                    for t in range(4):
                        last = v.tensor_tensor_scan(LL[:, t, :], RESET[:, :, :].rearrange("p c e -> p (c e)"), KF[:, t, :], 0.0, ALU.mult, ALU.add)
                    link(last)
                    l8 = LL[:, :, :].rearrange("p t (c e) -> p (t c) e", e=CH)
                    f8 = KF[:, :, :].rearrange("p t (c e) -> p (t c) e", e=CH)
                    ar = AR[:, :, :, :, :].rearrange("p t c a e -> p (t c) a e")
                    tot = TOT[:, :, :].rearrange("p t c -> p (t c)")
                    link(v.tensor_copy(tot, l8[:, :, CH - 1]))
                    if d:
                        link(v.tensor_tensor(l8, f8, l8, ALU.subtract))
                        link(v.tensor_tensor(l8, l8, tot.unsqueeze(2).broadcast_to([P, 32, CH]), ALU.add))
                    v.tensor_tensor(ar[:, :, 0, :], l8, f8, ALU.subtract).then_inc(ll_ready, 1)
                    dve.wait_ge(ex_a, d + 1)
                    kk8 = KK[:, :, :].rearrange("p t (c e) -> p (t c) e", e=CH)
                    v.scalar_tensor_tensor(out=ar[:, :, 0, :], in0=ar[:, :, 0, :], scalar=-1.0, in1=kk8, op0=ALU.mult, op1=ALU.mult)
                    dve.wait_ge(ex_r, d + 1)
                    for t in range(4):
                        v.tensor_tensor(AR[:, t, 4:8, 1, :], AR[:, t, 4:8, 1, :], SH[:, t, 1, :].rearrange("p (c e) -> p c e", e=CH), ALU.mult)
                    for t in range(4):
                        last = v.tensor_scalar(KF[:, t, :], BF[:, t, :], -1.0, V("k_a", t), ALU.add, ALU.mult)
                    link(last)
                    link(v.scalar_tensor_tensor(out=KF[:, :, :], in0=KF[:, :, :], scalar=1.0, in1=k4, op0=ALU.add, op1=ALU.mult))
                    if d == 0:
                        v.tensor_copy(KS, KF[:, :, T:2 * T])
                        link(v.memset(STT[:, :, :], 0.0))
                    else:
                        v.tensor_tensor(KS, KS, KF[:, :, T:2 * T], ALU.add)
                        link(v.memset(STT[:, :, :], 0.0))
                    dve.sem_inc(st_ready, 1)
                    dve.wait_ge(ex_inv, d + 1)
                    v.tensor_tensor(KF[:, :, :], KF[:, :, :], LL[:, :, :], ALU.mult)
                    link(v.tensor_tensor(BF[:, :, :], BF[:, :, :], KK[:, :, :], ALU.mult))
                    v.tensor_tensor(BF[:, :, :], BF[:, :, :], LL[:, :, :], ALU.mult).then_inc(feat_ready, 1)
                    mask = C("mask_f" if d == 0 else "mask_b")
                    level = C("level_f" if d == 0 else "level_b").rearrange("p (n e) -> p n e", n=6)
                    eye = C("eye2")

                    def over(a):
                        return a.unsqueeze(1).broadcast_to([P, 4, CH])

                    chunks = list(range(8)) if d == 0 else [3, 2, 1, 0, 7, 6, 5, 4]
                    for m in range(4):
                        Q = 4 * d + m

                        def edge(n, x):
                            v.tensor_tensor(EBS[x][:, n % 2, :, :], MTS[x][:, :, 0, :], over(level[:, n, :]), ALU.mult).then_inc(e_ready, 1)

                        for x in range(2):
                            dve.wait_ge(m_done, 2 * Q + x + 1)
                            if Q:
                                dve.wait_ge(s_done, 2 * Q)
                            v.tensor_tensor(MTS[x][:, :, :, :].rearrange("p a b c -> p a (b c)"),
                                            ps[:, 0:2, :].rearrange("p a (b c) -> p (a b) c", b=2),
                                            mask.unsqueeze(1).broadcast_to([P, 4, 256]), ALU.mult).then_inc(mt_ready, 1)
                            dve.wait_ge(mt_ready, 2 * Q + x + 1)
                            edge(0, x)
                            dve.wait_ge(e_ready, 12 * Q + x + 1)
                            link(v.tensor_tensor(XZS[x][:, 1, :, :], EBS[x][:, 0, :, :], over(eye), ALU.add))
                        for x in range(2):
                            edge(1, x)
                        for x in range(2):
                            dve.wait_ge(d_done, 12 * Q + x + 1)
                            v.tensor_tensor(XZS[x][:, 0, :, :], ps[:, (4, 1)[x], 0:256].rearrange("p (a b) -> p a b", a=4), over(eye), ALU.add).then_inc(xz_ready, 1)
                        for n in range(1, 6):
                            if n < 5:
                                for x in range(2):
                                    edge(n + 1, x)
                            for x in range(2):
                                first = 256 if n == 5 else 0
                                xz = XZS[x][:, :, :, :].rearrange("p s a b -> p (s a b)")[:, first:]
                                dve.wait_ge(d_done, 12 * Q + 2 * n + x + 1)
                                dve.wait_ge(xz_ready, 12 * Q + 2 * (n - 1) + x + 1)
                                v.tensor_tensor(xz, xz, ps[:, (5, 0)[x], first:], ALU.add).then_inc(xz_ready, 1)
                        for x in range(2):
                            i, c = 2 * m + x, chunks[2 * m + x]
                            B = 2 * Q + x
                            dve.wait_ge(s_done, B + 1)
                            link(v.tensor_tensor(STT[:, :, :], STT[:, :, :], ps[:, 7, 0:256].rearrange("p (a b) -> p a b", a=4), ALU.add))
                            if i >= 4:
                                dst = YO_at(c)
                                y = ps[:, 6, 0:256].rearrange("p (a b) -> p a b", a=4)
                                if d == 0:
                                    v.tensor_copy(dst, y)
                                else:
                                    v.tensor_tensor(dst, dst, y, ALU.add)
                            link(v.tensor_tensor(STT[:, :, :], STT[:, :, :], PC[:, :, c].unsqueeze(2).broadcast_to([P, 4, CH]), ALU.mult))
                            if B == 15:
                                link(v.tensor_copy(YO[:, :, :], Y))
                            dve.sem_inc(st_ready, 1)
                if stop == 96:
                    return
                dve.wait_ge(st_ready, 18)
                link(v.tensor_tensor(YB[:, :, :], r4, KS, ALU.mult))
                for t in range(4):
                    last = v.tensor_scalar(YB[:, t, :], YB[:, t, :], V("r_k", t), None, ALU.mult)
                last.then_inc(dve_step, 1)
                dve.wait_ge(pe_step, PE_STEP["y_mean"])
                y2 = YO[:, :, :].rearrange("p (b a) t -> p b (a t)", b=2)
                link(v.tensor_tensor(y2, y2, ps[:, 0:2, :], ALU.subtract))
                dve.sem_inc(dve_step, 1)
                dve.wait_ge(act_step, ACT_STEP["y_std"])
                link(v.reciprocal(YQ[:, :, :], YQ[:, :, :]))
                link(v.tensor_tensor(YO[:, :, :], YO[:, :, :], YQ[:, :, :], ALU.mult))
                for t in range(4):
                    last = v.tensor_scalar(YO[:, t, :], YO[:, t, :], V("ln_x_w", t), V("ln_x_b", t), ALU.mult, ALU.add)
                link(last)
                dve.wait_ge(pe_step, PE_STEP["rb_sum"])
                link(v.tensor_tensor(YB[:, :, :], SH[:, 8:12, 1, :], ps[:, 4:6, :].rearrange("p b (a t) -> p (b a) t", a=2), ALU.mult))
                link(v.tensor_tensor(YO[:, :, :], YO[:, :, :], YB[:, :, :], ALU.add))
                dve.wait_ge(pe_step, PE_STEP["gl_done"])
                v.tensor_tensor(y2, y2, ps[:, 6:8, :], ALU.mult).then_inc(dve_step, 1)
                dve.wait_ge(block_used, OUT0)
                g2 = G[:, :, :].rearrange("p (b a) t -> p b (a t)", a=2)
                v.tensor_tensor(MG[:, :, :].rearrange("p (b a) t -> p b (a t)", a=2), g2[:, 0:4, :], ps[:, 0:4, :], ALU.mult)
                link(v.tensor_tensor(MH[:, :, :].rearrange("p (b a) t -> p b (a t)", a=2), g2[:, 4:8, :], ps[:, 4:8, :], ALU.mult))
                v.tensor_tensor(MG[:, :, :], MG[:, :, :], MH[:, :, :], ALU.add).then_inc(dve_step, 1)
                dve.wait_ge(act_step, ACT_STEP["mix_std"])
                link(v.reciprocal(RS[:, 0, :], RS[:, 0, :]))
                link(v.tensor_tensor(MG[:, :, :], acc8, RS[:, 0, :].unsqueeze(1).broadcast_to([P, KD, T]), ALU.mult))
                for k in range(KD):
                    last = v.scalar_tensor_tensor(out=X[:, k, :], in0=MG[:, k, :], scalar=GP[:, k:k + 1], in1=X[:, k, :], op0=ALU.mult, op1=ALU.add)
                last.then_inc(dve_step, 1)
                dve.wait_ge(act_step, ACT_STEP["f_std"])
                link(v.reciprocal(RS[:, 1, :], RS[:, 1, :]))
                link(v.tensor_tensor(MG[:, :, :], X[:, :, :], RS[:, 1, :].unsqueeze(1).broadcast_to([P, KD, T]), ALU.mult))
                for k in range(KD):
                    last = v.tensor_scalar(MG[:, k, :], MG[:, k, :], GF[:, k:k + 1], ADA[:, 24 + k, 1:2], ALU.mult, ALU.add)
                last.then_inc(dve_step, 1)

            def YO_at(c):
                return SH[:, 0:4, 0, (c % 4) * CH:(c % 4 + 1) * CH]


            def moe():
                link(v.tensor_copy(GB[:, :, :], GQ.unsqueeze(2).broadcast_to([P, KD, P])))
                dve.sem_inc(dve_step, 1)
                dve.wait_ge(tri_ready, 1)
                dve.wait_ge(pe_step, PE_STEP["lg_done"])
                link(v.tensor_tensor(LG[:, :, :], ps[:, 0, 0:64].rearrange("p (n e) -> p n e", n=2),
                                     V("b_router", 0, EXPERTS).unsqueeze(1).broadcast_to([P, 2, EXPERTS]), ALU.add))
                for n in range(2):
                    other = LG[:, n, :].unsqueeze(1).broadcast_to([P, EXPERTS, EXPERTS])
                    own = LG[:, n, :].unsqueeze(2).broadcast_to([P, EXPERTS, EXPERTS])
                    link(v.tensor_tensor(CM[:, :, :], other, own, ALU.is_gt))
                    link(v.tensor_tensor(CN[:, :, :], other, own, ALU.is_equal))
                    link(v.tensor_tensor(CN[:, :, :], CN[:, :, :], TR[:, :, :], ALU.mult))
                    link(v.tensor_tensor(CM[:, :, :], CM[:, :, :], CN[:, :, :], ALU.add))
                    link(v.tensor_reduce(RK[:, n, :], CM[:, :, :], AX.X, ALU.add))
                v.tensor_scalar(MK[:, :, :], RK[:, :, :], 3.5, None, ALU.is_lt).then_inc(dve_step, 1)
                link(v.tensor_reduce(R2[:, 0:2], LG[:, :, :], AX.X, ALU.max))
                v.tensor_tensor(EX[:, :, :], LG[:, :, :], R2[:, 0:2].unsqueeze(2).broadcast_to([P, 2, EXPERTS]), ALU.subtract).then_inc(dve_step, 1)
                dve.wait_ge(act_step, ACT_STEP["lg_exp"])
                dve.wait_ge(dve_step, DVE_STEP["mask_ready"])
                link(v.tensor_tensor(EX[:, :, :], EX[:, :, :], MK[:, :, :], ALU.mult))
                link(v.tensor_reduce(R2[:, 2:4], EX[:, :, :], AX.X, ALU.add))
                link(v.reciprocal(R2[:, 4:6], R2[:, 2:4]))
                v.memset(GT[:, :, 0:1], 0.0)
                link(v.tensor_tensor(GT[:, :, 1:1 + EXPERTS], EX[:, :, :], R2[:, 4:6].unsqueeze(2).broadcast_to([P, 2, EXPERTS]), ALU.mult))
                dve.wait_ge(pe_step, PE_STEP["pos_done"])
                link(v.scalar_tensor_tensor(out=RK[:, :, :], in0=ps[:, 3, 0:64].rearrange("p (n e) -> p n e", n=2), scalar=1.0, in1=MK[:, :, :], op0=ALU.add, op1=ALU.mult))
                link(v.tensor_scalar(SLOT[:, :, 0:EXPERTS], RK[:, :, :], -1.0, None, ALU.add))
                link(v.tensor_copy(MORE, ps[:, 3, 64:64 + EXPERTS]))
                link(v.tensor_copy(PICK[:, 0:EXPERTS], C("pick")))
                v.memset(YT[:, :, :], 0.0)
                v.memset(YBE[:, :], 0.0)
                link(v.memset(PTE[:, :, :], 0.0))
                dve.wait_ge(bias_in, 16)
                link(v.tensor_copy(T3[0:96, :], BR[0:96, :]))
                v.tensor_copy(B3[0:32, :], T3[0:32, :])
                link(v.tensor_tensor(BR[0:96, :], BR[0:96, :], T3[0:96, :], ALU.subtract))
                link(v.tensor_copy(T3[0:96, :], BR[0:96, :]))
                v.tensor_copy(B3[32:64, :], T3[32:64, :])
                link(v.tensor_tensor(BR[0:96, :], BR[0:96, :], T3[0:96, :], ALU.subtract))
                link(v.tensor_copy(B3[64:96, :], BR[64:96, :]))
                dve.sem_inc(dve_step, 1)
                pick = C("pick")

                def onehot(E):
                    for n in range(2):
                        last = v.tensor_scalar(ON[:, n, :], C("iota"), SLOT[:, n, bass.ds(E, 1)], None, ALU.is_equal)
                    last.then_inc(onehot_ready, 1)

                def select(dst, E, done):
                    v.tensor_copy(dst[0:96, :], PICK[0:96, bass.ds(E, 1)].broadcast_to([96, 64])).then_inc(done, 1)

                def add_expert(E, added):
                    for n in range(2):
                        dve.wait_ge(comb_done, E * 2 + (n + 1))
                        y = YT[:, n, :]
                        b = (6, 2)[n]
                        v.scalar_tensor_tensor(out=y, in0=ps[:, b:b + 2, :].rearrange("p b n -> p (b n)"), scalar=GT[:, n, bass.ds(E, 1)], in1=y,
                                               op0=ALU.mult, op1=ALU.add).then_inc(added, 1)

                dve.sem_inc(comb_read, 1)
                dve.sem_inc(glu_done, 1)
                onehot(0)
                select(SELG, 0, selg_ready)
                for a in range(PASSES - 1):
                    v.tensor_scalar(OVER[:, a, :], MORE, CAP * (a + 1) + 0.5, None, ALU.is_gt)
                    v.tensor_scalar(PART[:, :, a * EXPERTS:(a + 1) * EXPERTS], SLOT[:, :, 0:EXPERTS], -1.0 * CAP * (a + 1), None, ALU.add)
                    v.tensor_copy(GATE3[:, :, a * EXPERTS:(a + 1) * EXPERTS], GT[:, :, 1:1 + EXPERTS])
                    v.tensor_copy(PICK3[:, a * EXPERTS:(a + 1) * EXPERTS], pick)
                    link(v.tensor_copy(WHO3[:, a * EXPERTS:(a + 1) * EXPERTS], C("iota")[:, 0:EXPERTS]))
                link(v.tensor_tensor(MORE, OVER[:, 0, :], OVER[:, 1, :], ALU.add))
                link(v.tensor_tensor(MORE, MORE, OVER[:, 2, :], ALU.add))
                link(v.tensor_tensor_scan(UPTO, C("ones")[:, 0:EXPERTS], MORE, 0.0, ALU.mult, ALU.add))
                link(v.tensor_copy(FLAG, UPTO[:, EXPERTS - 1:EXPERTS]))
                link(v.tensor_tensor(UPTO, UPTO, MORE, ALU.subtract))
                for a in range(PASSES - 1):
                    link(v.scalar_tensor_tensor(out=TURN[:, a, :], in0=UPTO, scalar=a + 1.0, in1=OVER[:, a, :], op0=ALU.add, op1=ALU.mult))
                turn96 = TURN[:, :, :].rearrange("p a e -> p (a e)")
                link(v.tensor_scalar(turn96, turn96, -1.0, None, ALU.add))
                link(v.tensor_tensor(SELJ[:, :, :], turn96.unsqueeze(1).broadcast_to([P, EXTRA, 96]), C("iota")[:, 0:EXTRA].unsqueeze(2).broadcast_to([P, EXTRA, 96]), ALU.is_equal))
                for values, dst in ((PART[:, 0, :], SLOT[:, 0, EXPERTS:EXPERTS + EXTRA]), (PART[:, 1, :], SLOT[:, 1, EXPERTS:EXPERTS + EXTRA]),
                                    (GATE3[:, 0, :], GT[:, 0, 1 + EXPERTS:]), (GATE3[:, 1, :], GT[:, 1, 1 + EXPERTS:]),
                                    (PICK3, PICK[:, EXPERTS:EXPERTS + EXTRA]), (WHO3, WHOF)):
                    link(v.tensor_tensor(PROD[:, :, :], SELJ[:, :, :], values.unsqueeze(1).broadcast_to([P, EXTRA, 96]), ALU.mult))
                    link(v.tensor_reduce(dst, PROD[:, :, :], AX.X, ALU.add))
                link(v.tensor_copy(WHO, WHOF))
                v.memset(PICK[:, EXPERTS + EXTRA:], 0.0)
                link(v.memset(SLOT[:, :, EXPERTS + EXTRA:], -1.0))
                dve.sem_inc(extra_ready, 1)

                def expert(E, used):
                    dve.wait_ge(block_used, used)
                    select(SELD, E, seld_ready)
                    for c in range(2):
                        dve.wait_ge(block_used, used + (4 * c + 4))
                        pair = ps[:, c, :].rearrange("p (n a) -> p n a", a=2)
                        dve.wait_ge(glu_done, E * 2 + (c + 1))
                        v.tensor_scalar(TU[:, :], pair[:, :, 1], 7.0, -7.0, ALU.min, ALU.max)
                        v.tensor_scalar(TG[:, :], pair[:, :, 0], 7.0, None, ALU.min).then_inc(clipped, 1)
                        dve.wait_ge(sigm_ready, E * 2 + (c + 1))
                        v.tensor_tensor(TG[:, :], TG[:, :], SGM[:, :], ALU.mult).then_inc(glu_half, 1)
                        dve.wait_ge(glu_half, E * 2 + (c + 1))
                        v.scalar_tensor_tensor(out=AC[:, c, :], in0=TU[:, :], scalar=1.0, in1=TG[:, :], op0=ALU.add, op1=ALU.mult).then_inc(glu_done, 1)
                        if c == 0:
                            add_expert(E, comb_read)
                            dve.wait_ge(pt_turned, E + 1)
                            onehot(E + 1)
                    select(SELG, E + 1, selg_ready)

                with dve.Fori(0, EXPERTS) as E:
                    expert(E, E * EXPERT_BLOCKS + MOE0)
                extra = dve.value_load(FLAG[0:1, 0:1], min_val=0, max_val=EXTRA - 1)
                with dve.If(extra > 0):
                    with dve.Fori(EXPERTS, extra + EXPERTS) as E:
                        expert(E, E * EXPERT_BLOCKS + MOE0)
                    add_expert(extra + EXPERTS, y_all)
                with dve.Else():
                    add_expert(EXPERTS, y_all)
                dve.wait_ge(y_all, 2)
                for n in range(2):
                    v.tensor_tensor_reduce(out=HT[:, n, :], in0=YT[:, n, :], in1=YT[:, n, :], scale=1.0, scalar=0.0, op0=ALU.mult, op1=ALU.add, accum_out=SS[:, n:n + 1]).then_inc(y_sum, 1)
                dve.wait_ge(y_sum, 2)
                dve.sem_inc(dve_step, 1)
                dve.wait_ge(act_step, ACT_STEP["y_root"])
                link(v.reciprocal(SS[:, 2:4], SS[:, 0:2]))
                for n in range(2):
                    last = v.scalar_tensor_tensor(out=YT[:, n, :], in0=YT[:, n, :], scalar=SS[:, 2 + n:3 + n], in1=GR[:, :], op0=ALU.mult, op1=ALU.mult)
                link(last)
                v.tensor_tensor(YT[:, :, :], YT[:, :, :], XT[:, :, :], ALU.add).then_inc(dve_step, 1)

            v.memset(EPS2[:, 0:1], LN_EPS)
            v.memset(EPS2[:, 1:2], RMS_EPS)
            v.memset(EPS2[:, 2:3], GN_EPS)
            v.memset(YP[:, :, 0:TAPS - 1], 0.0)
            v.memset(XB[:, :, 0:LTAPS - 1], 0.0)
            v.memset(RV[0:HEADS, :], NEG)
            link(v.memset(ZERO[:, :], 0.0))
            dve.sem_inc(zero_ready, 1)
            dve.wait_ge(lam_exp, 1)
            link(v.tensor_scalar(LT[:, 2, :], LT[:, 1, :], 2.0, None, ALU.add))
            link(v.reciprocal(LT[:, 2, :], LT[:, 2, :]))
            link(v.tensor_tensor(LT[:, 2, :], LT[:, 2, :], LT[:, 1, :], ALU.mult))
            link(v.tensor_tensor(LT[:, 3, :], LT[:, 2, :], LT[:, 2, :], ALU.mult))
            link(v.memset(LT[:, 4, :], 1.0 / 17))
            for n in range(15, 0, -2):
                link(v.tensor_tensor(LT[:, 4, :], LT[:, 4, :], LT[:, 3, :], ALU.mult))
                link(v.tensor_scalar(LT[:, 4, :], LT[:, 4, :], 1.0 / n, None, ALU.add))
            link(v.tensor_tensor(LT[:, 4, :], LT[:, 4, :], LT[:, 2, :], ALU.mult))
            link(v.tensor_scalar(LT[:, 5, :], V("lam", 0, 2 * LAYERS), -1.0, 0.0, ALU.mult, ALU.max))
            link(v.scalar_tensor_tensor(out=LT[:, 5, :], in0=LT[:, 4, :], scalar=2.0, in1=LT[:, 5, :], op0=ALU.mult, op1=ALU.add))
            link(v.tensor_scalar(LC[:, :], LT[:, 5, :], -8.0, None, ALU.mult))
            link(v.tensor_scalar(LN_[:, :], LT[:, 5, :], 8.0, None, ALU.mult))
            dve.wait_ge(rel_ready, 1)
            v.tensor_copy(RV[0:HEADS, P:2 * P], ps[0:HEADS, 7, 0:P]).then_inc(rv_ready, 1)
            for l in range(LAYERS):
                ffn(2 * l, LB[l])
                ln(3 * l, 0.5, LB[l] + FFN_BLOCKS)
                if stop == 1:
                    return
                mixer(l)
                ln(3 * l + 1, 1.0, LB[l] + FFN_BLOCKS + IN_BLOCKS + OUT_BLOCKS)
                if stop == 2:
                    return
                ffn(2 * l + 1, LB[l] + FFN_BLOCKS + IN_BLOCKS + OUT_BLOCKS)
                ln(3 * l + 2, 0.5, LB[l + 1] if l + 1 < LAYERS else ADA0)
            if stop > 3:
                second()
            if stop > 98:
                moe()


def _lay_out(inputs):
    f = {k: np.asarray(v) for k, v in inputs.items()}

    def cols(a):
        a = np.ascontiguousarray(a).reshape(-1, P)
        return a.T

    def rows(a):
        a = np.asarray(a).reshape(1, -1)
        return np.broadcast_to(a, (P, a.shape[1]))

    def top(a):
        z = np.zeros((P,) + a.shape[1:], a.dtype)
        z[:a.shape[0]] = a
        return z

    def by_k(w):
        k = w.shape[0] // P
        return w.reshape(k, P, w.shape[1]).transpose(1, 0, 2).reshape(P, -1)

    vec = np.zeros((P, NVEC), np.float32)

    def put(name, a):
        at, n = VEC[name]
        vec[:, at:at + n] = a

    put("ln_g", cols(f["ln_g"]))
    put("ln_b", cols(f["ln_b"]))
    for l in range(LAYERS):
        put(f"dw_w{l}", f["conv_dw_w"][l].reshape(TAPS, 2, P).transpose(2, 1, 0).reshape(P, -1))
        put(f"dw_b{l}", cols(f["conv_dw_b"][l]))
        put(f"cln_g{l}", cols(f["conv_ln_g"][l]))
        put(f"cln_b{l}", cols(f["conv_ln_b"][l]))
        put(f"lw{l}", f["lru_conv_w"][l].reshape(LTAPS, 2, P).transpose(2, 1, 0).reshape(P, -1))
        put(f"lb{l}", cols(f["lru_conv_b"][l]))
        put(f"ba{l}", cols(f["lru_ba"][l]))
        put(f"bx{l}", cols(f["lru_bx"][l]))
        put(f"sink{l}", rows(f["attn_sinks"][l]))
        g = np.zeros((P, 4, P), np.float32)
        for which, w in ((0, f["lru_wa"][l]), (1, f["lru_wx"][l])):
            for t in range(2):
                for h in range(2):
                    g[h * 64:h * 64 + 64, 2 * which + t, h * 64:h * 64 + 64] = w[2 * t + h]
        put(f"gate_w{l}", g.reshape(P, -1))
    put("lam", cols(f["lru_lambda"]))
    put("rel_bias", top(f["rel_bias"]))

    heads = np.concatenate([np.r_[t * 64:t * 64 + 64, (4 + t) * 64:(4 + t) * 64 + 64] for t in range(4)])
    perm_in = np.r_[0:1024, 1024 + heads, 1536:1792]
    perm_out = np.r_[0:512, 512 + heads]

    W = np.zeros((BLOCKS, P, BLK), np.float32)
    at = 0

    def cols_block(w, c):
        return by_k(w[:, c * 256:(c + 1) * 256])

    for l in range(LAYERS):
        for i in range(2):
            g, u, d = f["ffn_w_gate"][l, i], f["ffn_w_up"][l, i], f["ffn_w_down"][l, i]
            for j in range(FCH):
                W[at], W[at + 1] = cols_block(g, j), cols_block(u, j)
                at += 2
                if j:
                    W[at] = by_k(d[(j - 1) * 256:j * 256])
                    at += 1
            W[at] = by_k(d[(FCH - 1) * 256:])
            at += 1
            if i == 0:
                w = f["w_in"][l][:, perm_in]
                for b in range(IN_BLOCKS):
                    W[at] = cols_block(w, b)
                    at += 1
                w = f["w_out"][l][perm_out]
                for b in range(OUT_BLOCKS):
                    W[at] = cols_block(w, b)
                    at += 1
    _second(f, W, at, put, cols, rows, top, by_k, cols_block, heads)
    con = constants()
    x_t = f["x"][0].T.reshape(KD, P, T).transpose(1, 0, 2)
    ctx_t = f["ctx_2"][0].T.reshape(KD, P, T).transpose(1, 0, 2)
    b = np.concatenate([f["b_gate_up_2"][0], f["b_down_2"][0]], 1)
    bias = np.concatenate([b, b, b], 0)
    return {"weights": W, "vectors": vec, "consts": con, "x_t": np.ascontiguousarray(x_t),
            "ctx_t": np.ascontiguousarray(ctx_t), "moe_bias": bias}


def _second(f, W, at, put, cols, rows, top, by_k, cols_block, heads):
    for name in ("g_pre_mix", "g_post_mix", "g_pre_ffn", "g_post_ffn", "k_k", "k_a", "r_k", "ln_x_w", "ln_x_b", "mu_prev", "mu_next", "b_ada"):
        put(name, cols(f[name + "_2"][0]))
    zero = np.zeros(P, np.float32)
    perm = np.r_[heads, 512:4736]
    put("b_in", cols(f["b_in_2"][0][perm]))
    put("sink2", rows(f["att_sinks_2"][0]))
    put("w0", np.concatenate([cols(f["w0_f_2"][0]), cols(f["w0_b_2"][0])], 1))
    put("a0", np.concatenate([cols(f["a0_f_2"][0]), cols(f["a0_b_2"][0])], 1))
    put("b_router", rows(f["b_router_2"][0]))
    put("c", np.stack([cols(f["c_ctx_2"]), cols(f["c_2"][0])], 2).reshape(P, 16))
    put("w2", np.concatenate([f["w2_f_2"][0], f["w2_b_2"][0]], 0))
    put("a2", np.concatenate([f["a2_f_2"][0], f["a2_b_2"][0]], 0))
    put("g2", f["g2_2"][0])
    put("w_router", by_k(f["w_router_2"][0]))
    assert at == ADA0
    for b in range(ADA_BLOCKS):
        W[ADA0 + b] = cols_block(f["w_ada_2"][0], b)
    w = f["w_in_2"][0][:, perm]
    w = np.concatenate([w, np.zeros((D, P), np.float32)], 1)
    for b in range(PROJ_BLOCKS):
        W[PROJ0 + b] = cols_block(w, b)
    for b in range(2):
        W[UP0 + b] = by_k(f["w_up_att_2"][0][heads][:, b * 512:(b + 1) * 512])
        W[UP0 + 2 + b] = by_k(f["w_up_rwkv_2"][0][:, b * 512:(b + 1) * 512])
    for b in range(OUT_BLOCKS):
        W[OUT0 + b] = cols_block(f["w_out_2"][0], b)
    for e in range(EXPERTS):
        at = MOE0 + e * EXPERT_BLOCKS
        for pair in range(3):
            w, at_col = (f["w_gate_up_2"][0, e], 1024 * pair) if pair < 2 else (f["w_down_2"][0, e], 0)
            for k in range(2):
                for n in range(2):
                    c = at_col + 512 * n
                    W[at] = by_k(w[k * 512:(k + 1) * 512, c:c + 512])
                    at += 1


def _program(nc, arrays, stop=99):
    args = {n: nc.dram_tensor(n, a.shape, mybir.dt.from_np(a.dtype), kind="ExternalInput").ap()
            for n, a in arrays.items()}
    out = nc.dram_tensor("out", (P, 2048), F32, kind="ExternalOutput").ap()
    bass_two_blocks(nc, args["weights"], args["vectors"], args["consts"], args["x_t"], args["ctx_t"],
                    args["moe_bias"], out, stop)


def kernel(**inputs):
    import concourse.bacc as _bacc
    from concourse.bass_utils import run_bass_kernel_spmd as _run

    arrays = _lay_out(inputs)
    nc = _bacc.Bacc("TRN2", target_bir_lowering=False, num_devices=1)
    _program(nc, arrays)
    r = _run(nc, [arrays], core_ids=[0])
    return r.results[0]["out"].reshape(P, 2, D).transpose(1, 0, 2).reshape(1, T, D)
```
